# Optimizing a Trainium2 kernel written in Bass

```python
import math
import jax
import jax.numpy as jnp
from jax import lax
import numpy as np
import jax, jax.numpy as jnp

D_MODEL = 1024
BATCH = 1
SEQ = 256
DEPTH = 2

HEAD_DIM = 64
A_HEADS = 16
A_WIDTH = A_HEADS * HEAD_DIM
DILATED_PAIRS = ((128, 1), (512, 4), (2048, 16))
B_HEADS = D_MODEL // (2 * HEAD_DIM)
B_QK_WIDTH = 2 * B_HEADS * HEAD_DIM
B_V_DIM = 2 * HEAD_DIM
B_WIDTH = B_HEADS * B_V_DIM
IN_WIDTHS = (A_WIDTH, A_WIDTH, A_WIDTH, A_WIDTH,
             B_QK_WIDTH, B_QK_WIDTH, B_WIDTH, B_WIDTH,
             D_MODEL, D_MODEL)
IN_TOTAL = sum(IN_WIDTHS)
ROPE_THETA = 500000.0
ROPE_DIM = HEAD_DIM // 4
Q_BLOCK = 128
RMS_EPS = 1e-6
SUBLN_EPS = 1e-5
NEG = -1e30


def rms_norm(x, w, eps):
    xf = x.astype(jnp.float32)
    return xf * lax.rsqrt(jnp.mean(xf * xf, axis=-1, keepdims=True) + eps) * w.astype(jnp.float32)

def rope_tables(seq):
    inv = 1.0 / (ROPE_THETA ** (jnp.arange(0, ROPE_DIM, 2, dtype=jnp.float32) / ROPE_DIM))
    ang = jnp.arange(seq, dtype=jnp.float32)[:, None] * inv[None, :]
    return jnp.cos(ang), jnp.sin(ang)

def partial_rope(t, cos, sin):
    half = ROPE_DIM // 2
    tr = t[..., :ROPE_DIM].astype(jnp.float32)
    t1, t2 = tr[..., :half], tr[..., half:]
    c = cos[None, :, None, :]
    s = sin[None, :, None, :]
    rot = jnp.concatenate([t1 * c - t2 * s, t1 * s + t2 * c], axis=-1).astype(t.dtype)
    return jnp.concatenate([rot, t[..., ROPE_DIM:]], axis=-1)

def split_cols(u):
    outs = []
    start = 0
    for w in IN_WIDTHS:
        outs.append(u[..., start:start + w])
        start += w
    return outs

def dilated_pattern(q, k, v, window, dilation):
    b, s, h, dh = q.shape
    n = window // dilation
    chunk = dilation * n
    sp = -(-s // chunk) * chunk
    length = sp // dilation
    nb = length // n

    def to_blocks(t):
        t = jnp.pad(t, ((0, 0), (0, sp - s), (0, 0), (0, 0)))
        t = t.reshape(b, length, dilation, h, dh).transpose(0, 2, 1, 3, 4)
        return t.reshape(b, dilation, nb, n, h, dh)

    def with_prev(t):
        prev = jnp.pad(t, ((0, 0), (0, 0), (1, 0), (0, 0), (0, 0), (0, 0)))[:, :, :-1]
        return jnp.concatenate([prev, t], axis=3)

    qb = to_blocks(q)
    kb = with_prev(to_blocks(k))
    vb = with_prev(to_blocks(v))
    scores = jnp.einsum('brnqhd,brnkhd->brnqhk', qb, kb,
                        preferred_element_type=jnp.float32) * (HEAD_DIM ** -0.5)
    qi = jnp.arange(n)[:, None]
    kc = jnp.arange(2 * n)[None, :]
    dist = qi + n - kc
    blk = jnp.arange(nb)[:, None, None]
    valid = (dist >= 0) & (dist <= n) & (blk * n + kc - n >= 0)
    scores = jnp.where(valid[None, None, :, :, None, :], scores, NEG)
    m = jnp.max(scores, axis=-1)
    p = jnp.exp(scores - m[..., None])
    den = jnp.sum(p, axis=-1)
    o = jnp.einsum('brnqhk,brnkhd->brnqhd', p, vb.astype(jnp.float32)) / den[..., None]

    def from_blocks(t):
        t = t.reshape((b, dilation, length) + t.shape[4:])
        t = jnp.swapaxes(t, 1, 2)
        return t.reshape((b, sp) + t.shape[3:])[:, :s]

    return from_blocks(o), from_blocks(m), from_blocks(den)

def dilated_mixture(q, k, v):
    outs = [dilated_pattern(q, k, v, w, d) for (w, d) in DILATED_PAIRS]
    m_all = jnp.stack([r[1] for r in outs])
    d_all = jnp.stack([r[2] for r in outs])
    o_all = jnp.stack([r[0] for r in outs])
    wts = d_all * jnp.exp(m_all - jnp.max(m_all, axis=0))
    return jnp.sum(wts[..., None] * o_all, axis=0) / jnp.sum(wts, axis=0)[..., None]

def diff_attention(q1, q2, k1, k2, v, lam):
    b, s, h, dh = q1.shape
    nq = s // Q_BLOCK
    qs = jnp.stack([q1, q2], 0).reshape(2, b, nq, Q_BLOCK, h, dh).transpose(2, 0, 1, 3, 4, 5)
    ks = jnp.stack([k1, k2], 0)
    vf = v.astype(jnp.float32)
    kpos = jnp.arange(s)

    def one_block(args):
        qblk, bi = args
        sc = jnp.einsum('mbqhd,mbkhd->mbhqk', qblk, ks,
                        preferred_element_type=jnp.float32) * (dh ** -0.5)
        qpos = bi * Q_BLOCK + jnp.arange(Q_BLOCK)
        sc = jnp.where(kpos[None, :] <= qpos[:, None], sc, NEG)
        p = jax.nn.softmax(sc, axis=-1)
        a = p[0] - lam * p[1]
        return jnp.einsum('bhqk,bkhe->bqhe', a, vf)

    out = lax.map(one_block, (qs, jnp.arange(nq)))
    return out.transpose(1, 0, 2, 3, 4).reshape(b, s, h, 2 * dh)

def lambda_init_value(layer):
    return 0.8 - 0.6 * math.exp(-0.3 * layer)

def hybrid_layer(x, layer, norm_w, w_in, lq1, lk1, lq2, lk2, subln_w,
                 w_proj_a, w_proj_b, w_out, cos, sin):
    b, s, _ = x.shape
    hdn = rms_norm(x, norm_w, RMS_EPS).astype(x.dtype)
    u = hdn @ w_in
    qa, ka, va, za, qb, kb, vb, zb, ga, gb = split_cols(u)

    qa = partial_rope(qa.reshape(b, s, A_HEADS, HEAD_DIM), cos, sin)
    ka = partial_rope(ka.reshape(b, s, A_HEADS, HEAD_DIM), cos, sin)
    va = va.reshape(b, s, A_HEADS, HEAD_DIM)
    ya = dilated_mixture(qa, ka, va).reshape(b, s, A_WIDTH)
    ya = ya * jax.nn.silu(za.astype(jnp.float32))

    qb = partial_rope(qb.reshape(b, s, 2 * B_HEADS, HEAD_DIM), cos, sin)
    kb = partial_rope(kb.reshape(b, s, 2 * B_HEADS, HEAD_DIM), cos, sin)
    vb = vb.reshape(b, s, B_HEADS, B_V_DIM)
    lam_init = lambda_init_value(layer)
    lam = (jnp.exp(jnp.sum(lq1.astype(jnp.float32) * lk1.astype(jnp.float32)))
           - jnp.exp(jnp.sum(lq2.astype(jnp.float32) * lk2.astype(jnp.float32))) + lam_init)
    ob = diff_attention(qb[:, :, 0::2], qb[:, :, 1::2], kb[:, :, 0::2], kb[:, :, 1::2], vb, lam)
    ob = rms_norm(ob, subln_w, SUBLN_EPS) * (1.0 - lam_init)
    yb = ob.reshape(b, s, B_WIDTH) * jax.nn.silu(zb.astype(jnp.float32))

    pa = ya.astype(x.dtype) @ w_proj_a
    pb = yb.astype(x.dtype) @ w_proj_b
    merged = (jax.nn.sigmoid(ga.astype(jnp.float32)) * pa.astype(jnp.float32)
              + jax.nn.sigmoid(gb.astype(jnp.float32)) * pb.astype(jnp.float32))
    return x + (merged.astype(x.dtype) @ w_out).astype(x.dtype)

def first_inputs(seed: int = 0) -> dict:
    key = jax.random.key(seed)
    ks = jax.random.split(key, 16)
    f32 = jnp.float32
    x = jax.random.normal(ks[0], (BATCH, SEQ, D_MODEL), f32)
    norm_w = 1.0 + 0.02 * jax.random.normal(ks[1], (DEPTH, D_MODEL), f32)
    w_in = jax.random.normal(ks[2], (DEPTH, D_MODEL, IN_TOTAL), f32) * D_MODEL ** -0.5
    lambda_q1 = 0.1 * jax.random.normal(ks[3], (DEPTH, HEAD_DIM), f32)
    lambda_k1 = 0.1 * jax.random.normal(ks[4], (DEPTH, HEAD_DIM), f32)
    lambda_q2 = 0.1 * jax.random.normal(ks[5], (DEPTH, HEAD_DIM), f32)
    lambda_k2 = 0.1 * jax.random.normal(ks[6], (DEPTH, HEAD_DIM), f32)
    subln_w = 1.0 + 0.02 * jax.random.normal(ks[7], (DEPTH, B_V_DIM), f32)
    w_proj_a = jax.random.normal(ks[8], (DEPTH, A_WIDTH, D_MODEL), f32) * A_WIDTH ** -0.5
    w_proj_b = jax.random.normal(ks[9], (DEPTH, B_WIDTH, D_MODEL), f32) * B_WIDTH ** -0.5
    w_out = jax.random.normal(ks[10], (DEPTH, D_MODEL, D_MODEL), f32) * D_MODEL ** -0.5
    final_norm_w = 1.0 + 0.02 * jax.random.normal(ks[11], (D_MODEL,), f32)
    return {'x': x, 'norm_w': norm_w, 'w_in': w_in,
            'lambda_q1': lambda_q1, 'lambda_k1': lambda_k1,
            'lambda_q2': lambda_q2, 'lambda_k2': lambda_k2,
            'subln_w': subln_w, 'w_proj_a': w_proj_a, 'w_proj_b': w_proj_b,
            'w_out': w_out, 'final_norm_w': final_norm_w}

def first_block(x, norm_w, w_in, lambda_q1, lambda_k1, lambda_q2, lambda_k2,
              subln_w, w_proj_a, w_proj_b, w_out, final_norm_w):
    cos, sin = rope_tables(x.shape[1])
    h = x
    for layer in range(DEPTH):
        h = hybrid_layer(h, layer, norm_w[layer], w_in[layer],
                         lambda_q1[layer], lambda_k1[layer], lambda_q2[layer], lambda_k2[layer],
                         subln_w[layer], w_proj_a[layer], w_proj_b[layer], w_out[layer],
                         cos, sin)
    return rms_norm(h, final_norm_w, RMS_EPS).astype(x.dtype)


DN_HEADS = 8
DN_DK = 128
DN_DV = 128
DN_CONV = 4
DN_CHUNK = 64
SW_Q_HEADS = 16
SW_KV_HEADS = 2
SW_HEAD_DIM = 64
SW_WINDOW = 128
SW_BLOCK = 128
ROT_DIM = SW_HEAD_DIM // 4
D_FF = 4 * D_MODEL
EPS = 1e-6

DN_QK_W = DN_HEADS * DN_DK
DN_V_W = DN_HEADS * DN_DV
SW_Q_W = SW_Q_HEADS * SW_HEAD_DIM
SW_KV_W = SW_KV_HEADS * SW_HEAD_DIM
IN_SPLITS = [DN_QK_W, DN_QK_W, DN_V_W, DN_V_W, DN_HEADS, DN_HEADS,
             SW_Q_W, SW_KV_W, SW_KV_W, D_MODEL, D_MODEL]
D_IN = sum(IN_SPLITS)
IN_OFFSETS = np.cumsum(IN_SPLITS)[:-1].tolist()


def rmsnorm(x, g):
    xf = x.astype(jnp.float32)
    y = xf * lax.rsqrt(jnp.mean(xf * xf, axis=-1, keepdims=True) + EPS)
    return (y * g.astype(jnp.float32)).astype(x.dtype)

def l2norm(t):
    tf = t.astype(jnp.float32)
    return tf * lax.rsqrt(jnp.sum(tf * tf, axis=-1, keepdims=True) + EPS)

def causal_conv_silu(x, w):
    S = x.shape[1]
    K = w.shape[0]
    xp = jnp.pad(x, ((0, 0), (K - 1, 0), (0, 0)))
    y = sum(xp[:, j:j + S] * w[j] for j in range(K))
    return jax.nn.silu(y)

def gated_delta_rule(q, k, v, g, beta):
    B, S, H, dk = q.shape
    dv = v.shape[-1]
    C = DN_CHUNK
    N = S // C

    def chunks(t):
        return t.reshape(B, N, C, H, -1).transpose(0, 3, 1, 2, 4)

    q, k, v = chunks(q), chunks(k), chunks(v)
    g = g.reshape(B, N, C, H).transpose(0, 3, 1, 2)
    beta = beta.reshape(B, N, C, H).transpose(0, 3, 1, 2)
    g = jnp.cumsum(g, axis=-1)

    idx = jnp.arange(C)
    causal = idx[:, None] >= idx[None, :]
    strict = idx[:, None] > idx[None, :]
    diff = g[..., :, None] - g[..., None, :]
    decay = jnp.where(causal, jnp.exp(jnp.where(causal, diff, 0.0)), 0.0)

    kb = k * beta[..., None]
    L = jnp.where(strict, jnp.einsum('bhnid,bhnjd->bhnij', kb, k) * decay, 0.0)
    u = lax.linalg.triangular_solve(L, v * beta[..., None], left_side=True,
                                    lower=True, unit_diagonal=True)
    w = lax.linalg.triangular_solve(L, kb * jnp.exp(g)[..., None], left_side=True,
                                    lower=True, unit_diagonal=True)
    a_intra = jnp.einsum('bhnid,bhnjd->bhnij', q, k) * decay
    q_dec = q * jnp.exp(g)[..., None]
    g_last = g[..., -1]
    k_dec = k * jnp.exp(g_last[..., None] - g)[..., None]

    def to_front(t):
        return jnp.moveaxis(t, 2, 0)

    xs = (to_front(q_dec), to_front(k_dec), to_front(u), to_front(w),
          to_front(a_intra), jnp.moveaxis(g_last, 2, 0))

    def step(state, inp):
        qd, kd, u_c, w_c, a_c, gl = inp
        v_new = u_c - jnp.einsum('bhcd,bhde->bhce', w_c, state)
        o = (jnp.einsum('bhcd,bhde->bhce', qd, state)
             + jnp.einsum('bhij,bhje->bhie', a_c, v_new))
        state = state * jnp.exp(gl)[..., None, None] + jnp.einsum('bhcd,bhce->bhde', kd, v_new)
        return state, o

    state0 = jnp.zeros((B, H, dk, dv), jnp.float32)
    _, o = lax.scan(step, state0, xs)
    return o.transpose(1, 0, 3, 2, 4).reshape(B, S, H, dv)

def deltanet_branch(q_in, k_in, v_in, z, b_in, a_in, conv_w, a_log, dt_bias, norm_g):
    B, S, _ = q_in.shape
    qkv = causal_conv_silu(jnp.concatenate([q_in, k_in, v_in], axis=-1), conv_w)
    q, k, v = jnp.split(qkv, [DN_QK_W, 2 * DN_QK_W], axis=-1)
    q = l2norm(q.reshape(B, S, DN_HEADS, DN_DK)) * (DN_DK ** -0.5)
    k = l2norm(k.reshape(B, S, DN_HEADS, DN_DK))
    v = v.reshape(B, S, DN_HEADS, DN_DV).astype(jnp.float32)
    beta = jax.nn.sigmoid(b_in.astype(jnp.float32))
    g = -jnp.exp(a_log.astype(jnp.float32)) * jax.nn.softplus(
        a_in.astype(jnp.float32) + dt_bias.astype(jnp.float32))
    o = gated_delta_rule(q, k, v, g, beta)
    o = rmsnorm(o, norm_g) * jax.nn.silu(z.reshape(B, S, DN_HEADS, DN_DV).astype(jnp.float32))
    return o.reshape(B, S, DN_V_W).astype(q_in.dtype)

def partial_rope_2(x, positions):
    half = ROT_DIM // 2
    inv_freq = ROPE_THETA ** (-jnp.arange(half, dtype=jnp.float32) * (2.0 / ROT_DIM))
    ang = positions.astype(jnp.float32)[..., None] * inv_freq
    cos = jnp.cos(ang)[:, :, None, :]
    sin = jnp.sin(ang)[:, :, None, :]
    xr = x[..., :ROT_DIM].astype(jnp.float32)
    x1, x2 = xr[..., :half], xr[..., half:]
    rot = jnp.concatenate([x1 * cos - x2 * sin, x2 * cos + x1 * sin], axis=-1)
    return jnp.concatenate([rot.astype(x.dtype), x[..., ROT_DIM:]], axis=-1)

def swa_sink_branch(q_in, k_in, v_in, positions, sinks):
    B, S, _ = q_in.shape
    G = SW_Q_HEADS // SW_KV_HEADS
    nb = S // SW_BLOCK
    q = partial_rope_2(q_in.reshape(B, S, SW_Q_HEADS, SW_HEAD_DIM), positions)
    k = partial_rope_2(k_in.reshape(B, S, SW_KV_HEADS, SW_HEAD_DIM), positions)
    v = v_in.reshape(B, S, SW_KV_HEADS, SW_HEAD_DIM)

    qb = q.reshape(B, nb, SW_BLOCK, SW_KV_HEADS, G, SW_HEAD_DIM).astype(jnp.float32)

    def band(t):
        tp = jnp.pad(t, ((0, 0), (SW_BLOCK, 0), (0, 0), (0, 0)))
        tb = tp.reshape(B, nb + 1, SW_BLOCK, SW_KV_HEADS, SW_HEAD_DIM)
        return jnp.concatenate([tb[:, :-1], tb[:, 1:]], axis=2)

    kw = band(k).astype(jnp.float32)
    vw = band(v)
    scores = jnp.einsum('bnqhgd,bnkhd->bnhgqk', qb, kw) * (SW_HEAD_DIM ** -0.5)

    qi = jnp.arange(SW_BLOCK)[:, None] + SW_BLOCK
    ki = jnp.arange(2 * SW_BLOCK)[None, :]
    off = qi - ki
    in_band = (off >= 0) & (off < SW_WINDOW)
    blk = jnp.arange(nb)[:, None, None]
    valid = (blk * SW_BLOCK + ki[None] - SW_BLOCK) >= 0
    mask = (in_band[None] & valid)[None, :, None, None]
    scores = jnp.where(mask, scores, -jnp.inf)

    sink = sinks.astype(jnp.float32).reshape(SW_KV_HEADS, G)[None, None, :, :, None, None]
    m = jnp.maximum(jnp.max(scores, axis=-1, keepdims=True), sink)
    p = jnp.exp(scores - m)
    probs = p / (jnp.sum(p, axis=-1, keepdims=True) + jnp.exp(sink - m))
    o = jnp.einsum('bnhgqk,bnkhd->bnqhgd', probs.astype(vw.dtype), vw)
    return o.reshape(B, S, SW_Q_W)

def hybrid_layer_2(x, positions, pre_mix_g, w_in, dn_conv_w, dn_a_log, dn_dt_bias, dn_norm_g,
                 sw_sinks, w_up_dn, w_up_sw, w_o, post_mix_g, pre_mlp_g, w_ff1, w_ff2,
                 post_mlp_g):
    h = rmsnorm(x, pre_mix_g)
    proj = h @ w_in
    (dn_q, dn_k, dn_v, dn_z, dn_b, dn_a, sw_q, sw_k, sw_v,
     gate_a, gate_b) = jnp.split(proj, IN_OFFSETS, axis=-1)
    y_a = deltanet_branch(dn_q, dn_k, dn_v, dn_z, dn_b, dn_a, dn_conv_w, dn_a_log,
                          dn_dt_bias, dn_norm_g) @ w_up_dn
    y_b = swa_sink_branch(sw_q, sw_k, sw_v, positions, sw_sinks) @ w_up_sw
    mix = (jax.nn.sigmoid(gate_a) * y_a + jax.nn.sigmoid(gate_b) * y_b) @ w_o
    x = x + rmsnorm(mix, post_mix_g)

    h2 = rmsnorm(x, pre_mlp_g)
    ff = jnp.square(jax.nn.relu(h2 @ w_ff1)) @ w_ff2
    return x + rmsnorm(ff, post_mlp_g)

def second_inputs(seed: int = 0) -> dict:
    key = jax.random.key(seed)
    ks = jax.random.split(key, 20)
    f32 = jnp.float32

    def nrm(k, shape, scale):
        return jax.random.normal(k, shape, f32) * scale

    def gain(k, shape):
        return 1.0 + 0.02 * jax.random.normal(k, shape, f32)

    x = jax.random.normal(ks[0], (BATCH, SEQ, D_MODEL), f32)
    positions = jnp.broadcast_to(jnp.arange(SEQ, dtype=jnp.int32), (BATCH, SEQ))
    dt = jnp.exp(jax.random.uniform(ks[5], (DEPTH, DN_HEADS), f32,
                                    np.log(1e-3), np.log(1e-1)))
    return {
        'x': x,
        'positions': positions,
        'pre_mix_g': gain(ks[1], (DEPTH, D_MODEL)),
        'w_in': nrm(ks[2], (DEPTH, D_MODEL, D_IN), D_MODEL ** -0.5),
        'dn_conv_w': nrm(ks[3], (DEPTH, DN_CONV, 2 * DN_QK_W + DN_V_W), DN_CONV ** -0.5),
        'dn_a_log': jnp.log(jax.random.uniform(ks[4], (DEPTH, DN_HEADS), f32, 1.0, 16.0)),
        'dn_dt_bias': dt + jnp.log(-jnp.expm1(-dt)),
        'dn_norm_g': gain(ks[6], (DEPTH, DN_DV)),
        'sw_sinks': nrm(ks[7], (DEPTH, SW_Q_HEADS), 0.5),
        'w_up_dn': nrm(ks[8], (DEPTH, DN_V_W, D_MODEL), DN_V_W ** -0.5),
        'w_up_sw': nrm(ks[9], (DEPTH, SW_Q_W, D_MODEL), SW_Q_W ** -0.5),
        'w_o': nrm(ks[10], (DEPTH, D_MODEL, D_MODEL), D_MODEL ** -0.5),
        'post_mix_g': gain(ks[11], (DEPTH, D_MODEL)),
        'pre_mlp_g': gain(ks[12], (DEPTH, D_MODEL)),
        'w_ff1': nrm(ks[13], (DEPTH, D_MODEL, D_FF), D_MODEL ** -0.5),
        'w_ff2': nrm(ks[14], (DEPTH, D_FF, D_MODEL), D_FF ** -0.5),
        'post_mlp_g': gain(ks[15], (DEPTH, D_MODEL)),
    }

def second_block(x, positions, pre_mix_g, w_in, dn_conv_w, dn_a_log, dn_dt_bias, dn_norm_g,
              sw_sinks, w_up_dn, w_up_sw, w_o, post_mix_g, pre_mlp_g, w_ff1, w_ff2,
              post_mlp_g):
    for l in range(DEPTH):
        x = hybrid_layer_2(x, positions, pre_mix_g[l], w_in[l], dn_conv_w[l], dn_a_log[l],
                         dn_dt_bias[l], dn_norm_g[l], sw_sinks[l], w_up_dn[l], w_up_sw[l],
                         w_o[l], post_mix_g[l], pre_mlp_g[l], w_ff1[l], w_ff2[l],
                         post_mlp_g[l])
    return x


def setup_inputs(seed=0):
    out = dict(first_inputs(seed))
    for name, value in second_inputs(seed + 1).items():
        if name != "x":
            out[name + "_2"] = value
    return out


def reference(
    x, norm_w, w_in, lambda_q1, lambda_k1, lambda_q2, lambda_k2, subln_w, w_proj_a, w_proj_b,
    w_out, final_norm_w, positions_2, pre_mix_g_2, w_in_2, dn_conv_w_2, dn_a_log_2,
    dn_dt_bias_2, dn_norm_g_2, sw_sinks_2, w_up_dn_2, w_up_sw_2, w_o_2, post_mix_g_2,
    pre_mlp_g_2, w_ff1_2, w_ff2_2, post_mlp_g_2,
):
    x = first_block(
        x, norm_w, w_in, lambda_q1, lambda_k1, lambda_q2, lambda_k2, subln_w, w_proj_a,
        w_proj_b, w_out, final_norm_w,
    )
    return second_block(
        x, positions_2, pre_mix_g_2, w_in_2, dn_conv_w_2, dn_a_log_2, dn_dt_bias_2, dn_norm_g_2,
        sw_sinks_2, w_up_dn_2, w_up_sw_2, w_o_2, post_mix_g_2, pre_mlp_g_2, w_ff1_2, w_ff2_2,
        post_mlp_g_2,
    )


_drawn_inputs = setup_inputs


def setup_inputs(seed=0):
    import zlib

    import numpy as np

    out = dict(_drawn_inputs(seed))
    spreads = {}
    factors = {'subln_w': 4.503,
     'dn_norm_g_2': 2.875,
     'sw_sinks_2': 3.866,
     'post_mix_g_2': 2.7,
     'pre_mlp_g_2': 2.815,
     'post_mlp_g_2': 3.418}
    for name, (base, spread) in spreads.items():
        noise = np.random.default_rng([zlib.crc32(name.encode()), seed]).standard_normal(out[name].shape)
        drawn = base * np.exp(spread * noise) if base else spread * noise
        out[name] = jnp.asarray(drawn.astype(out[name].dtype))
    for name, factor in factors.items():
        out[name] = (out[name] * factor).astype(out[name].dtype)
    return out
```

```python
import math
from contextlib import ExitStack

import numpy as np

import concourse.bass as bass
from concourse import mybir

F32 = mybir.dt.float32
F32R = mybir.dt.float32r
I32 = mybir.dt.int32
ALU = mybir.AluOpType
ACT = mybir.ActivationFunctionType
AX = mybir.AxisListType

P = 128
D = 1024
S = 256
TB = S // P
KB = D // P
DEPTH = 2
CH = 512
HEADS = 16
HD = 64
DHEADS = 8
DV = 128
ROT = HD // 4
NEG = -1e30
SCALE = HD ** -0.5
RAW = 4
RING = 4
LEAD = 3
LEVELS = 7
W_IN2 = 7440


def lambda_init(layer):
    return 0.8 - 0.6 * math.exp(-0.3 * layer)


def shape_constants():
    q = np.arange(P)[:, None]
    k = np.arange(-P, P)[None, :]
    dist = q - k
    causal = dist >= 0
    count = ((causal & (dist <= 128)).astype(int) + (causal & (dist % 4 == 0))
             + (causal & (dist % 16 == 0)))
    dilated = np.where(count > 0, np.log(np.maximum(count, 1)) / SCALE, NEG)
    full = np.where(causal, 0.0, NEG)
    window = np.where(causal & (dist < 128), 0.0, NEG)
    masks = np.stack([dilated, full, window], 1).astype(np.float32)
    t = np.arange(P)
    ident = (t[:, None] == t[None, :])
    upper = (t[:, None] <= t[None, :])
    ones = np.ones((P, P))
    levels = [(t[:, None] // (2 * b) == t[None, :] // (2 * b)) & (t[:, None] // b + 1 == t[None, :] // b)
              for b in (2 ** n for n in range(LEVELS))]
    square = np.stack([ident, upper, ones] + levels, 1).astype(np.float32)
    inv = (1.0 / (np.float32(500000.0) ** (np.arange(0, ROT, 2, dtype=np.float32) / np.float32(ROT))))
    inv = inv.astype(np.float32)
    ang = (np.arange(S, dtype=np.float32)[:, None] * inv[None, :]).astype(np.float32)
    cos, sin = np.cos(ang).astype(np.float32), np.sin(ang).astype(np.float32)
    rope = np.stack([cos, cos, -sin, sin], 1)
    rope = rope.reshape(TB, P, 4 * ROT // 2)
    inv2 = (np.float32(500000.0) ** (-np.arange(ROT // 2, dtype=np.float32) * np.float32(2.0 / ROT)))
    inv2 = np.broadcast_to(inv2.astype(np.float32), (P, ROT // 2))
    return {"masks": masks, "square": square, "rope": np.ascontiguousarray(rope),
            "inv_freq": np.ascontiguousarray(inv2)}


class Signals:

    def __init__(self, nc, ctx, prefix, tally=None, after=None):
        self.after = after
        self.nc, self.ctx, self.prefix, self.tally = nc, ctx, prefix, tally
        self.sems, self.count, self.keys, self.layer = {}, {}, {}, 0
        self.final = dict(tally) if tally else {}

    def shared(self, name):
        return self.after and (self.tally is None or name in self.after.tally)

    def sem(self, name):
        if self.shared(name):
            return self.after.sem(name)
        if name not in self.sems:
            self.sems[name] = self.ctx.enter_context(self.nc.semaphore(f"{self.prefix}_{name}"))
        return self.sems[name]

    def up(self, name, key=0, by=1):
        self.count[name] = self.count.get(name, 0) + by
        self.keys[name, key] = self.count[name]
        return self.sem(name), by

    def at(self, name, key=0):
        if self.tally is None:
            return self.sem(name), self.layer * 2 + 1
        per_layer, n = self.tally[name], self.tally[name, key]
        if self.shared(name):
            n += DEPTH * self.after.tally[name]
        return self.sem(name), self.layer * per_layer + n

    def totals(self):
        return {**self.count, **self.keys}


class Job:

    def __init__(self, name, weight, row, col, rows, cols, unit_rows, xt, xt_block, banks,
                 start=True, stop=True):
        self.name, self.weight, self.row, self.col = name, weight, row, col
        self.rows, self.cols, self.unit = rows, cols, unit_rows
        self.xt, self.xt_block, self.banks = xt, xt_block, banks
        self.start, self.stop = start, stop
        self.pieces = 2 * (rows // unit_rows)


def section(name, weight, col, xt):
    return [Job(f"{name}{c}", weight, 0, col + c * CH, KB, CH, 4, xt, 0, (2 * c, 2 * c + 1))
            for c in range(2)]


class Plan:

    def __init__(self):
        self.steps, self.jobs, self.pieces, self.units = [], [], [], []

    def step(self, *what):
        self.steps.append(what)

    def run(self, jobs, between=(), halves=False):
        between = list(between)
        for job in jobs:
            self.jobs.append(job)
            for n in range(job.pieces):
                if n % 2 == 0:
                    self.units.append((job, n // 2))
                self.pieces.append((job, n))
                g = len(self.pieces) - 1
                if halves:
                    self.steps.append(("piece", g, "half"))
                    if between:
                        self.steps.extend(between.pop(0))
                    self.steps.append(("more", g))
                else:
                    self.steps.append(("piece", g))
                if n == job.pieces - 1 and job.stop:
                    self.steps.append(("evac", job.name))
                if between:
                    self.steps.extend(between.pop(0))
        for rest in between:
            self.steps.extend(rest)

    def close(self):
        self.by_name = {j.name: j for j in self.jobs}
        self.end = {j.name: max(g for g, (k, _) in enumerate(self.pieces) if k is j) for j in self.jobs}
        return self


def attention(kind, heads, first=0):
    out = []
    for t in range(heads + 2):
        out.append(([(f"{kind}_scores", t)] if t < heads else [])
                   + ([(f"{kind}_turn", t - 1)] if 1 <= t <= heads else [])
                   + ([(f"{kind}_out", t - 2)] if t >= 2 else []))
    return out


def spread(groups, every):
    out = []
    for g in groups:
        out += [g] + [[]] * (every - 1)
    return out


def turns(name, a=0, b=4):
    return [[("turn", name, f)] for f in range(a, b)]


def plan_one():
    p = Plan()
    sec = lambda n, i: section(n, "w_in", i * D, 0)
    p.step("norm")
    for t in turns("h"):
        p.steps.extend(t)
    p.run(sec("qa", 0))
    p.run(sec("ka", 1), [[("rope", "qa")]] + turns("qa"))
    p.run(sec("va", 2), [[("rope", "ka")], []] + turns("ka"))
    work = attention("a", HEADS)
    p.run(sec("qb", 4), work[:8])
    p.run(sec("kb", 5), work[8:16])
    p.run(sec("vb", 6), [[("rope", "qb"), ("rope", "kb")] + work[16], work[17], [], []]
          + turns("qb"))
    work = spread(attention("b", DHEADS), 2)
    p.run(sec("za", 3), [a + b for a, b in zip(turns("kb"), [[], [], [], []])] + work[:4])
    p.run(sec("ga", 8), [work[4] + [("gate", "a")]] + work[5:12])
    p.run(sec("gb", 9), [a + b for a, b in zip(work[12:20], [[]] + turns("ya") + [[]] * 3)])
    p.run(sec("zb", 7), [])
    p.step("head_norm")
    p.step("gate", "b")
    p.run(section("pa", "w_proj_a", 0, 1), [[], []] + turns("yb"))
    pb = section("pb", "w_proj_b", 0, 0)
    p.run(pb[:1])
    p.run(pb[1:], [[], [("turn", "mix", 0)], [("turn", "mix", 1)], []])
    p.step("turn", "mix", 2)
    p.step("turn", "mix", 3)
    p.run(section("out", "w_out", 0, 1))
    return p.close()


class Core:

    def __init__(self, nc, ctx):
        self.nc, self.ctx = nc, ctx
        sb = lambda name, shape, dt=F32: ctx.enter_context(nc.sbuf_tensor(name, shape, dt))
        sem = lambda name: ctx.enter_context(nc.semaphore(name))
        self.x = sb("x_res", [P, TB, D])
        self.raw = [sb(f"raw{i}", [P, 4 * CH]) for i in range(RAW)]
        self.hi = [sb(f"hi{i}", [P, 2 * CH], F32R) for i in range(RING)]
        self.lo = [sb(f"lo{i}", [P, 2 * CH], F32R) for i in range(RING)]
        self.xh = [sb(f"xh{i}", [P, KB, S], F32R) for i in range(2)]
        self.xl = [sb(f"xl{i}", [P, KB, S], F32R) for i in range(2)]
        self.buf = [sb(f"buf{i}", [P, TB, D]) for i in range(9)]
        self.scratch = sb("scratch", [P, 5120])
        self.masks = sb("masks", [P, 3, S])
        self.square = sb("square", [P, 3 + LEVELS, P])
        self.rope1 = sb("rope1", [P, TB, 4, ROT // 2])
        self.rope2 = sb("rope2", [P, TB, 4, ROT // 2])
        self.ident, self.upper, self.ones = (self.square[:, i, :] for i in range(3))
        self.small = sb("small", [P, 850])
        self.small_used = 0
        self.bank = [ctx.enter_context(nc.psum_tensor(f"bank{i}", [P, CH], F32)) for i in range(8)]
        self.passed = sem("passed")
        self.x_ready = sem("x_ready")
        self.programs = {e: [] for e in ("tensor", "scalar", "vector", "gpsimd", "sync")}
        self.unit_loaded = [sem(f"unit_loaded{i}") for i in range(RAW)]
        self.hi_ready, self.lo_ready, self.lo_ready_pool = sem("hi_ready"), sem("lo_ready"), sem("lo_ready_pool")
        self.pieces_used = sem("pieces_used")

    def program(self, engine):
        return self.programs[engine].append

    def tile(self, *shape):
        n = int(np.prod(shape))
        a = self.small[:, self.small_used:self.small_used + n]
        self.small_used += n
        assert self.small_used <= 850
        if len(shape) == 2:
            a = a.rearrange("p (a b) -> p a b", b=shape[1])
        if len(shape) == 3:
            a = a.rearrange("p (a b c) -> p a b c", b=shape[1], c=shape[2])
        return a


    def seed_ring(self, dve):
        z = self.small[0:1, 0:1]
        dve.memset(z, 0.0).then_inc(self.lo_ready, 6)
        dve.memset(self.small[0:1, 1:2], 0.0).then_inc(self.lo_ready_pool, 2)
        dve.memset(self.small[0:1, 2:3], 0.0).then_inc(self.pieces_used, RING)

    @staticmethod
    def lo_engine(g):
        return "pool" if g % 4 == 3 else "dve"

    def lo_wait(self, layer, base, pieces, g):
        quads = (base // 4) + layer * (pieces // 4) + g // 4
        if self.lo_engine(g) == "pool":
            return self.lo_ready_pool, quads + 3
        return self.lo_ready, quads * 3 + (7 + g % 4)

    def load_unit(self, sp, layer, base, pieces, u, job, n):
        quads = base // 4 + layer * (pieces // 4) + u // 2
        if u % 2 == 0:
            sp.wait_ge(self.lo_ready, quads * 3 + 2)
        else:
            sp.wait_ge(self.lo_ready, quads * 3 + 3)
            sp.sem_inc(self.passed, 1)
            sp.wait_ge(self.lo_ready_pool, quads + 1)
        sp.sem_inc(self.passed, 1)
        slot, k = u % RAW, job.unit
        r0 = (job.row + n * k) * P
        src = job.weight[layer, r0:r0 + k * P, job.col:job.col + job.cols].rearrange("(k p) c -> p k c", p=P)
        dst = self.raw[slot][:, 0:k * job.cols].rearrange("p (k c) -> p k c", k=k)
        sp.dma_start(dst, src).then_inc(self.unit_loaded[slot], 16)

    def piece_raw(self, plan, g):
        job, n = plan.pieces[g]
        w = job.unit // 2 * job.cols
        return self.raw[(g // 2) % RAW][:, n % 2 * w:n % 2 * w + w], w

    def split_hi(self, act, layer, base, plan, g):
        np_ = len(plan.pieces)
        src, w = self.piece_raw(plan, g)
        if g % 2 == 0:
            act.wait_ge(self.unit_loaded[(g // 2) % RAW],
                        (layer * (np_ // 8) + (base // 8 + g // 8 + 1)) * 16)
        act.wait_ge(self.pieces_used, layer * np_ + (base + g + 1))
        act.activation(self.hi[g % RING][:, 0:w], src, ACT.Copy).then_inc(self.hi_ready, 1)

    def split_lo(self, eng, layer, base, plan, g):
        np_ = len(plan.pieces)
        src, w = self.piece_raw(plan, g)
        eng.wait_ge(self.hi_ready, layer * np_ + (base + g + 1))
        sem = self.lo_ready_pool if self.lo_engine(g) == "pool" else self.lo_ready
        eng.tensor_tensor(self.lo[g % RING][:, 0:w], src, self.hi[g % RING][:, 0:w].bitcast(F32),
                          ALU.subtract).then_inc(sem, 1)

    def multiply(self, pe, layer, base, plan, g, rows=(0, 1)):
        job, n = plan.pieces[g]
        pe.wait_ge(*self.lo_wait(layer, base, len(plan.pieces), g))
        k, c, slot = job.unit // 2, job.cols, g % RING
        xh, xl = self.xh[job.xt], self.xl[job.xt]
        for kk in rows[:k]:
            row = job.xt_block + n * k + kk
            w = slice(kk * c, kk * c + c)
            for tb in range(TB):
                out, t = self.bank[job.banks[tb]][:, 0:c], slice(tb * P, tb * P + P)
                first = job.start and n == 0 and kk == 0
                last = job.stop and n == job.pieces - 1 and kk == k - 1
                pe.matmul(out, xh[:, row, t], self.hi[slot][:, w], start=first, stop=False)
                pe.matmul(out, xh[:, row, t], self.lo[slot][:, w], start=False, stop=False)
                mm = pe.matmul(out, xl[:, row, t], self.hi[slot][:, w], start=False, stop=last)
        if rows[-1] >= k - 1:
            mm.then_inc(self.pieces_used, 1)


SCORE, TURN, OUT = (4, 5), 6, 7


def bcast(ap, axis, n):
    a = ap.unsqueeze(axis)
    shape = list(a.shape)
    shape[axis] = n
    return a.to_broadcast(shape)


def turn_fill(nc, pe, core, bank, src, f):
    for j in range(2):
        for tb in range(TB):
            c = (2 * f + j) * P
            mm = pe.transpose(bank[:, (j * TB + tb) * P:(j * TB + tb + 1) * P],
                              src[:, tb, c:c + P], core.ident)
    return mm


def block_one(nc, core, s, plan, ins):
    q_tok, k_tok, qT, kT, va, vb, ya, yb, z = core.buf
    role = {"qa": q_tok, "ka": k_tok, "va": va, "qb": q_tok, "kb": k_tok, "vb": vb, "za": z, "zb": z,
            "ga": q_tok, "gb": k_tok, "mix": qT}
    source = {"h": q_tok, "qa": q_tok, "ka": k_tok, "qb": q_tok, "kb": k_tok, "ya": ya, "yb": yb, "mix": qT}
    target = {"qa": qT, "ka": kT, "qb": qT, "kb": kT}
    xt_of = {"h": 0, "ya": 1, "yb": 0, "mix": 1}
    gain_of = {"h": [0] * 0 + list(range(KB)), "yb": [KB] * KB}
    scr = core.scratch
    prob = [scr[:, i * 768:(i + 1) * 768].rearrange("p (m c) -> p m c", m=2) for i in range(2)]
    masked = scr[:, 1536:2304].rearrange("p (m c) -> p m c", m=2)
    turned = scr[:, 2304:2688]
    diff = scr[:, 2688:3072]
    junk = scr[:, 3072:4096]
    gated = scr[:, 4096:4096 + CH]
    rope_tmp = k_tok
    t = core.t1
    P_ = len(plan.pieces)
    base = 0
    at, up = s.at, s.up
    B = core.bank
    own, both = slice(P, 2 * P), slice(0, 2 * P)

    parts = [(0, slice(0, P), own), (1, slice(P, 3 * P), both)]

    @core.program("tensor")
    def _(pe):
        with pe.Fori(0, DEPTH) as layer:
            s.layer = layer
            last_read = {}

            def free(b):
                if b in last_read:
                    pe.wait_ge(*at(*last_read[b]))

            turn_at = 0
            for what in plan.steps:
                kind, arg = what[0], what[1] if len(what) > 1 else None
                if kind == "piece":
                    job, n = plan.pieces[arg]
                    if n == 0:
                        for b in job.banks:
                            free(b)
                        if job.name == "qa0":
                            pe.wait_ge(*at("cut", ("h", 3)))
                        if job.name == "pa0":
                            pe.wait_ge(*at("cut", ("ya", 3)))
                        if job.name == "pb0":
                            pe.wait_ge(*at("cut", ("yb", 3)))
                    if job.name == "out0" and n in (0, 2):
                        pe.wait_ge(*at("cut", ("mix", n + 1)))
                    core.multiply(pe, layer, base, plan, arg)
                    if n == job.pieces - 1:
                        for b in job.banks:
                            last_read[b] = ("sigmoid" if job.name[0] == "g" else "evac", job.name)
                if kind == "turn":
                    f = what[2]
                    b = (TURN, OUT)[turn_at % 2]
                    turn_at += 1
                    free(b)
                    if arg == "h":
                        pe.wait_ge(*at("h_ready"))
                    elif arg in ("qa", "ka", "qb", "kb"):
                        pe.wait_ge(*at("rotated", arg))
                    elif arg == "mix":
                        pe.wait_ge(*at("mix", f // 2))
                    else:
                        pe.wait_ge(*at("gated", arg[1]))
                    turn_fill(nc, pe, core, B[b], source[arg], f).then_inc(*up("turned", (arg, f)))
                    t.turn_bank[arg, f] = b
                    last_read[b] = ("cut" if arg in xt_of else "turn_copied", (arg, f))
                if kind == "a_scores":
                    h, b = arg, SCORE[arg % 2]
                    free(b)
                    pe.wait_ge(*at("turn_copied", ("ka", h // 4)))
                    r = slice(HD * (h % 2), HD * (h % 2) + HD)
                    pe.matmul(B[b][:, 0:P], qT_(qT)[r, h // 2, 0:P], qT_(kT)[r, h // 2, 0:P],
                              start=True, stop=True)
                    pe.matmul(B[b][:, P:3 * P], qT_(qT)[r, h // 2, P:S], qT_(kT)[r, h // 2, :],
                              start=True, stop=True).then_inc(*up("a_scored", h))
                    last_read[b] = ("a_max", h)
                if kind == "a_turn":
                    h = arg
                    free(TURN)
                    pe.wait_ge(*at("a_prob", h))
                    for c in range(3):
                        mm = pe.transpose(B[TURN][:, c * P:c * P + P], prob[h % 2][:, 0, c * P:c * P + P],
                                          core.ident)
                    mm.then_inc(*up("a_turned", h))
                    last_read[TURN] = ("a_copied", h)
                if kind == "a_out":
                    h = arg
                    free(OUT)
                    pe.wait_ge(*at("a_copied", h))
                    if h == 0:
                        pe.wait_ge(*at("evac", "va1"))
                    values = slice(h * HD, h * HD + HD)
                    pe.matmul(B[OUT][:, 0:HD], turned[:, 0:P], va[:, 0, values], start=True, stop=True)
                    pe.matmul(B[OUT][:, HD:2 * HD], turned[:, P:2 * P], va[:, 0, values], start=True, stop=False)
                    pe.matmul(B[OUT][:, HD:2 * HD], turned[:, 2 * P:3 * P], va[:, 1, values],
                              start=False, stop=True).then_inc(*up("a_summed", h))
                    last_read[OUT] = ("ya", h)
                if kind == "b_scores":
                    h = arg
                    pe.wait_ge(*at("turn_copied", ("kb", h // 2)))
                    for m in range(2):
                        b = SCORE[m]
                        free(b)
                        r = slice(HD * m, HD * m + HD)
                        pe.matmul(B[b][:, 0:P], qT_(qT)[r, h, 0:P], qT_(kT)[r, h, 0:P], start=True, stop=True)
                        pe.matmul(B[b][:, P:3 * P], qT_(qT)[r, h, P:S], qT_(kT)[r, h, :],
                                  start=True, stop=True).then_inc(*up("b_scored", (h, m)))
                        last_read[b] = ("b_max", (h, m))
                if kind == "b_turn":
                    h = arg
                    free(TURN)
                    pe.wait_ge(*at("b_diff", h))
                    for c in range(3):
                        mm = pe.transpose(B[TURN][:, c * P:c * P + P], diff[:, c * P:c * P + P], core.ident)
                    mm.then_inc(*up("b_turned", h))
                    last_read[TURN] = ("b_copied", h)
                if kind == "b_out":
                    h = arg
                    free(OUT)
                    pe.wait_ge(*at("b_copied", h))
                    if h == 0:
                        pe.wait_ge(*at("evac", "vb1"))
                    values = slice(h * DV, h * DV + DV)
                    pe.matmul(B[OUT][:, 0:DV], turned[:, 0:P], vb[:, 0, values], start=True, stop=True)
                    pe.matmul(B[OUT][:, DV:2 * DV], turned[:, P:2 * P], vb[:, 0, values], start=True, stop=False)
                    pe.matmul(B[OUT][:, DV:2 * DV], turned[:, 2 * P:3 * P], vb[:, 1, values],
                              start=False, stop=True).then_inc(*up("b_summed", h))
                    last_read[OUT] = ("yb", h)

    @core.program("scalar")
    def _(act):
        with act.Fori(0, DEPTH) as layer:
            s.layer = layer
            for g in range(LEAD):
                core.split_hi(act, layer, base, plan, g)
            for what in plan.steps:
                kind, arg = what[0], what[1] if len(what) > 1 else None
                if kind == "norm":
                    act.wait_ge(core.x_ready, layer + 1)
                    for tb in range(TB):
                        if tb:
                            act.wait_ge(*at("x_square", 0))
                        act.activation(junk, core.x[:, tb, :], ACT.Square,
                                       accum_out=t.ssq[:, tb:tb + 1]).then_inc(*up("x_square", tb))
                if kind == "piece" and arg + LEAD < P_:
                    core.split_hi(act, layer, base, plan, arg + LEAD)
                if kind == "turn" and arg in xt_of:
                    f = what[2]
                    act.wait_ge(*at("turned", (arg, f)))
                    bank = B[t.turn_bank[arg, f]][:, :].rearrange("p (j t) -> p j t", j=2)
                    xh = core.xh[xt_of[arg]]
                    if arg in gain_of:
                        for j in range(2):
                            gain = t.gain[:, gain_of[arg][2 * f + j]:gain_of[arg][2 * f + j] + 1]
                            act.activation(xh[:, 2 * f + j, :], bank[:, j, :], ACT.Copy,
                                           scale=gain).then_inc(*up("high", (arg, f, j)))
                    else:
                        act.activation(xh[:, 2 * f:2 * f + 2, :], bank, ACT.Copy).then_inc(*up("high", (arg, f, 1)))
                if kind == "evac" and arg[:2] in ("za", "zb", "ga", "gb"):
                    c = int(arg[2])
                    if arg == "zb0":
                        act.wait_ge(*at("gated", "a"))
                    if arg == "ga0":
                        act.wait_ge(*at("turned", ("qb", 3)))
                    if arg == "gb0":
                        act.wait_ge(*at("turned", ("kb", 3)))
                    for tb in range(TB):
                        act.wait_ge(core.pieces_used, layer * P_ + (base + plan.end[arg] + RING + 1))
                        ins = act.activation(role[arg[:2]][:, tb, c * CH:c * CH + CH],
                                             B[plan.by_name[arg].banks[tb]][:, :], ACT.Sigmoid)
                        if tb == TB - 1:
                            ins.then_inc(*up("sigmoid", arg))
                if kind == "a_scores":
                    h = arg
                    act.wait_ge(*at("a_max", h))
                    if h >= 2:
                        act.wait_ge(*at("a_turned", h - 2))
                    for tb, cols, _ in parts:
                        ins = act.activation(prob[h % 2][:, 0, cols], masked[:, h % 2, cols], ACT.Exp, scale=SCALE,
                                             bias=t.negmax[:, h % 2, tb:tb + 1],
                                             accum_out=t.total[:, h % 4, tb:tb + 1])
                    ins.then_inc(*up("a_prob", h))
                if kind == "b_scores":
                    h = arg
                    for m in range(2):
                        act.wait_ge(*at("b_max", (h, m)))
                        if h >= 2:
                            act.wait_ge(*at("b_diff", h - 2))
                        for tb, cols, _ in parts:
                            ins = act.activation(prob[h % 2][:, m, cols], masked[:, m, cols], ACT.Exp, scale=SCALE,
                                                 bias=t.negmax[:, m, tb:tb + 1],
                                                 accum_out=t.total[:, (h % 2) * 2 + m, tb:tb + 1])
                        ins.then_inc(*up("b_prob", (h, m)))
                if kind in ("a_turn", "b_turn"):
                    w, h = kind[0], arg
                    act.wait_ge(*at(f"{w}_turned", h))
                    if h >= 1:
                        act.wait_ge(*at(f"{w}_summed", h - 1))
                    act.activation(turned, B[TURN][:, 0:3 * P], ACT.Copy).then_inc(*up(f"{w}_copied", h))
                if kind == "b_out":
                    h = arg
                    act.wait_ge(*at("yb", h))
                    for tb in range(TB):
                        if h or tb:
                            act.wait_ge(*at("yb_square", (h, 0) if tb else (h - 1, 1)))
                        act.activation(junk[:, 0:DV], yb[:, tb, h * DV:h * DV + DV], ACT.Square,
                                       accum_out=t.head_ssq[:, tb, h:h + 1]).then_inc(*up("yb_square", (h, tb)))

    @core.program("vector")
    def _(dve):
        with dve.Fori(0, DEPTH) as layer:
            s.layer = layer
            dve.tensor_copy(t.gain[:, 0:KB + 1], t.gain_all[:, layer, :]).then_inc(*up("gain", 0))
            dve.tensor_copy(t.neglam[:, 0:1], t.neglam_all[:, layer, :]).then_inc(*up("gain", 1))
            for g in range(LEAD):
                if core.lo_engine(g) == "dve":
                    core.split_lo(dve, layer, base, plan, g)
            for what in plan.steps:
                kind, arg = what[0], what[1] if len(what) > 1 else None
                if kind == "piece" and arg + LEAD < P_ and core.lo_engine(arg + LEAD) == "dve":
                    core.split_lo(dve, layer, base, plan, arg + LEAD)
                if kind == "norm":
                    dve.wait_ge(*at("rstd"))
                    for tb in range(TB):
                        ins = dve.tensor_scalar(q_tok[:, tb, :], core.x[:, tb, :], t.rstd[:, tb:tb + 1], None, ALU.mult)
                    ins.then_inc(*up("h_ready"))
                if kind == "turn":
                    f = what[2]
                    bank = B[t.turn_bank[arg, f]][:, :].rearrange("p (j t) -> p j t", j=2)
                    if arg in xt_of:
                        xh, xl = core.xh[xt_of[arg]], core.xl[xt_of[arg]]
                        if arg in gain_of:
                            for j in range(2):
                                n = 2 * f + j
                                gain = t.gain[:, gain_of[arg][n]:gain_of[arg][n] + 1]
                                dve.wait_ge(*at("high", (arg, f, 1)))
                                ins = dve.scalar_tensor_tensor(xl[:, n, :], bank[:, j, :], gain,
                                                               xh[:, n, :].bitcast(F32), ALU.mult, ALU.subtract)
                        else:
                            dve.wait_ge(*at("high", (arg, f, 1)))
                            ins = dve.tensor_tensor(xl[:, 2 * f:2 * f + 2, :], bank,
                                                    xh[:, 2 * f:2 * f + 2, :].bitcast(F32), ALU.subtract)
                        ins.then_inc(*up("cut", (arg, f)))
                    else:
                        dve.wait_ge(*at("turned", (arg, f)))
                        if arg in ("qb", "kb") and f == 0:
                            dve.wait_ge(*at("a_scored", HEADS - 1))
                        dve.tensor_copy(qT_(target[arg])[:, 2 * f:2 * f + 2, :], bank)\
                           .then_inc(*up("turn_copied", (arg, f)))
                if kind == "evac":
                    job, c = plan.by_name[arg], int(arg[-1])
                    cols = slice(c * CH, c * CH + CH)
                    name = arg[:-1]
                    done = (core.pieces_used, layer * P_ + (base + plan.end[arg] + RING + 1))
                    if name in ("qa", "ka", "va", "qb", "kb", "vb"):
                        if arg == "qa0":
                            dve.wait_ge(*at("turned", ("h", 3)))
                        if arg == "qb0":
                            dve.wait_ge(*at("turned", ("qa", 3)))
                        if arg == "kb0":
                            dve.wait_ge(*at("turned", ("ka", 3)))
                        for tb in range(TB):
                            dve.wait_ge(*done)
                            ins = dve.tensor_copy(role[name][:, tb, cols], B[job.banks[tb]][:, :])
                        ins.then_inc(*up("evac", arg))
                    if name in ("za", "zb"):
                        for tb in range(TB):
                            dve.wait_ge(*at("sigmoid", arg))
                            ins = dve.tensor_tensor(z[:, tb, cols], B[job.banks[tb]][:, :], z[:, tb, cols], ALU.mult)
                        ins.then_inc(*up("evac", arg))
                    if name == "pa":
                        for tb in range(TB):
                            dve.wait_ge(*done)
                            dve.wait_ge(*at("sigmoid", "ga1"))
                            dve.wait_ge(*at("b_scored", (DHEADS - 1, 1)))
                            ins = dve.tensor_tensor(qT[:, tb, cols], B[job.banks[tb]][:, :], q_tok[:, tb, cols], ALU.mult)
                        ins.then_inc(*up("evac", arg))
                    if name == "pb":
                        for tb in range(TB):
                            dve.wait_ge(*done)
                            dve.wait_ge(*at("sigmoid", "gb1"))
                            dve.tensor_tensor(k_tok[:, tb, cols], B[job.banks[tb]][:, :], k_tok[:, tb, cols],
                                              ALU.mult).then_inc(*up("evac", (arg, tb)))
                        dve.wait_ge(*at("evac", (arg, 1)))
                        dve.wait_ge(*at("evac", "pa1"))
                        dve.tensor_tensor(qT[:, :, cols], qT[:, :, cols], k_tok[:, :, cols], ALU.add)\
                           .then_inc(*up("mix", c))
                        s.keys["evac", arg] = s.keys["evac", (arg, 1)]
                    if name == "out":
                        for tb in range(TB):
                            dve.wait_ge(*done)
                            ins = dve.tensor_tensor(core.x[:, tb, cols], B[job.banks[tb]][:, :],
                                                    core.x[:, tb, cols], ALU.add)
                        if c == 1:
                            ins.then_inc(core.x_ready, 1)
                if kind == "a_scores":
                    h = arg
                    masked_max(dve, core, s, B[SCORE[h % 2]], masked[:, h % 2, :], t.top[:, h % 2, :],
                               t.negmax[:, h % 2, :], parts, 0, ("a_scored", h), ("a_prob", h - 2) if h >= 2 else None,
                               ("a_top", h), ("a_max", h))
                if kind == "b_scores":
                    h = arg
                    for m in range(2):
                        masked_max(dve, core, s, B[SCORE[m]], masked[:, m, :], t.top[:, m, :],
                                   t.negmax[:, m, :], parts, 1, ("b_scored", (h, m)),
                                   ("b_prob", (h - 1, m)) if h >= 1 else ("a_prob", HEADS - 1),
                                   ("b_top", (h, m)), ("b_max", (h, m)))
                if kind == "a_turn":
                    h = arg
                    dve.wait_ge(*at("a_prob", h))
                    dve.reciprocal(t.inverse[:, h % 4, :], t.total[:, h % 4, :]).then_inc(*up("a_inverse", h))
                if kind == "a_out":
                    h = arg
                    dve.wait_ge(*at("a_summed", h))
                    dve.wait_ge(*at("a_inverse", h))
                    dve.tensor_tensor(ya[:, :, h * HD:h * HD + HD],
                                      B[OUT][:, 0:2 * HD].rearrange("p (t d) -> p t d", t=TB),
                                      bcast(t.inverse[:, h % 4, :], 2, HD), ALU.mult).then_inc(*up("ya", h))
                if kind == "b_turn":
                    h = arg
                    i = (h % 2) * 2
                    dve.wait_ge(*at("b_prob", (h, 1)))
                    dve.reciprocal(t.inverse[:, i:i + 2, :], t.total[:, i:i + 2, :]).then_inc(*up("b_inverse", h))
                    dve.wait_ge(*at("b_inverse", h))
                    dve.scalar_tensor_tensor(t.weight[:, 0:2], t.inverse[:, i + 1, :], t.neglam[:, 0:1],
                                             t.total[:, i, :], ALU.mult, ALU.mult).then_inc(*up("b_weight", h))
                    dve.wait_ge(*at("b_weight", h))
                    if h >= 1:
                        dve.wait_ge(*at("b_turned", h - 1))
                    for tb, cols, _ in parts:
                        ins = dve.scalar_tensor_tensor(diff[:, cols], prob[h % 2][:, 1, cols], t.weight[:, tb:tb + 1],
                                                       prob[h % 2][:, 0, cols], ALU.mult, ALU.add)
                    ins.then_inc(*up("b_diff", h))
                if kind == "b_out":
                    h = arg
                    i = (h % 2) * 2
                    dve.wait_ge(*at("b_summed", h))
                    dve.tensor_tensor(yb[:, :, h * DV:h * DV + DV],
                                      B[OUT][:, 0:2 * DV].rearrange("p (t d) -> p t d", t=TB),
                                      bcast(t.inverse[:, i, :], 2, DV), ALU.mult).then_inc(*up("yb", h))

    @core.program("gpsimd")
    def _(pool):
        with pool.Fori(0, DEPTH) as layer:
            s.layer = layer
            for what in plan.steps:
                kind, arg = what[0], what[1] if len(what) > 1 else None
                if kind == "piece" and arg + LEAD < P_ and core.lo_engine(arg + LEAD) == "pool":
                    core.split_lo(pool, layer, base, plan, arg + LEAD)
                if kind == "norm":
                    pool.wait_ge(*at("x_square", 1))
                    rsqrt(pool, s, core, t.ssq[:, 0:TB], t.rstd[:, 0:TB], 1.0 / D, 1e-6, "rstd_mean", "rstd", 0)
                if kind == "rope":
                    rotate(pool, s, role[arg], core.rope1, t.rot[0], t.rot[1], ("evac", f"{arg}1"), arg, HEADS)
                if kind == "head_norm":
                    pool.wait_ge(*at("yb_square", (DHEADS - 1, 1)))
                    rsqrt(pool, s, core, t.head_ssq, t.head_rstd, 1.0 / DV, 1e-5, "head_mean", "head_rstd", 0)
                    pool.wait_ge(*at("head_rstd"))
                    v = yb[:, :, :].rearrange("p t (h d) -> p (t h) d", d=DV)
                    pool.tensor_tensor(v, v, bcast(t.head_rstd.rearrange("p t h -> p (t h)"), 2, DV), ALU.mult)\
                        .then_inc(*up("head_normed"))
                if kind == "gate":
                    y, zz = (ya, "za1") if arg == "a" else (yb, "zb1")
                    pool.wait_ge(*at("evac", zz))
                    pool.wait_ge(*(at("ya", HEADS - 1) if arg == "a" else at("head_normed")))
                    pool.tensor_tensor(y[:, :, :], y[:, :, :], z[:, :, :], ALU.mult).then_inc(*up("gated", arg))

    @core.program("sync")
    def _(sp):
        with sp.Fori(0, DEPTH) as layer:
            for u, (job, n) in enumerate(plan.units):
                job.weight = ins[job.weight] if isinstance(job.weight, str) else job.weight
                core.load_unit(sp, layer, base, P_, u, job, n)


def qT_(buf):
    return buf[:, :, :].rearrange("p a b -> p (a b)").rearrange("p (k t) -> p k t", t=S)


def masked_max(dve, core, s, bank, masked, top, negmax, parts, which, scored, tile_free, top_sig, done, sink=None):
    dve.wait_ge(*s.at(*scored))
    if tile_free:
        dve.wait_ge(*s.at(*tile_free))
    dve.sem_inc(core.passed, 1)
    for tb, cols, keys in parts:
        ins = dve.tensor_tensor_reduce(masked[:, cols], bank[:, cols], core.masks[:, which, keys], 1.0,
                                       NEG if sink is None else sink[0],
                                       ALU.add, ALU.max, top[:, tb:tb + 1])
    ins.then_inc(*s.up(*top_sig))
    dve.wait_ge(*s.at(*top_sig))
    if sink:
        dve.tensor_scalar(sink[1], top[:, :], sink[0], -SCALE, ALU.subtract, ALU.mult)
    dve.tensor_scalar(negmax[:, :], top[:, :], -SCALE, None, ALU.mult).then_inc(*s.up(*done))


def rsqrt(pool, s, core, total, out, scale, eps, mean_sig, done_sig, key):
    pool.sem_inc(core.passed, 1)
    pool.tensor_scalar(out, total, scale, eps, ALU.mult, ALU.add).then_inc(*s.up(mean_sig, key))
    pool.wait_ge(*s.at(mean_sig, key))
    n = int(np.prod(out.shape[1:]))
    half = core.t1.minus_half[:, 0:n]
    if len(out.shape) == 3:
        half = half.rearrange("p (a b) -> p a b", b=out.shape[2])
    pool.tensor_tensor(out, out, half, ALU.pow).then_inc(*s.up(done_sig, key))


def rotate(pool, s, buf, table, r0, r1, ready, name, heads):
    half = ROT // 2
    pool.wait_ge(*s.at(*ready))
    for tb in range(TB):
        v = buf[:, tb, 0:heads * HD].rearrange("p (h d) -> p h d", d=HD)
        a, b = v[:, :, 0:half], v[:, :, half:ROT]
        cos = bcast(table[:, tb, 0, :], 1, heads)
        if tb == 0 and name in s.rot_before:
            pool.wait_ge(*s.at("rotated", s.rot_before[name]))
        if tb:
            pool.wait_ge(*s.at("rot_done", (name, 0)))
        pool.tensor_tensor(r0[:, 0:heads, 0:half], b, bcast(table[:, tb, 2, :], 1, heads), ALU.mult)
        pool.tensor_tensor(r0[:, 0:heads, half:ROT], a, bcast(table[:, tb, 3, :], 1, heads), ALU.mult)
        pool.tensor_tensor(r1[:, 0:heads, 0:half], a, cos, ALU.mult)
        pool.tensor_tensor(r1[:, 0:heads, half:ROT], b, cos, ALU.mult).then_inc(*s.up("rot_parts", (name, tb)))
        pool.wait_ge(*s.at("rot_parts", (name, tb)))
        pool.tensor_tensor(v[:, :, 0:ROT], r0[:, 0:heads, :], r1[:, 0:heads, :], ALU.add)\
            .then_inc(*s.up("rot_done" if tb < TB - 1 else "rotated", (name, tb) if tb < TB - 1 else name))


class Tiles:
    pass


def setup(nc, core, s, ins):
    t = core.t1 = Tiles()
    t.ssq, t.rstd = core.tile(TB), core.tile(TB)
    t.head_ssq, t.head_rstd = core.tile(TB, DHEADS), core.tile(TB, DHEADS)
    t.top, t.negmax = core.tile(2, TB), core.tile(2, TB)
    t.total, t.inverse, t.weight = core.tile(4, TB), core.tile(4, TB), core.tile(TB)
    t.gain, t.gain_all = core.tile(KB + 1), core.tile(DEPTH, KB + 1)
    t.neglam, t.neglam_all = core.tile(1), core.tile(DEPTH, 1)
    t.minus_half = core.tile(32)
    t.rot = [core.tile(HEADS, ROT) for _ in range(0)] or [
        core.scratch[:, 4608:4864].rearrange("p (h d) -> p h d", d=ROT),
        core.scratch[:, 4864:5120].rearrange("p (h d) -> p h d", d=ROT)]
    t.turn_bank = {}
    s.rot_before = {"ka": "qa", "qb": "ka", "kb": "qb"}
    at, up = s.at, s.up
    rows = core.buf[8][:, 0, 0:P]
    lam = core.scratch[:, 0:4 * DEPTH * HD].rearrange("p (n l d) -> p n l d", n=4, l=DEPTH)
    dots = core.tile(2, DEPTH)
    junk = core.scratch[:, 1024:1024 + HD]
    R = KB + 1

    @core.program("sync")
    def _(sp):
        for tb in range(TB):
            sp.dma_start(core.x[:, tb, :], ins["x"][0, tb * P:tb * P + P, :]).then_inc(*up("x_loaded", tb, 16))
        sp.dma_start(core.square[:, :, :], ins["square"]).then_inc(*up("square_loaded", 0, 16))
        for l in range(DEPTH):
            sp.dma_start(rows[l * R:l * R + KB, :], ins["norm_w"][l].rearrange("(k p) -> k p", p=P))\
              .then_inc(*up("rows_loaded", (l, 0), 16))
            sp.dma_start(rows[l * R + KB:l * R + R, :], ins["subln_w"][l:l + 1, :])\
              .then_inc(*up("rows_loaded", (l, 1), 16))
        for n, name in enumerate(("lambda_q1", "lambda_k1", "lambda_q2", "lambda_k2")):
            sp.dma_start(lam[:, n, :, :], ins[name].partition_broadcast(P)).then_inc(*up("lambda_loaded", n, 16))
        sp.dma_start(core.masks[:, :, :], ins["masks"]).then_inc(*up("tables_loaded", 0, 16))
        sp.dma_start(core.rope1[:, :, :, :], ins["rope"].rearrange("t p (r d) -> p t r d", d=ROT // 2))\
          .then_inc(*up("tables_loaded", 1, 16))

    @core.program("tensor")
    def _(pe):
        pe.wait_ge(*at("square_loaded"))
        pe.wait_ge(*at("rows_loaded", (DEPTH - 1, 1)))
        pe.transpose(core.bank[TURN][:, 0:DEPTH * R], rows[0:DEPTH * R, :],
                     core.ident[0:DEPTH * R, 0:DEPTH * R]).then_inc(*up("gains_turned"))

    @core.program("scalar")
    def _(act):
        act.wait_ge(*at("dots", (1, DEPTH - 1)))
        act.activation(dots, dots, ACT.Exp).then_inc(*up("dots_exp"))

    @core.program("vector")
    def _(dve):
        core.seed_ring(dve)
        dve.memset(t.minus_half, -0.5).then_inc(*up("minus_half"))
        dve.wait_ge(*at("gains_turned"))
        dve.tensor_copy(t.gain_all, core.bank[TURN][:, 0:DEPTH * R].rearrange("p (l r) -> p l r", r=R))\
           .then_inc(*up("gains", 0))
        dve.wait_ge(*at("lambda_loaded", 3))
        for n in range(2):
            for l in range(DEPTH):
                if n or l:
                    dve.wait_ge(*at("dots", (n, 0) if l else (n - 1, DEPTH - 1)))
                dve.tensor_tensor_reduce(junk, lam[:, 2 * n, l, :], lam[:, 2 * n + 1, l, :], 1.0, 0.0,
                                         ALU.mult, ALU.add, dots[:, n, l:l + 1]).then_inc(*up("dots", (n, l)))
        dve.wait_ge(*at("dots_exp"))
        dve.tensor_tensor(t.neglam_all.rearrange("p l a -> p (l a)"), dots[:, 1, :], dots[:, 0, :], ALU.subtract).then_inc(*up("neglam", 0))
        dve.wait_ge(*at("neglam", 0))
        dve.wait_ge(*at("gains", 0))
        for l in range(DEPTH):
            dve.tensor_scalar(t.neglam_all[:, l, :], t.neglam_all[:, l, :], -lambda_init(l), None,
                              ALU.add).then_inc(*up("neglam", l + 1))
            g = t.gain_all[:, l, KB:KB + 1]
            dve.tensor_scalar(g, g, 1.0 - lambda_init(l), None, ALU.mult).then_inc(*up("gains", l + 1))
        dve.wait_ge(*at("neglam", DEPTH))
        dve.wait_ge(*at("gains", DEPTH))
        dve.wait_ge(*at("tables_loaded", 1))
        dve.wait_ge(*at("x_loaded", 1))
        dve.memset(t.top, 0.0).then_inc(core.x_ready, 1)


def final_norm(nc, core, s, ins):
    t = core.t1
    row = core.buf[3][:, 0, :]
    junk = core.buf[3][:, 1, :]
    at, up = s.at, s.up

    @core.program("scalar")
    def _(act):
        act.wait_ge(core.x_ready, DEPTH + 1)
        act.dma_start(row, ins["final_norm_w"].partition_broadcast(P)).then_inc(*up("row_loaded", 0, 16))
        for tb in range(TB):
            if tb:
                act.wait_ge(*at("x_square", 0))
            act.activation(junk, core.x[:, tb, :], ACT.Square,
                           accum_out=t.ssq[:, tb:tb + 1]).then_inc(*up("x_square", tb))

    @core.program("gpsimd")
    def _(pool):
        pool.wait_ge(*at("x_square", 1))
        rsqrt(pool, s, core, t.ssq[:, 0:TB], t.rstd[:, 0:TB], 1.0 / D, 1e-6, "final_mean", "final_rstd", 0)

    @core.program("vector")
    def _(dve):
        dve.wait_ge(*at("row_loaded"))
        dve.wait_ge(*at("final_rstd"))
        for tb in range(TB):
            ins_ = dve.scalar_tensor_tensor(core.x[:, tb, :], core.x[:, tb, :], t.rstd[:, tb:tb + 1], row,
                                            ALU.mult, ALU.mult)
        ins_.then_inc(core.x_ready, 1)


def store(nc, core, s, out, layers):
    @core.program("sync")
    def _(sp):
        sp.wait_ge(core.x_ready, layers)
        for tb in range(TB):
            sp.dma_start(out[0, tb * P:tb * P + P, :], core.x[:, tb, :]).then_inc(*s.up("stored", tb, 16))
        sp.wait_ge(*s.at("stored", TB - 1))



def plan_two():
    p = Plan()
    sec = lambda n, col: section(n, "w_in_2", col, 0)
    small = 2 * DHEADS + 256
    at_sw = 4 * D
    p.step("norm")
    for t in turns("h"):
        p.steps.extend(t)
    p.run([Job("ba0", "w_in_2", 0, at_sw, KB, small, 2, 0, 0, (2, 3))])
    p.run(sec("sq", at_sw + small), [[("decay",)], [("decay_sum",)]])
    work = attention("s", HEADS)
    p.run(sec("dq", 0), [[("rope", "sk"), ("rope", "sq")], [], [("turn", "sk", 0)]] + turns("sq")
          + [work[0]])
    conv = lambda n: spread(turns(n), 2)
    p.run(sec("dk", D), [a + b for a, b in zip(conv("dq"), work[1:9])])
    p.run(sec("dv", 2 * D), [a + b for a, b in zip([[("silu", "dq")]] + conv("dk")[:7], work[9:17])])
    groups = [[step] for g in range(DHEADS // 2) for step in delta_steps(g)]
    before = [conv("dk")[7] + work[17] + [("silu", "dk")], [("squares", "dq")], [("squares", "dk")],
              [("scales",)], [("turn", "dv", 0)], [("turn", "dv", 1)], [("turn", "dv", 2)],
              [("turn", "dv", 3)], [("silu", "dv")]]
    slots = [[] for _ in range(64)]
    for i, b in enumerate(before):
        slots[i] += b
    first = 4
    back = [[("turn", "v", f)] for f in range(4)] + [[("turn", "kd", f)] for f in range(2)]
    for i, b in enumerate(back):
        slots[9 + i] += b
    room = len(slots) - first - 4
    for i, b in enumerate(groups):
        slots[first + i * room // len(groups)] += b
    ys = turns("ys")
    for i in range(4):
        slots[34 + 3 * i] += ys[i]
    p.run(sec("gb", at_sw + small + 2 * CH + D), slots[:16], halves=True)
    p.run(sec("ga", at_sw + small + 2 * CH), slots[16:32], halves=True)
    p.run(sec("zz", 3 * D), slots[32:48], halves=True)
    p.run(section("us", "w_up_sw_2", 0, 1), slots[48:], halves=True)
    p.step("post_rows")
    p.step("head_norm")
    for t in turns("yd"):
        p.steps.extend(t)
    ud = section("ud", "w_up_dn_2", 0, 0)
    p.run(ud[:1])
    p.run(ud[1:], [[], [("turn", "mix", 0)], [("turn", "mix", 1)], []])
    p.step("turn", "mix", 2)
    p.step("turn", "mix", 3)
    p.run(section("oo", "w_o_2", 0, 1))
    p.step("post", 0)
    p.step("norm_mlp")
    for t in turns("h2"):
        p.steps.extend(t)
    parts = 4 * D // CH
    up_ = lambda j: [Job(f"up{j}", "w_ff1_2", 0, j * CH, KB, CH, 4, 0, 0, SCORE)]
    p.run(up_(0))
    for j in range(parts):
        turn = [[], [("turn", f"f{j}", 0)], [("turn", f"f{j}", 1)], []]
        if j + 1 < parts:
            p.run(up_(j + 1), turn)
        else:
            for steps in turn:
                p.steps.extend(steps)
        p.run([Job(f"dn{j}_{c}", "w_ff2_2", 4 * j, c * CH, 4, CH, 4, 1, 4 * (j % 2), (2 * c, 2 * c + 1),
                   start=j == 0, stop=j == parts - 1) for c in range(2)])
    p.step("post", 1)
    return p.close()


def delta_steps(g):
    steps = [("rows", g), ("gram", g), ("inverse", g)]
    for l in range(1, LEVELS):
        steps += [("level_y", g, l), ("level_t", g, l)]
    return steps + [("delta_u", g), ("delta_s", g), ("delta_r", g), ("delta_v", g), ("delta_o", g)]


def setup_two(nc, core, s, ins):
    t2 = core.t2 = Tiles()
    t1 = core.t1
    R = 2 * KB + 1 + 4 * 3 * DHEADS
    t2.cols, t2.cols_all = core.tile(R), core.tile(DEPTH, R)
    t2.sink, t2.sink_all = core.tile(HEADS), core.tile(DEPTH, HEADS)
    t2.nega, t2.nega_all = core.tile(DHEADS), core.tile(DEPTH, DHEADS)
    t2.dtb, t2.dtb_all = core.tile(DHEADS), core.tile(DEPTH, DHEADS)
    at, up = s.at, s.up
    half = ROT // 2
    late = core.buf[7][:, :, :].rearrange("p a b -> p (a b)")
    rows = [late[:, l * P:l * P + P] for l in range(DEPTH)]
    work = late[:, 1024:1024 + 12 * TB * half].rearrange("p (n t r) -> p n t r", n=12, t=TB)
    pos_i = late[:, 1400:1400 + TB].bitcast(I32)
    pos = late[:, 1404:1404 + TB]
    inv = late[:, 1410:1410 + half]
    chain = [0]

    @core.program("sync")
    def _(sp):
        for l in range(DEPTH):
            for n, (name, k) in enumerate((("pre_mix_g_2", KB), ("pre_mlp_g_2", KB))):
                sp.dma_start(rows[l][n * KB:n * KB + k, :], ins[name][l].rearrange("(k p) -> k p", p=P))\
                  .then_inc(*up("rows", (l, n), 16))
            sp.dma_start(rows[l][2 * KB:2 * KB + 1, :], ins["dn_norm_g_2"][l:l + 1, :]).then_inc(*up("rows", (l, 2), 16))
            sp.dma_start(rows[l][2 * KB + 1:R, :], ins["dn_conv_w_2"][l].rearrange("j (k p) -> (j k) p", p=P))\
              .then_inc(*up("rows", (l, 3), 16))
        sp.dma_start(t2.sink_all, ins["sw_sinks_2"].partition_broadcast(P)).then_inc(*up("vectors", 0, 16))
        sp.dma_start(t2.nega_all, ins["dn_a_log_2"].partition_broadcast(P)).then_inc(*up("vectors", 1, 16))
        sp.dma_start(t2.dtb_all, ins["dn_dt_bias_2"].partition_broadcast(P)).then_inc(*up("vectors", 2, 16))
        sp.dma_start(inv, ins["inv_freq"]).then_inc(*up("positions", 0, 16))
        for tb in range(TB):
            sp.dma_start(pos_i[:, tb:tb + 1], ins["positions_2"][0, tb * P:tb * P + P].unsqueeze(1))\
              .then_inc(*up("positions", 1 + tb, 16))

    @core.program("tensor")
    def _(pe):
        pe.wait_ge(*at("rows", (DEPTH - 1, 3)))
        for l in range(DEPTH):
            pe.transpose(core.bank[SCORE[l]][:, 0:R], rows[l][0:R, :], core.ident[0:R, 0:R]).then_inc(*up("turned", l))

    @core.program("vector")
    def _(dve):
        for l in range(DEPTH):
            dve.wait_ge(*at("turned", l))
            dve.tensor_copy(t2.cols_all[:, l, :], core.bank[SCORE[l]][:, 0:R]).then_inc(*up("cols", l))
        dve.wait_ge(*at("exp_a"))
        dve.tensor_scalar(t2.nega_all, t2.nega_all, -1.0, None, ALU.mult).then_inc(*up("nega"))

        def link(ins_):
            chain[0] += 1
            ins_.then_inc(*up("chain", chain[0]))
            dve.wait_ge(*at("chain", chain[0]))

        def parts(x):
            out = []
            for _ in range(3):
                a = float(np.float32(x)) if len(out) == 2 else math.ldexp(round(math.ldexp(x, 10 - math.frexp(x)[1])), math.frexp(x)[1] - 10)
                out.append(a)
                x -= a
            return out

        dve.wait_ge(*at("positions", TB))
        link(dve.tensor_copy(pos, pos_i))
        ang, n, r, c = (work[:, i, :, :] for i in range(4))
        for tb in range(TB):
            link(dve.tensor_scalar(ang[:, tb, :], inv, pos[:, tb:tb + 1], None, ALU.mult))
        magic = 1.5 * 2.0 ** 23

        def reduce(out, src, period, shift):
            link(dve.tensor_scalar(n, src, 1.0 / period, shift, ALU.mult, ALU.add))
            link(dve.tensor_scalar(n, n, magic, None, ALU.add))
            link(dve.tensor_scalar(n, n, -magic, None, ALU.add))
            for i, part in enumerate(parts(period)):
                link(dve.scalar_tensor_tensor(out, n, -part, src if i == 0 else out, ALU.mult, ALU.add))

        two_pi = 2 * math.pi
        reduce(r, ang, 2048 * two_pi, 0.0)
        reduce(c, r, two_pi, 0.25)
        link(dve.tensor_scalar(c, c, math.pi / 2, None, ALU.add))
        reduce(r, r, two_pi, 0.0)
        edge = float(np.float32(3.1415925))
        for a in (c, r):
            link(dve.tensor_scalar(a, a, edge, -edge, ALU.min, ALU.max))
        s.keys["chain", "reduced"] = s.keys["chain", chain[0]]
        dve.wait_ge(*at("sines", 1))
        rope = core.rope2
        link(dve.tensor_copy(rope[:, :, 0, :], work[:, 4, :, :]))
        link(dve.tensor_copy(rope[:, :, 1, :], work[:, 4, :, :]))
        link(dve.tensor_copy(rope[:, :, 3, :], work[:, 5, :, :]))
        dve.tensor_scalar(rope[:, :, 2, :], work[:, 5, :, :], -1.0, None, ALU.mult).then_inc(*up("rope"))

    @core.program("scalar")
    def _(act):
        act.wait_ge(*at("vectors", 2))
        act.activation(t2.nega_all, t2.nega_all, ACT.Exp).then_inc(*up("exp_a"))
        act.wait_ge(*at("chain", "reduced"))
        act.activation(work[:, 4, :, :], work[:, 3, :, :], ACT.Sin).then_inc(*up("sines", 0))
        act.activation(work[:, 5, :, :], work[:, 2, :, :], ACT.Sin).then_inc(*up("sines", 1))


def block_two(nc, core, s, plan, ins, base):
    b0, b1, qd, kd_T, vb, qs, ys, zz, b8 = core.buf
    flat8 = b8[:, :, :].rearrange("p a b -> p (a b)")
    k_dup = flat8[:, 0:512].rearrange("p (t c) -> p t c", t=TB)
    ks = flat8[:, 512:1024].rearrange("p (k t) -> p k t", t=S)
    vs = flat8[:, 1024:1280].rearrange("p (t c) -> p t c", t=TB)
    k_dec = flat8[:, 0:1024].rearrange("p (h d) -> p h d", d=P)
    source = {"h": b1, "sq": b0, "sk": k_dup, "dq": b1, "dk": b0, "dv": b1, "ys": ys, "yd": vb,
              "mix": qs, "h2": b1}
    xt_of = {"h": 0, "ys": 1, "yd": 0, "mix": 1, "h2": 0}
    gain_of = {"h": list(range(KB)), "h2": list(range(KB, 2 * KB)), "yd": [2 * KB] * KB}
    tap = lambda j, n: 2 * KB + 1 + j * 3 * DHEADS + n
    conv_out = {"dq": (qd, 0), "dk": (kd_T, DHEADS), "dv": (zz, 2 * DHEADS)}
    scr = core.scratch
    prob = [scr[:, i * 384:(i + 1) * 384] for i in range(2)]
    masked = [scr[:, 768 + i * 384:768 + (i + 1) * 384] for i in range(2)]
    turned = scr[:, 2304:2688]
    junk = scr[:, 3072:4096]

    def region(first, n, *shape):
        a = scr[:, first:first + n]
        if len(shape) == 2:
            return a.rearrange("p (a b) -> p a b", b=shape[1])
        return a.rearrange("p (h c t) -> p h c t", c=shape[1], t=shape[2])

    decay = region(0, 512, 2, TB, P)
    score = region(512, 512, 2, TB, P)
    lm = [region(1024 + 512 * i, 512, 2, TB, P) for i in range(2)]
    tr = [scr[:, 2048 + 512 * i:2560 + 512 * i].rearrange("p (c w t) -> p c w t", c=TB, w=2) for i in range(2)]
    tr_all = scr[:, 2048:3072].rearrange("p (h c w t) -> p (h c) w t", h=2, c=TB, w=2)
    yy = region(3072, 512, 2, TB, P)
    state, uu, rr, xx = (region(3584 + 256 * i, 256, 2, P) for i in range(4))
    t1, t = core.t1, core.t2
    t.ba = core.tile(TB, 2 * DHEADS)
    t.beta, t.g, t.abs, t.soft = (core.tile(TB, DHEADS) for _ in range(4))
    t.cum, t.ec = core.tile(TB, DHEADS), core.tile(2, DHEADS)
    t.ssq2, t.rk, t.rq, t.brk = (core.tile(TB, DHEADS) for _ in range(4))
    t.kds, t.rs = core.tile(DHEADS), core.tile(DHEADS)
    t.sinkexp = core.tile(2, TB)
    t.junk = scr[:, 4608:4736]
    t.turn_bank = {}
    s.rot_before = {"sq": "sk"}
    P_ = len(plan.pieces)
    at, up = s.at, s.up
    B = core.bank
    own, both = slice(P, 2 * P), slice(0, 2 * P)
    parts = [(0, slice(0, P), own), (1, slice(P, 3 * P), both)]
    HC = [(h, c) for h in range(2) for c in range(TB)]
    level_mask = lambda l: core.square[:, 3 + l, :]
    f_src = lambda j: b0 if j % 2 == 0 else b1

    def ended(name, layer):
        return core.pieces_used, layer * P_ + (base + plan.end[name] + RING + 1)

    def is_cut(name):
        return name in xt_of or name[0] == "f"

    @core.program("tensor")
    def _(pe):
        with pe.Fori(0, DEPTH) as layer:
            s.layer = layer
            last_read = {}
            turn_at = 0

            def free(b):
                if b in last_read:
                    pe.wait_ge(*at(*last_read[b]))

            for what in plan.steps:
                kind, arg = what[0], what[1] if len(what) > 1 else None
                if kind == "piece":
                    job, n = plan.pieces[arg]
                    if n == 0 and job.start:
                        for b in job.banks:
                            free(b)
                    if n == 0:
                        ready = {"ba0": ("cut", ("h", 3)), "us0": ("cut", ("ys", 3)), "ud0": ("cut", ("yd", 3)),
                                 "up0": ("cut", ("h2", 3))}.get(job.name)
                        if ready:
                            pe.wait_ge(*at(*ready))
                        if job.name[:2] == "dn":
                            pe.wait_ge(*at("cut", ("f" + job.name[2], 1)))
                    if job.name == "oo0" and n in (0, 2):
                        pe.wait_ge(*at("cut", ("mix", n + 1)))
                    core.multiply(pe, layer, base, plan, arg, (0,) if what[-1] == "half" else (0, 1))
                if kind == "more":
                    job, n = plan.pieces[arg]
                    core.multiply(pe, layer, base, plan, arg, (1,))
                if kind in ("piece", "more"):
                    if n == job.pieces - 1 and what[-1] != "half":
                        name = "sigmoid" if job.name[:2] in ("ga", "gb") else "evac"
                        for b in job.banks:
                            last_read[b] = (name, job.name)
                if kind == "turn":
                    f = what[2]
                    b = (TURN, OUT)[turn_at % 2]
                    turn_at += 1
                    free(b)
                    wait = {"h": ("h_ready", 0), "h2": ("h_ready", 1), "sq": ("rotated", "sq"), "sk": ("rotated", "sk"),
                            "dq": ("evac", "dq1"), "dk": ("evac", "dk1"), "dv": ("evac", "dv1"),
                            "ys": ("ys", HEADS - 1), "yd": ("yd_gated", 0), "mix": ("mix", f // 2),
                            "v": ("silu", "dv"), "kd": ("silu", "dk")}.get(arg) or ("evac", f"up{arg[1:]}")
                    pe.wait_ge(*at(*wait))
                    if arg == "v":
                        for j in range(2):
                            for tb in range(TB):
                                mm = pe.transpose(B[b][:, (j * TB + tb) * P:(j * TB + tb + 1) * P],
                                                  qT_(zz)[:, 2 * f + j, tb * P:tb * P + P], core.ident)
                    elif arg == "kd":
                        for j in range(4):
                            mm = pe.transpose(B[b][:, j * P:j * P + P], qT_(kd_T)[:, 4 * f + j, 0:P], core.ident)
                    elif arg[0] == "f":
                        mm = turn_fill(nc, pe, core, B[b], f_src(int(arg[1:])), f)
                    else:
                        mm = turn_fill(nc, pe, core, B[b], source[arg], f)
                    mm.then_inc(*up("turned", (arg, f)))
                    t.turn_bank[arg, f] = b
                    if arg[0] == "f":
                        last_read[b] = ("cut", (arg, f))
                    elif arg in xt_of:
                        last_read[b] = ("cut", (arg, f))
                    elif arg in conv_out:
                        last_read[b] = ("convolved", (arg, f))
                    elif arg == "sq":
                        last_read[b] = ("sq_copied", f)
                    else:
                        last_read[b] = ("turn_copied", (arg, f))
                if kind == "decay_sum":
                    free(TURN)
                    pe.wait_ge(*at("g"))
                    for c in range(TB):
                        pe.matmul(B[TURN][:, c * DHEADS:(c + 1) * DHEADS], core.upper, t.g[:, c, :], start=True, stop=True)
                    pe.matmul(B[TURN][:, 16:16 + DHEADS], core.ones, t.g[:, 0, :], start=True, stop=True)\
                      .then_inc(*up("decay_summed"))
                    last_read[TURN] = ("cum", 1)
                if kind == "squares":
                    free(TURN)
                    pe.wait_ge(*at("squared", arg))
                    for tb in range(TB):
                        for h in range(DHEADS):
                            mm = pe.matmul(B[TURN][:, tb * DHEADS + h:tb * DHEADS + h + 1],
                                           qT_(zz)[:, h, tb * P:tb * P + P], core.ones[:, 0:1], start=True, stop=True)
                    mm.then_inc(*up("squares_summed", arg))
                    last_read[TURN] = ("ssq", arg)
                if kind == "s_scores":
                    h, b = arg, SCORE[arg % 2]
                    free(b)
                    pe.wait_ge(*at("sq_copied", h // 4))
                    if h == 0:
                        pe.wait_ge(*at("turn_copied", ("sk", 0)))
                    r = slice(HD * (h % 2), HD * (h % 2) + HD)
                    q, k = qT_(qs)[r, h // 2, :], ks[r, h // (HEADS // 2), :]
                    pe.matmul(B[b][:, 0:P], q[:, 0:P], k[:, 0:P], start=True, stop=True)
                    pe.matmul(B[b][:, P:3 * P], q[:, P:S], k, start=True, stop=True).then_inc(*up("s_scored", h))
                    last_read[b] = ("s_max", h)
                if kind == "s_turn":
                    h = arg
                    free(TURN)
                    pe.wait_ge(*at("s_prob", h))
                    for c in range(3):
                        mm = pe.transpose(B[TURN][:, c * P:c * P + P], prob[h % 2][:, c * P:c * P + P], core.ident)
                    mm.then_inc(*up("s_turned", h))
                    last_read[TURN] = ("s_copied", h)
                if kind == "s_out":
                    h = arg
                    free(OUT)
                    pe.wait_ge(*at("s_copied", h))
                    v = slice(HD * (h // (HEADS // 2)), HD * (h // (HEADS // 2)) + HD)
                    pe.matmul(B[OUT][:, 0:HD], turned[:, 0:P], vs[:, 0, v], start=True, stop=True)
                    pe.matmul(B[OUT][:, HD:2 * HD], turned[:, P:2 * P], vs[:, 0, v], start=True, stop=False)
                    pe.matmul(B[OUT][:, HD:2 * HD], turned[:, 2 * P:3 * P], vs[:, 1, v],
                              start=False, stop=True).then_inc(*up("s_summed", h))
                    last_read[OUT] = ("ys", h)
                if kind == "rows":
                    for j in range(2):
                        h, b = 2 * arg + j, SCORE[j]
                        free(b)
                        if j == 0:
                            pe.wait_ge(*at("brk"))
                        for c in range(TB):
                            pe.matmul(B[b][:, c * P:c * P + P], t.g[:, c, h:h + 1].to_broadcast([P, P]), core.upper,
                                      start=True, stop=True)
                        for c in range(TB):
                            mm = pe.matmul(B[b][:, (2 + c) * P:(3 + c) * P], t.brk[:, c, h:h + 1].to_broadcast([P, P]),
                                           core.ident, start=True, stop=True)
                        last_read[b] = ("decay_beta", arg)
                    mm.then_inc(*up("rows", arg))
                if kind == "gram":
                    for j in range(2):
                        h, b = 2 * arg + j, (TURN, OUT)[j]
                        free(b)
                        k, q = qT_(kd_T)[:, h, :], qT_(qd)[:, h, :]
                        for c in range(TB):
                            pe.matmul(B[b][:, c * P:c * P + P], k[:, c * P:c * P + P], k[:, c * P:c * P + P],
                                      start=True, stop=True)
                        for c in range(TB):
                            mm = pe.matmul(B[b][:, (2 + c) * P:(3 + c) * P], k[:, c * P:c * P + P],
                                           q[:, c * P:c * P + P], start=True, stop=True)
                        last_read[b] = ("score", arg)
                    mm.then_inc(*up("gram", arg))
                if kind == "inverse":
                    free(TURN)
                    pe.wait_ge(*at("inverse", (arg, 0)))
                    for i, (h, c) in enumerate(HC):
                        mm = pe.transpose(B[TURN][:, i * P:i * P + P], tr[h][:, c, 1, :], core.ident)
                    mm.then_inc(*up("inverse_turned", arg))
                    last_read[TURN] = ("inverse_copied", arg)
                if kind == "level_y":
                    g, l = arg, what[2]
                    free(TURN)
                    pe.wait_ge(*at("level_mask", (g, l)))
                    if l == 1:
                        pe.wait_ge(*at("inverse_copied", g))
                    else:
                        pe.wait_ge(*at("inverse", (g, l - 1)))
                    for i, (h, c) in enumerate(HC):
                        mm = pe.matmul(B[TURN][:, i * P:i * P + P], lm[l % 2][:, h, c, :], tr[h][:, c, 0, :],
                                       start=True, stop=True)
                    mm.then_inc(*up("level_y", (g, l)))
                    last_read[TURN] = ("y_copied", (g, l))
                if kind == "level_t":
                    g, l = arg, what[2]
                    for h in range(2):
                        free(SCORE[h])
                    pe.wait_ge(*at("y_copied", (g, l)))
                    for h, c in HC:
                        o = B[SCORE[h]][:, 2 * c * P:2 * (c + 1) * P]
                        if l < LEVELS - 1:
                            pe.matmul(o[:, 0:P], tr[h][:, c, 1, :], yy[:, h, c, :], start=True, stop=True)
                        mm = pe.matmul(o[:, P:2 * P], yy[:, h, c, :], tr[h][:, c, 1, :], start=True, stop=True)
                    mm.then_inc(*up("level_t", (g, l)))
                    for h in range(2):
                        last_read[SCORE[h]] = ("inverse", (g, l))
                if kind == "delta_u":
                    free(TURN)
                    pe.wait_ge(*at("inverse", (arg, LEVELS - 1)))
                    if arg == 0:
                        pe.wait_ge(*at("turn_copied", ("v", 3)))
                    for j in range(2):
                        h = 2 * arg + j
                        mm = pe.matmul(B[TURN][:, j * P:j * P + P], tr[j][:, 0, 1, :], vb[:, 0, h * DV:h * DV + DV],
                                       start=True, stop=True)
                    mm.then_inc(*up("u", arg))
                    last_read[TURN] = ("u_copied", arg)
                if kind == "delta_s":
                    free(OUT)
                    pe.wait_ge(*at("u_copied", arg))
                    if arg == 0:
                        pe.wait_ge(*at("turn_copied", ("kd", 1)))
                    for j in range(2):
                        pe.matmul(B[OUT][:, j * P:j * P + P], k_dec[:, 2 * arg + j, :], uu[:, j, :], start=True, stop=True)
                    for j in range(2):
                        mm = pe.matmul(B[OUT][:, (2 + j) * P:(3 + j) * P], score[:, j, 0, :], uu[:, j, :],
                                       start=True, stop=True)
                    mm.then_inc(*up("state", arg))
                    last_read[OUT] = ("out0", arg)
                if kind == "delta_r":
                    free(TURN)
                    pe.wait_ge(*at("state_copied", arg))
                    for i, a in enumerate((kd_T, kd_T, qd, qd)):
                        mm = pe.matmul(B[TURN][:, i * P:i * P + P], qT_(a)[:, 2 * arg + i % 2, P:S], state[:, i % 2, :],
                                       start=True, stop=True)
                    mm.then_inc(*up("from_state", arg))
                    last_read[TURN] = ("x1", arg)
                if kind == "delta_v":
                    free(OUT)
                    pe.wait_ge(*at("rest", arg))
                    for j in range(2):
                        mm = pe.matmul(B[OUT][:, j * P:j * P + P], tr[j][:, 1, 1, :], rr[:, j, :], start=True, stop=True)
                    mm.then_inc(*up("v_new", arg))
                    last_read[OUT] = ("v_copied", arg)
                if kind == "delta_o":
                    free(TURN)
                    pe.wait_ge(*at("v_copied", arg))
                    for j in range(2):
                        mm = pe.matmul(B[TURN][:, j * P:j * P + P], score[:, j, 1, :], uu[:, j, :], start=True, stop=True)
                    mm.then_inc(*up("o1", arg))
                    last_read[TURN] = ("o_sum", arg)

    @core.program("scalar")
    def _(act):
        with act.Fori(0, DEPTH) as layer:
            s.layer = layer
            for g in range(LEAD):
                core.split_hi(act, layer, base, plan, g)
            for what in plan.steps:
                kind, arg = what[0], what[1] if len(what) > 1 else None
                if kind in ("norm", "norm_mlp"):
                    n = int(kind == "norm_mlp")
                    if n:
                        act.wait_ge(*at("x_mid"))
                    else:
                        act.wait_ge(core.x_ready, layer + (DEPTH + 2))
                    row_squares(act, s, core.x, junk, t1.ssq, f"x{n}")
                if kind == "post":
                    act.wait_ge(*at("evac", ("oo1", "dn7_1")[arg]))
                    row_squares(act, s, ys, junk, t1.ssq, f"p{arg}")
                if kind == "post_rows":
                    act.wait_ge(*at("from_state", DHEADS // 2 - 1))
                    for i, name in enumerate(("post_mix_g_2", "post_mlp_g_2")):
                        act.dma_start(kd_T[:, i, :], ins[name][layer].partition_broadcast(P))\
                           .then_inc(*up("post_rows", i, 16))
                if kind == "piece" and arg + LEAD < P_:
                    core.split_hi(act, layer, base, plan, arg + LEAD)
                if kind == "decay":
                    act.wait_ge(*at("evac", "ba0"))
                    act.activation(t.beta, t.ba[:, :, 0:DHEADS], ACT.Sigmoid).then_inc(*up("beta"))
                    act.wait_ge(*at("abs"))
                    act.activation(t.abs, t.abs, ACT.Exp, scale=-1.0).then_inc(*up("soft", 0))
                    act.wait_ge(*at("soft", 0))
                    act.activation(t.abs, t.abs, ACT.Ln, bias=1.0).then_inc(*up("soft", 1))
                if kind == "decay_sum":
                    act.wait_ge(*at("cum", 1))
                    act.activation(t.ec, t.ec, ACT.Exp).then_inc(*up("ec"))
                if kind == "turn" and is_cut(arg):
                    f = what[2]
                    act.wait_ge(*at("turned", (arg, f)))
                    bank = B[t.turn_bank[arg, f]][:, :].rearrange("p (j t) -> p j t", j=2)
                    if arg[0] == "f":
                        k = 4 * (int(arg[1:]) % 2) + 2 * f
                        act.activation(core.xh[1][:, k:k + 2, :], bank, ACT.Copy).then_inc(*up("high", (arg, f, 1)))
                    elif arg in gain_of:
                        for j in range(2):
                            gain = t.cols[:, gain_of[arg][2 * f + j]:gain_of[arg][2 * f + j] + 1]
                            act.activation(core.xh[xt_of[arg]][:, 2 * f + j, :], bank[:, j, :], ACT.Copy,
                                           scale=gain).then_inc(*up("high", (arg, f, j)))
                    else:
                        act.activation(core.xh[xt_of[arg]][:, 2 * f:2 * f + 2, :], bank, ACT.Copy)\
                           .then_inc(*up("high", (arg, f, 1)))
                if kind == "turn" and arg == "sq":
                    f = what[2]
                    act.wait_ge(*at("turned", (arg, f)))
                    act.activation(qT_(qs)[:, 2 * f:2 * f + 2, :],
                                   B[t.turn_bank[arg, f]][:, :].rearrange("p (j t) -> p j t", j=2), ACT.Copy)\
                       .then_inc(*up("sq_copied", f))
                if kind == "silu":
                    a = qT_(conv_out[arg][0])
                    act.wait_ge(*at("convolved", (arg, 3)))
                    act.activation(a, a, ACT.Silu).then_inc(*up("silu", arg))
                if kind == "squares":
                    act.wait_ge(*at("silu", arg))
                    if arg == "dk":
                        act.wait_ge(*at("squares_summed", "dq"))
                    act.activation(qT_(zz), qT_(conv_out[arg][0]), ACT.Square).then_inc(*up("squared", arg))
                if kind == "evac" and arg[:2] in ("zz", "ga", "gb"):
                    c = int(arg[2])
                    dst = {"zz": zz, "ga": b1, "gb": b0}[arg[:2]]
                    if arg == "zz0":
                        act.wait_ge(*at("turned", ("v", 3)))
                    if arg == "gb0":
                        act.wait_ge(*at("turned", ("dk", 3)))
                    if arg == "ga0":
                        act.wait_ge(*at("turned", ("dv", 3)))
                    for tb in range(TB):
                        act.wait_ge(*ended(arg, layer))
                        ins_ = act.activation(dst[:, tb, c * CH:c * CH + CH],
                                              B[plan.by_name[arg].banks[tb]][:, :], ACT.Sigmoid)
                    ins_.then_inc(*up("sigmoid", arg))
                if kind == "evac" and arg[:2] == "up":
                    j = int(arg[2:])
                    if j == 0:
                        act.wait_ge(*at("evac", "ud1"))
                    if j >= 2:
                        act.wait_ge(*at("turned", (f"f{j - 2}", 1)))
                    for tb in range(TB):
                        act.wait_ge(*ended(arg, layer))
                        ins_ = act.activation(f_src(j)[:, tb, 0:CH], B[plan.by_name[arg].banks[tb]][:, :], ACT.Relu)
                    ins_.then_inc(*up("relu", j))
                if kind == "s_scores":
                    h = arg
                    act.wait_ge(*at("s_max", h))
                    if h >= 2:
                        act.wait_ge(*at("s_turned", h - 2))
                    for tb, cols, _ in parts:
                        act.activation(prob[h % 2][:, cols], masked[h % 2][:, cols], ACT.Exp, scale=SCALE,
                                       bias=t1.negmax[:, h % 2, tb:tb + 1],
                                       accum_out=t1.total[:, h % 4, tb:tb + 1])
                    act.activation(t.sinkexp[:, h % 2, :], t.sinkexp[:, h % 2, :], ACT.Exp).then_inc(*up("s_prob", h))
                if kind == "s_turn":
                    h = arg
                    act.wait_ge(*at("s_turned", h))
                    if h >= 1:
                        act.wait_ge(*at("s_summed", h - 1))
                    act.activation(turned, B[TURN][:, 0:3 * P], ACT.Copy).then_inc(*up("s_copied", h))
                if kind == "rows":
                    act.wait_ge(*at("decay", arg))
                    act.activation(decay, decay, ACT.Exp).then_inc(*up("decay_exp", arg))
                if kind == "inverse":
                    act.wait_ge(*at("inverse_turned", arg))
                    act.activation(tr_all[:, :, 0, :], B[TURN][:, :].rearrange("p (i t) -> p i t", t=P), ACT.Copy)\
                       .then_inc(*up("inverse_copied", arg))
                if kind == "level_y":
                    g, l = arg, what[2]
                    act.wait_ge(*at("level_y", (g, l)))
                    act.activation(yy.rearrange("p h c t -> p (h c t)"), B[TURN][:, :], ACT.Copy).then_inc(*up("y_copied", (g, l)))
                if kind == "delta_u":
                    act.wait_ge(*at("u", arg))
                    act.activation(uu.rearrange("p h t -> p (h t)"), B[TURN][:, 0:2 * P], ACT.Copy).then_inc(*up("u_copied", arg))
                if kind == "delta_v":
                    act.wait_ge(*at("v_new", arg))
                    act.activation(uu.rearrange("p h t -> p (h t)"), B[OUT][:, 0:2 * P], ACT.Copy).then_inc(*up("v_copied", arg))
                if kind == "delta_o":
                    act.wait_ge(*at("yd", arg))
                    for j in range(2):
                        for tb in range(TB):
                            h = 2 * arg + j
                            if arg or j or tb:
                                act.wait_ge(*at("yd_square", last))
                            last = (arg, j, tb)
                            act.activation(t.junk, vb[:, tb, h * DV:h * DV + DV], ACT.Square,
                                           accum_out=t1.head_ssq[:, tb, h:h + 1]).then_inc(*up("yd_square", last))

    @core.program("vector")
    def _(dve):
        with dve.Fori(0, DEPTH) as layer:
            s.layer = layer
            dve.tensor_copy(t.cols, t.cols_all[:, layer, :]).then_inc(*up("small", 0))
            dve.tensor_scalar(t.sink, t.sink_all[:, layer, :], 1.0 / SCALE, None, ALU.mult).then_inc(*up("small", 1))
            dve.tensor_copy(t.nega, t.nega_all[:, layer, :]).then_inc(*up("small", 2))
            dve.tensor_copy(t.dtb, t.dtb_all[:, layer, :]).then_inc(*up("small", 3))
            for g in range(LEAD):
                if core.lo_engine(g) == "dve":
                    core.split_lo(dve, layer, base, plan, g)
            for what in plan.steps:
                kind, arg = what[0], what[1] if len(what) > 1 else None
                if kind == "piece" and arg + LEAD < P_ and core.lo_engine(arg + LEAD) == "dve":
                    core.split_lo(dve, layer, base, plan, arg + LEAD)
                if kind in ("norm", "norm_mlp"):
                    n = int(kind == "norm_mlp")
                    dve.wait_ge(*at("rstd", f"x{n}"))
                    for tb in range(TB):
                        ins_ = dve.tensor_scalar(b1[:, tb, :], core.x[:, tb, :], t1.rstd[:, tb:tb + 1], None, ALU.mult)
                    ins_.then_inc(*up("h_ready", n))
                if kind == "turn":
                    f = what[2]
                    bank = B[t.turn_bank[arg, f]][:, :].rearrange("p (j t) -> p j t", j=2)
                    if is_cut(arg):
                        if arg[0] == "f":
                            k = 4 * (int(arg[1:]) % 2) + 2 * f
                            dve.wait_ge(*at("high", (arg, f, 1)))
                            dve.tensor_tensor(core.xl[1][:, k:k + 2, :], bank, core.xh[1][:, k:k + 2, :].bitcast(F32),
                                              ALU.subtract).then_inc(*up("cut", (arg, f)))
                            continue
                        xh, xl = core.xh[xt_of[arg]], core.xl[xt_of[arg]]
                        dve.wait_ge(*at("high", (arg, f, 1)))
                        if arg in gain_of:
                            for j in range(2):
                                n = 2 * f + j
                                ins_ = dve.scalar_tensor_tensor(xl[:, n, :], bank[:, j, :],
                                                                t.cols[:, gain_of[arg][n]:gain_of[arg][n] + 1],
                                                                xh[:, n, :].bitcast(F32), ALU.mult, ALU.subtract)
                        else:
                            ins_ = dve.tensor_tensor(xl[:, 2 * f:2 * f + 2, :], bank,
                                                     xh[:, 2 * f:2 * f + 2, :].bitcast(F32), ALU.subtract)
                        ins_.then_inc(*up("cut", (arg, f)))
                    elif arg in conv_out:
                        out, first = conv_out[arg]
                        if arg == "dv" and f == 0:
                            dve.wait_ge(*at("squares_summed", "dk"))
                        dve.wait_ge(*at("turned", (arg, f)))
                        for j in (3, 2, 1, 0):
                            if j < 3:
                                dve.wait_ge(*at("taps", (arg, f, j + 1)))
                            for n in range(2):
                                w = t.cols[:, tap(j, first + 2 * f + n):tap(j, first + 2 * f + n) + 1]
                                y = qT_(out)[:, 2 * f + n, 3 - j:S]
                                x = bank[:, n, 0:S - 3 + j]
                                if j == 3:
                                    ins_ = dve.tensor_scalar(y, x, w, None, ALU.mult)
                                else:
                                    ins_ = dve.scalar_tensor_tensor(y, x, w, y, ALU.mult, ALU.add)
                            if j:
                                ins_.then_inc(*up("taps", (arg, f, j)))
                        ins_.then_inc(*up("convolved", (arg, f)))
                    elif arg == "v":
                        dve.wait_ge(*at("turned", (arg, f)))
                        dve.wait_ge(*at("beta"))
                        for j in range(2):
                            h = 2 * f + j
                            ins_ = dve.tensor_tensor(vb[:, :, h * DV:h * DV + DV],
                                                     B[t.turn_bank[arg, f]][:, j * S:j * S + S].rearrange("p (t d) -> p t d", d=DV),
                                                     bcast(t.beta[:, :, h], 2, DV), ALU.mult)
                        ins_.then_inc(*up("turn_copied", (arg, f)))
                    elif arg == "kd":
                        dve.wait_ge(*at("turned", (arg, f)))
                        dve.wait_ge(*at("kds"))
                        dve.tensor_tensor(k_dec[:, 4 * f:4 * f + 4, :],
                                          B[t.turn_bank[arg, f]][:, :].rearrange("p (h d) -> p h d", d=P),
                                          bcast(t.kds[:, 4 * f:4 * f + 4], 2, P), ALU.mult)\
                           .then_inc(*up("turn_copied", (arg, f)))
                    elif arg == "sk":
                        dve.wait_ge(*at("turned", (arg, f)))
                        dve.tensor_copy(ks, bank).then_inc(*up("turn_copied", (arg, f)))
                if kind == "decay":
                    y, b = t.ba[:, :, DHEADS:2 * DHEADS], t.ba[:, :, DHEADS:2 * DHEADS]
                    dve.wait_ge(*at("evac", "ba0"))
                    dve.wait_ge(*at("small", 3))
                    dve.tensor_tensor(y, b, bcast(t.dtb, 1, TB), ALU.add).then_inc(*up("y"))
                    dve.wait_ge(*at("y"))
                    dve.scalar_tensor_tensor(t.abs, y, -1.0, y, ALU.mult, ALU.max).then_inc(*up("abs"))
                    dve.wait_ge(*at("soft", 1))
                    dve.scalar_tensor_tensor(t.soft, y, 0.0, t.abs, ALU.max, ALU.add).then_inc(*up("softplus"))
                    dve.wait_ge(*at("softplus"))
                    dve.tensor_tensor(t.g, t.soft, bcast(t.nega, 1, TB), ALU.mult).then_inc(*up("g"))
                if kind == "decay_sum":
                    dve.wait_ge(*at("decay_summed"))
                    dve.tensor_copy(t.cum.rearrange("p c h -> p (c h)"), B[TURN][:, 0:2 * DHEADS]).then_inc(*up("cum", 0))
                    dve.wait_ge(*at("cum", 0))
                    dve.tensor_copy(t.ec[:, 0, :], t.cum[:, 1, :])
                    dve.tensor_tensor(t.ec[:, 1, :], B[TURN][:, 16:16 + DHEADS], t.cum[:, 0, :], ALU.subtract)\
                       .then_inc(*up("cum", 1))
                if kind == "squares":
                    dve.wait_ge(*at("squares_summed", arg))
                    if arg == "dk":
                        dve.wait_ge(*at("rq"))
                    dve.tensor_copy(t.ssq2.rearrange("p c h -> p (c h)"), B[TURN][:, 0:2 * DHEADS]).then_inc(*up("ssq", arg))
                if kind == "scales":
                    dve.wait_ge(*at("rk"))
                    dve.wait_ge(*at("beta"))
                    dve.wait_ge(*at("ec"))
                    dve.tensor_tensor(t.brk, t.beta, t.rk, ALU.mult).then_inc(*up("brk"))
                    dve.tensor_tensor(t.kds, t.ec[:, 1, :], t.rk[:, 0, :], ALU.mult).then_inc(*up("kds"))
                    dve.wait_ge(*at("brk"))
                    dve.scalar_tensor_tensor(t.rs, t.ec[:, 0, :], -1.0, t.brk[:, 1, :], ALU.mult, ALU.mult)\
                       .then_inc(*up("rs"))
                if kind == "evac":
                    job, name = plan.by_name[arg], arg[:2]
                    c = int(arg[-1])
                    cols = slice(c * CH, c * CH + CH)
                    done = ended(arg, layer)
                    if arg == "ba0":
                        for tb in range(TB):
                            dve.wait_ge(*done)
                            dve.tensor_copy(t.ba[:, tb, :], B[job.banks[tb]][:, 0:16])
                            ins_ = dve.tensor_copy(b0[:, tb, 0:256], B[job.banks[tb]][:, 16:272])
                        ins_.then_inc(*up("evac", arg))
                    if arg == "sq0":
                        for tb in range(TB):
                            dve.wait_ge(*done)
                            ins_ = dve.tensor_copy(b0[:, tb, 256:768], B[job.banks[tb]][:, :])
                        ins_.then_inc(*up("evac", arg))
                    if arg == "sq1":
                        for tb in range(TB):
                            bank = B[job.banks[tb]]
                            dve.wait_ge(*done)
                            dve.tensor_copy(b0[:, tb, 768:1024], bank[:, 0:256])
                            for r in range(2):
                                dve.tensor_copy(k_dup[:, tb, :].rearrange("p (k r d) -> p k r d", k=2, r=2)[:, :, r, :],
                                                bank[:, 256:384].rearrange("p (k d) -> p k d", k=2))
                            ins_ = dve.tensor_copy(vs[:, tb, :], bank[:, 384:512])
                        ins_.then_inc(*up("evac", arg))
                    if name in ("dq", "dk", "dv"):
                        dst, before = {"dq": (b1, ("h", 3)), "dk": (b0, ("sq", 3)), "dv": (b1, ("dq", 3))}[name]
                        if c == 0:
                            dve.wait_ge(*at("turned", before))
                        for tb in range(TB):
                            dve.wait_ge(*done)
                            ins_ = dve.tensor_copy(dst[:, tb, cols], B[job.banks[tb]][:, :])
                        ins_.then_inc(*up("evac", arg))
                    if name == "zz":
                        for tb in range(TB):
                            dve.wait_ge(*at("sigmoid", arg))
                            ins_ = dve.tensor_tensor(zz[:, tb, cols], B[job.banks[tb]][:, :], zz[:, tb, cols], ALU.mult)
                        ins_.then_inc(*up("evac", arg))
                    if name == "us":
                        for tb in range(TB):
                            dve.wait_ge(*done)
                            dve.wait_ge(*at("sigmoid", "gb1"))
                            ins_ = dve.tensor_tensor(qs[:, tb, cols], B[job.banks[tb]][:, :], b0[:, tb, cols], ALU.mult)
                        ins_.then_inc(*up("evac", arg))
                    if name == "ud":
                        for tb in range(TB):
                            dve.wait_ge(*done)
                            dve.wait_ge(*at("sigmoid", "ga1"))
                            dve.tensor_tensor(b1[:, tb, cols], B[job.banks[tb]][:, :], b1[:, tb, cols],
                                              ALU.mult).then_inc(*up("evac", (arg, tb)))
                        dve.wait_ge(*at("evac", (arg, 1)))
                        dve.wait_ge(*at("evac", "us1"))
                        dve.tensor_tensor(qs[:, :, cols], qs[:, :, cols], b1[:, :, cols], ALU.add).then_inc(*up("mix", c))
                        s.keys["evac", arg] = s.keys["evac", (arg, 1)]
                    if name in ("oo", "dn"):
                        for tb in range(TB):
                            dve.wait_ge(*done)
                            ins_ = dve.tensor_copy(ys[:, tb, cols], B[job.banks[tb]][:, :])
                        ins_.then_inc(*up("evac", arg))
                    if name == "up":
                        j = int(arg[2:])
                        for tb in range(TB):
                            dve.wait_ge(*at("relu", j))
                            f = f_src(j)[:, tb, 0:CH]
                            ins_ = dve.tensor_tensor(f, B[job.banks[tb]][:, :], f, ALU.mult)
                        ins_.then_inc(*up("evac", arg))
                if kind == "post":
                    dve.wait_ge(*at("rstd", f"p{arg}"))
                    dve.wait_ge(*at("post_rows", 1))
                    for tb in range(TB):
                        dve.scalar_tensor_tensor(ys[:, tb, :], ys[:, tb, :], t1.rstd[:, tb:tb + 1], kd_T[:, arg, :],
                                                 ALU.mult, ALU.mult).then_inc(*up("post", (arg, tb)))
                    for tb in range(TB):
                        dve.wait_ge(*at("post", (arg, tb)))
                        ins_ = dve.tensor_tensor(core.x[:, tb, :], core.x[:, tb, :], ys[:, tb, :], ALU.add)
                    if arg == 0:
                        ins_.then_inc(*up("x_mid"))
                    else:
                        ins_.then_inc(core.x_ready, 1)
                if kind == "s_scores":
                    h = arg
                    masked_max(dve, core, s, B[SCORE[h % 2]], masked[h % 2], t1.top[:, h % 2, :],
                               t1.negmax[:, h % 2, :], parts, 2, ("s_scored", h), ("s_prob", h - 2) if h >= 2 else None,
                               ("s_top", h), ("s_max", h), sink=(t.sink[:, h:h + 1], t.sinkexp[:, h % 2, :]))
                if kind == "s_turn":
                    h = arg
                    dve.wait_ge(*at("s_prob", h))
                    tot = t1.total[:, h % 4, :]
                    dve.tensor_tensor(tot, tot, t.sinkexp[:, h % 2, :], ALU.add).then_inc(*up("s_total", h))
                    dve.wait_ge(*at("s_total", h))
                    dve.reciprocal(t1.inverse[:, h % 4, :], tot).then_inc(*up("s_inverse", h))
                if kind == "s_out":
                    h = arg
                    dve.wait_ge(*at("s_summed", h))
                    dve.wait_ge(*at("s_inverse", h))
                    dve.tensor_tensor(ys[:, :, h * HD:h * HD + HD],
                                      B[OUT][:, 0:2 * HD].rearrange("p (t d) -> p t d", t=TB),
                                      bcast(t1.inverse[:, h % 4, :], 2, HD), ALU.mult).then_inc(*up("ys", h))
                if kind == "rows":
                    dve.wait_ge(*at("rows", arg))
                    for j, c in HC:
                        h = 2 * arg + j
                        ins_ = dve.tensor_scalar(decay[:, j, c, :], B[SCORE[j]][:, c * P:c * P + P],
                                                 t.cum[:, c, h:h + 1], 0.0, ALU.subtract, ALU.min)
                    ins_.then_inc(*up("decay", arg))
                    dve.wait_ge(*at("decay_masked", arg))
                    for j in range(2):
                        ins_ = dve.tensor_tensor(decay[:, j, :, :].rearrange("p c t -> p (c t)"), B[SCORE[j]][:, S:2 * S],
                                                 score[:, j, :, :].rearrange("p c t -> p (c t)"), ALU.mult)
                    ins_.then_inc(*up("decay_beta", arg))
                if kind == "gram":
                    dve.wait_ge(*at("gram", arg))
                    dve.wait_ge(*at("decay_beta", arg))
                    for j, c in HC:
                        h, b = 2 * arg + j, B[(TURN, OUT)[j]]
                        ins_ = dve.scalar_tensor_tensor(decay[:, j, c, :], b[:, c * P:c * P + P], t.rk[:, c, h:h + 1],
                                                        decay[:, j, c, :], ALU.mult, ALU.mult)
                    ins_.then_inc(*up("lower", arg))
                    for j, c in HC:
                        h, b = 2 * arg + j, B[(TURN, OUT)[j]]
                        ins_ = dve.scalar_tensor_tensor(score[:, j, c, :], b[:, (2 + c) * P:(3 + c) * P], t.rk[:, c, h:h + 1],
                                                        score[:, j, c, :], ALU.mult, ALU.mult)
                    ins_.then_inc(*up("score", arg))
                if kind == "inverse":
                    dve.wait_ge(*at("level_mask", (arg, 0)))
                    dve.tensor_tensor(tr_all[:, :, 1, :], bcast(core.ident, 1, 4),
                                      lm[0].rearrange("p h c t -> p (h c) t"), ALU.subtract).then_inc(*up("inverse", (arg, 0)))
                if kind == "level_t":
                    g, l = arg, what[2]
                    dve.wait_ge(*at("level_t", (g, l)))
                    for h in range(2):
                        w = slice(0, 2) if l < LEVELS - 1 else slice(1, 2)
                        bank = B[SCORE[h]][:, :].rearrange("p (c w t) -> p c w t", c=TB, w=2)[:, :, w, :]
                        ins_ = dve.tensor_tensor(tr[h][:, :, w, :], tr[h][:, :, w, :], bank, ALU.subtract)
                    ins_.then_inc(*up("inverse", (g, l)))
                if kind == "delta_s":
                    dve.wait_ge(*at("state", arg))
                    dve.tensor_copy(state.rearrange("p h t -> p (h t)"), B[OUT][:, 0:2 * P]).then_inc(*up("state_copied", arg))
                    v = vb[:, 0, 2 * arg * DV:2 * (arg + 1) * DV].rearrange("p (h d) -> p h d", d=DV)
                    dve.tensor_tensor(v, B[OUT][:, 2 * P:4 * P].rearrange("p (h d) -> p h d", d=DV),
                                      bcast(t.rq[:, 0, 2 * arg:2 * arg + 2], 2, DV), ALU.mult).then_inc(*up("out0", arg))
                if kind == "delta_r":
                    dve.wait_ge(*at("from_state", arg))
                    dve.wait_ge(*at("rs"))
                    for j in range(2):
                        h = 2 * arg + j
                        ins_ = dve.scalar_tensor_tensor(rr[:, j, :], B[TURN][:, j * P:j * P + P], t.rs[:, h:h + 1],
                                                        vb[:, 1, h * DV:h * DV + DV], ALU.mult, ALU.add)
                    ins_.then_inc(*up("rest", arg))
                    dve.tensor_tensor(xx, B[TURN][:, 2 * P:4 * P].rearrange("p (h d) -> p h d", d=DV),
                                      bcast(t.ec[:, 0, 2 * arg:2 * arg + 2], 2, DV), ALU.mult).then_inc(*up("x1", arg))
                if kind == "delta_o":
                    dve.wait_ge(*at("o1", arg))
                    dve.wait_ge(*at("x1", arg))
                    dve.tensor_tensor(xx, xx, B[TURN][:, 0:2 * P].rearrange("p (h d) -> p h d", d=DV), ALU.add)\
                       .then_inc(*up("o_sum", arg))
                    dve.wait_ge(*at("o_sum", arg))
                    v = vb[:, 1, 2 * arg * DV:2 * (arg + 1) * DV].rearrange("p (h d) -> p h d", d=DV)
                    dve.tensor_tensor(v, xx, bcast(t.rq[:, 1, 2 * arg:2 * arg + 2], 2, DV), ALU.mult).then_inc(*up("yd", arg))
                if kind == "head_norm":
                    v = vb[:, :, :].rearrange("p t (h d) -> p (t h) d", d=DV)
                    dve.wait_ge(*at("head_rstd"))
                    dve.tensor_tensor(v, v, bcast(t1.head_rstd.rearrange("p t h -> p (t h)"), 2, DV), ALU.mult)\
                       .then_inc(*up("head_scaled"))
                    dve.wait_ge(*at("head_scaled"))
                    dve.wait_ge(*at("evac", "zz1"))
                    dve.tensor_tensor(vb[:, :, :], vb[:, :, :], zz[:, :, :], ALU.mult).then_inc(*up("yd_gated"))

    @core.program("gpsimd")
    def _(pool):
        with pool.Fori(0, DEPTH) as layer:
            s.layer = layer
            for what in plan.steps:
                kind, arg = what[0], what[1] if len(what) > 1 else None
                if kind == "piece" and arg + LEAD < P_ and core.lo_engine(arg + LEAD) == "pool":
                    core.split_lo(pool, layer, base, plan, arg + LEAD)
                if kind in ("norm", "norm_mlp", "post"):
                    key = {"norm": "x0", "norm_mlp": "x1", "post": f"p{arg}"}[kind]
                    pool.wait_ge(*at("row_square", (key, 1)))
                    rsqrt(pool, s, core, t1.ssq[:, 0:TB], t1.rstd[:, 0:TB], 1.0 / D, 1e-6, "rstd_mean", "rstd", key)
                if kind == "rope":
                    if arg == "sk":
                        rotate(pool, s, k_dup, core.rope2, t1.rot[0], t1.rot[1], ("evac", "sq1"), "sk", 4)
                    else:
                        rotate(pool, s, b0, core.rope2, t1.rot[0], t1.rot[1], ("evac", "sq1"), "sq", HEADS)
                if kind == "squares":
                    pool.wait_ge(*at("ssq", arg))
                    if arg == "dq":
                        rsqrt(pool, s, core, t.ssq2, t.rq, DV, 1e-6 * DV, "rq_mean", "rq", 0)
                    else:
                        rsqrt(pool, s, core, t.ssq2, t.rk, 1.0, 1e-6, "rk_mean", "rk", 0)
                if kind == "rows":
                    pool.wait_ge(*at("decay_exp", arg))
                    pool.tensor_tensor(score.rearrange("p h c t -> p (h c) t"), decay.rearrange("p h c t -> p (h c) t"),
                                       bcast(core.upper, 1, 4), ALU.mult).then_inc(*up("decay_masked", arg))
                if kind == "inverse" or kind == "level_t" and what[2] < LEVELS - 1:
                    for l in ((0, 1) if kind == "inverse" else (what[2] + 1,)):
                        if l == 0:
                            pool.wait_ge(*at("lower", arg))
                        if l >= 2:
                            pool.wait_ge(*(at("level_y", (arg, l - 2)) if l > 2 else at("inverse", (arg, 0))))
                        pool.tensor_tensor(lm[l % 2].rearrange("p h c t -> p (h c) t"), decay.rearrange("p h c t -> p (h c) t"),
                                           bcast(level_mask(l), 1, 4), ALU.mult).then_inc(*up("level_mask", (arg, l)))
                if kind == "head_norm":
                    pool.wait_ge(*at("yd_square", (DHEADS // 2 - 1, 1, TB - 1)))
                    rsqrt(pool, s, core, t1.head_ssq, t1.head_rstd, 1.0 / DV, 1e-6, "head_mean", "head_rstd", 0)

    @core.program("sync")
    def _(sp):
        with sp.Fori(0, DEPTH) as layer:
            for u, (job, n) in enumerate(plan.units):
                job.weight = ins[job.weight] if isinstance(job.weight, str) else job.weight
                core.load_unit(sp, layer, base, P_, u, job, n)


def row_squares(act, s, src, junk, ssq, key):
    for tb in range(TB):
        if tb:
            act.wait_ge(*s.at("row_square", (key, 0)))
        act.activation(junk, src[:, tb, :], ACT.Square,
                       accum_out=ssq[:, tb:tb + 1]).then_inc(*s.up("row_square", (key, tb)))


BLOCKS = 2


def build(nc, ins, out, tally=None):
    with ExitStack() as ctx:
        core = Core(nc, ctx)
        names = ["setup", "one", "final", "setup2", "two"] + ["end"]
        sig = {n: Signals(nc, ctx, n, tally and tally[n]) for n in names}
        sig["two"].after = sig["one"]
        setup(nc, core, sig["setup"], ins)
        setup_two(nc, core, sig["setup2"], ins)
        block_one(nc, core, sig["one"], plan_one(), ins)
        sig["one"].rot_before = sig["setup"].rot_before
        final_norm(nc, core, sig["final"], ins)
        if BLOCKS > 1:
            block_two(nc, core, sig["two"], plan_two(), ins, len(plan_one().pieces) * DEPTH)
        store(nc, core, sig["end"], out, DEPTH + 2 if BLOCKS == 1 else 2 * DEPTH + 2)
        block = ctx.enter_context(nc.Block())

        @block.tensor
        def _(pe):
            for part in core.programs["tensor"]:
                part(pe)

        @block.scalar
        def _(act):
            for part in core.programs["scalar"]:
                part(act)

        @block.vector
        def _(dve):
            for part in core.programs["vector"]:
                part(dve)

        @block.gpsimd
        def _(pool):
            for part in core.programs["gpsimd"]:
                part(pool)

        @block.sync
        def _(sp):
            for part in core.programs["sync"]:
                part(sp)

        return {n: x.totals() for n, x in sig.items()}


_INS = ["x", "norm_w", "w_in", "lambda_q1", "lambda_k1", "lambda_q2", "lambda_k2", "subln_w", "w_proj_a",
        "w_proj_b", "w_out", "final_norm_w"]
_INS2 = ["positions_2", "pre_mix_g_2", "w_in_2", "dn_conv_w_2", "dn_a_log_2", "dn_dt_bias_2", "dn_norm_g_2",
         "sw_sinks_2", "w_up_dn_2", "w_up_sw_2", "w_o_2", "post_mix_g_2", "pre_mlp_g_2", "w_ff1_2", "w_ff2_2",
         "post_mlp_g_2"]


def kernel(**inputs):
    import concourse.bacc as bacc
    from concourse.bass_utils import run_bass_kernel_spmd

    names = _INS + (_INS2 if BLOCKS > 1 else [])
    arrays = {n: np.ascontiguousarray(inputs[n]) for n in names}
    arrays.update(shape_constants())

    def program(tally):
        nc = bacc.Bacc("TRN2", target_bir_lowering=False, num_devices=1)
        ins = {n: nc.dram_tensor(f"in_{n}", a.shape, mybir.dt.from_np(a.dtype), kind="ExternalInput").ap()
               for n, a in arrays.items()}
        out = nc.dram_tensor("out", (1, S, D), F32, kind="ExternalOutput").ap()
        return nc, build(nc, ins, out, tally)

    _, tally = program(None)
    nc, again = program(tally)
    assert again == tally
    r = run_bass_kernel_spmd(nc, [{f"in_{n}": a for n, a in arrays.items()}], core_ids=[0])
    return r.results[0]["out"]
```

```python
import math
from contextlib import ExitStack

import numpy as np

import concourse.bass as bass
from concourse import mybir

F32 = mybir.dt.float32
F32R = mybir.dt.float32r
I32 = mybir.dt.int32
ALU = mybir.AluOpType
ACT = mybir.ActivationFunctionType

P = 128
D = 1024
S = 256
TB = S // P
KB = D // P
DEPTH = 2
CH = 512
HEADS = 16
HD = 64
DHEADS = 8
DV = 128
ROT = HD // 4
NEG = -1e30
SCALE = HD ** -0.5
RAW = 4
RING = 4
LEAD = 3
LO_LEAD = 2
LEVELS = 7


def lambda_init(layer):
    return 0.8 - 0.6 * math.exp(-0.3 * layer)


def shape_constants():
    q = np.arange(P)[:, None]
    k = np.arange(-P, P)[None, :]
    dist = q - k
    causal = dist >= 0
    count = ((causal & (dist <= 128)).astype(int) + (causal & (dist % 4 == 0))
             + (causal & (dist % 16 == 0)))
    dilated = np.where(count > 0, np.log(np.maximum(count, 1)) / SCALE, NEG)
    full = np.where(causal, 0.0, NEG)
    window = np.where(causal & (dist < 128), 0.0, NEG)
    masks = np.stack([dilated, full, window], 1).astype(np.float32)
    t = np.arange(P)
    ident = (t[:, None] == t[None, :])
    upper = (t[:, None] <= t[None, :])
    ones = np.ones((P, P))
    levels = [(t[:, None] // (2 * b) == t[None, :] // (2 * b)) & (t[:, None] // b + 1 == t[None, :] // b)
              for b in (2 ** n for n in range(LEVELS))]
    square = np.stack([ident, upper, ones] + levels, 1).astype(np.float32)
    inv = (1.0 / (np.float32(500000.0) ** (np.arange(0, ROT, 2, dtype=np.float32) / np.float32(ROT))))
    inv = inv.astype(np.float32)
    ang = (np.arange(S, dtype=np.float32)[:, None] * inv[None, :]).astype(np.float32)
    cos, sin = np.cos(ang).astype(np.float32), np.sin(ang).astype(np.float32)
    rope = np.stack([cos, cos, -sin, sin], 1)
    rope = rope.reshape(TB, P, 4 * ROT // 2)
    inv2 = (np.float32(500000.0) ** (-np.arange(ROT // 2, dtype=np.float32) * np.float32(2.0 / ROT)))
    inv2 = np.broadcast_to(inv2.astype(np.float32), (P, ROT // 2))
    return {"masks": masks, "square": square, "rope": np.ascontiguousarray(rope),
            "inv_freq": np.ascontiguousarray(inv2)}


class Signals:

    def __init__(self, nc, ctx, prefix, tally=None, after=None):
        self.after = after
        self.nc, self.ctx, self.prefix, self.tally = nc, ctx, prefix, tally
        self.sems, self.count, self.keys, self.layer = {}, {}, {}, 0
        self.final = dict(tally) if tally else {}

    def shared(self, name):
        return self.after and (self.tally is None or name in self.after.tally)

    def sem(self, name):
        if self.shared(name):
            return self.after.sem(name)
        if name not in self.sems:
            self.sems[name] = self.ctx.enter_context(self.nc.semaphore(f"{self.prefix}_{name}"))
        return self.sems[name]

    def up(self, name, key=0, by=1):
        self.count[name] = self.count.get(name, 0) + by
        self.keys[name, key] = self.count[name]
        return self.sem(name), by

    def at(self, name, key=0):
        if self.tally is None:
            return self.sem(name), self.layer * 2 + 1
        per_layer, n = self.tally[name], self.tally[name, key]
        if self.shared(name):
            n += DEPTH * self.after.tally[name]
        return self.sem(name), self.layer * per_layer + n

    def totals(self):
        return {**self.count, **self.keys}


class Job:

    def __init__(self, name, weight, row, col, rows, cols, unit_rows, xt, xt_block, banks,
                 start=True, stop=True):
        self.name, self.weight, self.row, self.col = name, weight, row, col
        self.rows, self.cols, self.unit = rows, cols, unit_rows
        self.xt, self.xt_block, self.banks = xt, xt_block, banks
        self.start, self.stop = start, stop
        self.pieces = 2 * (rows // unit_rows)


def section(name, weight, col, xt):
    return [Job(f"{name}{c}", weight, 0, col + c * CH, KB, CH, 4, xt, 0, (2 * c, 2 * c + 1))
            for c in range(2)]


class Plan:

    def __init__(self):
        self.steps, self.jobs, self.pieces, self.units = [], [], [], []

    def step(self, *what):
        self.steps.append(what)

    def run(self, jobs, between=(), halves=False):
        between = list(between)
        for job in jobs:
            self.jobs.append(job)
            for n in range(job.pieces):
                if n % 2 == 0:
                    self.units.append((job, n // 2))
                self.pieces.append((job, n))
                g = len(self.pieces) - 1
                if halves:
                    self.steps.append(("piece", g, "half"))
                    if between:
                        self.steps.extend(between.pop(0))
                    self.steps.append(("more", g))
                else:
                    self.steps.append(("piece", g))
                if n == job.pieces - 1 and job.stop:
                    self.steps.append(("evac", job.name))
                if between:
                    self.steps.extend(between.pop(0))
        for rest in between:
            self.steps.extend(rest)

    def close(self):
        self.by_name = {j.name: j for j in self.jobs}
        self.end = {j.name: max(g for g, (k, _) in enumerate(self.pieces) if k is j) for j in self.jobs}
        return self


def attention(kind, heads, first=0):
    out = []
    for t in range(heads + 2):
        out.append(([(f"{kind}_scores", t)] if t < heads else [])
                   + ([(f"{kind}_turn", t - 1)] if 1 <= t <= heads else [])
                   + ([(f"{kind}_out", t - 2)] if t >= 2 else []))
    return out


def spread(groups, every):
    out = []
    for g in groups:
        out += [g] + [[]] * (every - 1)
    return out


def start_turns(plan, name, jobs, between=()):
    t = turns(name)
    plan.steps.extend(t[0] + t[1])
    between = list(between) + [[]] * 3
    plan.run(jobs, [t[2] + between[0], t[3] + between[1]] + between[2:])


def turns(name, a=0, b=4):
    return [[("turn", name, f)] for f in range(a, b)]


def plan_one():
    p = Plan()
    sec = lambda n, i: section(n, "w_in", i * D, 0)
    p.step("norm")
    start_turns(p, "h", sec("qa", 0))
    p.run(sec("ka", 1), [[("rope", "qa", 0)], [("rope", "qa", 1)], []] + turns("qa"))
    p.run(sec("va", 2), [[("rope", "ka", 0)], [("rope", "ka", 1)], []] + turns("ka"))
    work = attention("a", HEADS)
    p.run(sec("qb", 4), work[:8])
    p.run(sec("kb", 5), work[8:16])
    p.run(sec("vb", 6), [[("rope", "qb", 0)] + work[16], [("rope", "qb", 1)] + work[17], [("rope", "kb", 0)], [("rope", "kb", 1)]]
          + turns("qb"))
    work = []
    for w in attention("b", DHEADS):
        scores = [x for x in w if x[0] == "b_scores"]
        work += [scores, [x for x in w if x not in scores]]
    p.run(sec("za", 3), [a + b for a, b in zip(turns("kb"), [[], [], [], []])] + work[:4])
    p.run(sec("ga", 8), [work[4] + [("gate", "a")]] + work[5:12])
    p.run(sec("gb", 9), [a + b for a, b in zip(work[12:20], [[]] + turns("ya") + [[]] * 3)])
    p.run(sec("zb", 7), [[("head_norm",)], [], [], [("gate", "b", 0)], [], [], [], [("gate", "b", 1)]])
    p.run(section("pa", "w_proj_a", 0, 1), [[], []] + turns("yb"))
    pb = section("pb", "w_proj_b", 0, 0)
    p.run(pb[:1])
    p.run(pb[1:], [[], [("turn", "mix", 0)], [("turn", "mix", 1)], []])
    p.run(section("out", "w_out", 0, 1), turns("mix", 2))
    return p.close()


class Core:

    def __init__(self, nc, ctx):
        self.nc, self.ctx = nc, ctx
        sb = lambda name, shape, dt=F32: ctx.enter_context(nc.sbuf_tensor(name, shape, dt))
        sem = lambda name: ctx.enter_context(nc.semaphore(name))
        self.x = sb("x_res", [P, TB, D])
        self.raw = [sb(f"raw{i}", [P, 4 * CH]) for i in range(RAW)]
        self.hi = [sb(f"hi{i}", [P, 2 * CH], F32R) for i in range(RING)]
        self.lo = [sb(f"lo{i}", [P, 2 * CH], F32R) for i in range(RING)]
        self.xh = [sb(f"xh{i}", [P, KB, S], F32R) for i in range(2)]
        self.xl = [sb(f"xl{i}", [P, KB, S], F32R) for i in range(2)]
        self.buf = [sb(f"buf{i}", [P, TB, D]) for i in range(9)]
        self.scratch = sb("scratch", [P, 5120])
        self.diagonal = self.scratch[:, 4096:4096 + TB * P].rearrange("p (t i) -> p t i", t=TB)
        self.masks = sb("masks", [P, 3, S])
        self.square = sb("square", [P, 3 + LEVELS, P])
        self.rope1 = sb("rope1", [P, TB, 4, ROT // 2])
        self.rope2 = sb("rope2", [P, TB, 4, ROT // 2])
        self.ident, self.upper, self.ones = (self.square[:, i, :] for i in range(3))
        self.small = sb("small", [P, 850])
        self.small_used = 0
        self.bank = [ctx.enter_context(nc.psum_tensor(f"bank{i}", [P, CH], F32)) for i in range(8)]
        self.passed = sem("passed")
        self.x_ready = sem("x_ready")
        self.programs = {e: [] for e in ("tensor", "scalar", "vector", "gpsimd", "sync")}
        self.unit_loaded = [sem(f"unit_loaded{i}") for i in range(RAW)]
        self.hi_ready, self.lo_ready, self.lo_ready_pool = sem("hi_ready"), sem("lo_ready"), sem("lo_ready_pool")
        self.pieces_used = sem("pieces_used")

    def program(self, engine):
        return self.programs[engine].append

    def tile(self, *shape):
        n = int(np.prod(shape))
        a = self.small[:, self.small_used:self.small_used + n]
        self.small_used += n
        assert self.small_used <= 850
        if len(shape) == 2:
            a = a.rearrange("p (a b) -> p a b", b=shape[1])
        if len(shape) == 3:
            a = a.rearrange("p (a b c) -> p a b c", b=shape[1], c=shape[2])
        return a


    def seed_ring(self, dve):
        z = self.small[0:1, 0:1]
        dve.memset(z, 0.0).then_inc(self.lo_ready, RAW)
        dve.memset(self.small[0:1, 1:2], 0.0).then_inc(self.lo_ready_pool, RAW)
        dve.memset(self.small[0:1, 2:3], 0.0).then_inc(self.pieces_used, RING)

    @staticmethod
    def lo_engine(g):
        return "pool" if g % 2 else "dve"

    def lo_wait(self, layer, base, pieces, g):
        pairs = layer * (pieces // 2) + (base // 2 + g // 2)
        return (self.lo_ready_pool if g % 2 else self.lo_ready), pairs + (RAW + 1)

    def load_unit(self, sp, layer, base, pieces, u, job, n):
        cut = layer * (pieces // 2) + (base // 2 + u + 1)
        sp.wait_ge(self.lo_ready, cut)
        sp.sem_inc(self.passed, 1)
        sp.wait_ge(self.lo_ready_pool, cut)
        sp.sem_inc(self.passed, 1)
        slot, k = u % RAW, job.unit
        r0 = (job.row + n * k) * P
        src = job.weight[layer, r0:r0 + k * P, job.col:job.col + job.cols].rearrange("(k p) c -> p k c", p=P)
        dst = self.raw[slot][:, 0:k * job.cols].rearrange("p (k c) -> p k c", k=k)
        sp.dma_start(dst, src).then_inc(self.unit_loaded[slot], 16)

    def piece_raw(self, plan, g):
        job, n = plan.pieces[g]
        w = job.unit // 2 * job.cols
        return self.raw[(g // 2) % RAW][:, n % 2 * w:n % 2 * w + w], w

    def split_hi(self, act, layer, base, plan, g):
        np_ = len(plan.pieces)
        src, w = self.piece_raw(plan, g)
        if g % 2 == 0:
            act.wait_ge(self.unit_loaded[(g // 2) % RAW],
                        (layer * (np_ // 8) + (base // 8 + g // 8 + 1)) * 16)
        act.wait_ge(self.pieces_used, layer * np_ + (base + g + 1))
        act.activation(self.hi[g % RING][:, 0:w], src, ACT.Copy).then_inc(self.hi_ready, 1)

    def split_lo(self, eng, layer, base, plan, g):
        np_ = len(plan.pieces)
        src, w = self.piece_raw(plan, g)
        eng.wait_ge(self.hi_ready, layer * np_ + (base + g + 1))
        sem = self.lo_ready_pool if self.lo_engine(g) == "pool" else self.lo_ready
        eng.tensor_tensor(self.lo[g % RING][:, 0:w], src, self.hi[g % RING][:, 0:w].bitcast(F32),
                          ALU.subtract).then_inc(sem, 1)

    def multiply(self, pe, layer, base, plan, g, rows=(0, 1)):
        job, n = plan.pieces[g]
        pe.wait_ge(*self.lo_wait(layer, base, len(plan.pieces), g))
        k, c, slot = job.unit // 2, job.cols, g % RING
        xh, xl = self.xh[job.xt], self.xl[job.xt]
        for kk in rows[:k]:
            row = job.xt_block + n * k + kk
            w = slice(kk * c, kk * c + c)
            for tb in range(TB):
                out, t = self.bank[job.banks[tb]][:, 0:c], slice(tb * P, tb * P + P)
                first = job.start and n == 0 and kk == 0
                last = job.stop and n == job.pieces - 1 and kk == k - 1
                pe.matmul(out, xh[:, row, t], self.hi[slot][:, w], start=first, stop=False)
                pe.matmul(out, xh[:, row, t], self.lo[slot][:, w], start=False, stop=False)
                mm = pe.matmul(out, xl[:, row, t], self.hi[slot][:, w], start=False, stop=last)
        if rows[-1] >= k - 1:
            mm.then_inc(self.pieces_used, 1)


SCORE, TURN, OUT = (4, 5), 6, 7


def bcast(ap, axis, n):
    a = ap.unsqueeze(axis)
    shape = list(a.shape)
    shape[axis] = n
    return a.to_broadcast(shape)


def turn_fill(nc, pe, core, bank, src, f):
    for j in range(2):
        for tb in range(TB):
            c = (2 * f + j) * P
            mm = pe.transpose(bank[:, (j * TB + tb) * P:(j * TB + tb + 1) * P],
                              src[:, tb, c:c + P], core.ident)
    return mm


def block_one(nc, core, s, plan, ins):
    q_tok, k_tok, qT, kT, va, vb, ya, yb, z = core.buf
    role = {"qa": q_tok, "ka": k_tok, "va": va, "qb": q_tok, "kb": k_tok, "vb": vb, "za": z, "zb": z,
            "ga": q_tok, "gb": k_tok, "mix": qT}
    source = {"qa": q_tok, "ka": k_tok, "qb": q_tok, "kb": k_tok, "ya": ya, "yb": yb, "mix": qT}
    target = {"qa": qT, "ka": kT, "qb": qT, "kb": kT}
    xt_of = {"h": 0, "ya": 1, "yb": 0, "mix": 1}
    gain_of = {"h": list(range(KB)), "yb": [KB] * KB}
    scr = core.scratch
    prob = [scr[:, i * 768:(i + 1) * 768].rearrange("p (m c) -> p m c", m=2) for i in range(2)]
    masked = scr[:, 1536:2304].rearrange("p (m c) -> p m c", m=2)
    turned = scr[:, 2304:2688]
    diff = scr[:, 2688:3072]
    junk = scr[:, 3072:4096]
    t = core.t1
    P_ = len(plan.pieces)
    base = 0
    at, up = s.at, s.up
    B = core.bank
    own, both = slice(P, 2 * P), slice(0, 2 * P)

    parts = [(0, slice(0, P), own), (1, slice(P, 3 * P), both)]

    @core.program("tensor")
    def _(pe):
        with pe.Fori(0, DEPTH) as layer:
            s.layer = layer
            last_read = {}

            def free(b):
                if b in last_read:
                    pe.wait_ge(*at(*last_read[b]))

            turn_at = 0
            for what in plan.steps:
                kind, arg = what[0], what[1] if len(what) > 1 else None
                if kind == "piece":
                    job, n = plan.pieces[arg]
                    if n == 0:
                        for b in job.banks:
                            free(b)
                        if job.name == "pa0":
                            pe.wait_ge(*at("cut", ("ya", 3)))
                        if job.name == "pb0":
                            pe.wait_ge(*at("cut", ("yb", 3)))
                    if job.name == "qa0":
                        pe.wait_ge(*at("cut", ("h", n)))
                    if job.name == "out0":
                        pe.wait_ge(*at("cut", ("mix", n)))
                    core.multiply(pe, layer, base, plan, arg)
                    if n == job.pieces - 1:
                        for b in job.banks:
                            last_read[b] = ("sigmoid" if job.name[0] == "g" else "evac", job.name)
                if kind == "turn":
                    f = what[2]
                    b = (TURN, OUT)[turn_at % 2]
                    turn_at += 1
                    free(b)
                    if arg == "h":
                        pe.wait_ge(*at("h_ready"))
                    elif arg in ("qa", "ka", "qb", "kb"):
                        pe.wait_ge(*at("rotated", arg))
                    elif arg == "mix":
                        pe.wait_ge(*at("mix", f // 2))
                    elif arg == "yb":
                        pe.wait_ge(*at("yb_gated", f // 2))
                    else:
                        pe.wait_ge(*at("gated", "a"))
                    mm = turn_scaled(pe, core, B[b], f) if arg == "h" else turn_fill(nc, pe, core, B[b], source[arg], f)
                    mm.then_inc(*up("turned", (arg, f)))
                    t.turn_bank[arg, f] = b
                    last_read[b] = ("cut" if arg in xt_of else "turn_copied", (arg, f))
                if kind == "a_scores":
                    h, b = arg, SCORE[arg % 2]
                    free(b)
                    pe.wait_ge(*at("turn_copied", ("ka", h // 4)))
                    r = slice(HD * (h % 2), HD * (h % 2) + HD)
                    pe.matmul(B[b][:, 0:P], qT_(qT)[r, h // 2, 0:P], qT_(kT)[r, h // 2, 0:P],
                              start=True, stop=True)
                    pe.matmul(B[b][:, P:3 * P], qT_(qT)[r, h // 2, P:S], qT_(kT)[r, h // 2, :],
                              start=True, stop=True).then_inc(*up("a_scored", h))
                    last_read[b] = ("a_max", h)
                if kind == "a_turn":
                    h = arg
                    free(TURN)
                    pe.wait_ge(*at("a_prob", h))
                    for c in range(3):
                        mm = pe.transpose(B[TURN][:, c * P:c * P + P], prob[h % 2][:, 0, c * P:c * P + P],
                                          core.ident)
                    mm.then_inc(*up("a_turned", h))
                    last_read[TURN] = ("a_copied", h)
                if kind == "a_out":
                    h = arg
                    free(OUT)
                    pe.wait_ge(*at("a_copied", h))
                    if h == 0:
                        pe.wait_ge(*at("evac", "va1"))
                    values = slice(h * HD, h * HD + HD)
                    pe.matmul(B[OUT][:, 0:HD], turned[:, 0:P], va[:, 0, values], start=True, stop=True)
                    pe.matmul(B[OUT][:, HD:2 * HD], turned[:, P:2 * P], va[:, 0, values], start=True, stop=False)
                    pe.matmul(B[OUT][:, HD:2 * HD], turned[:, 2 * P:3 * P], va[:, 1, values],
                              start=False, stop=True).then_inc(*up("a_summed", h))
                    last_read[OUT] = ("ya", h)
                if kind == "b_scores":
                    h = arg
                    pe.wait_ge(*at("turn_copied", ("kb", h // 2)))
                    for m in range(2):
                        b = SCORE[m]
                        free(b)
                        r = slice(HD * m, HD * m + HD)
                        pe.matmul(B[b][:, 0:P], qT_(qT)[r, h, 0:P], qT_(kT)[r, h, 0:P], start=True, stop=True)
                        pe.matmul(B[b][:, P:3 * P], qT_(qT)[r, h, P:S], qT_(kT)[r, h, :],
                                  start=True, stop=True).then_inc(*up("b_scored", (h, m)))
                        last_read[b] = ("b_max", (h, m))
                if kind == "b_turn":
                    h = arg
                    free(TURN)
                    pe.wait_ge(*at("b_diff", h))
                    for c in range(3):
                        mm = pe.transpose(B[TURN][:, c * P:c * P + P], diff[:, c * P:c * P + P], core.ident)
                    mm.then_inc(*up("b_turned", h))
                    last_read[TURN] = ("b_copied", h)
                if kind == "b_out":
                    h = arg
                    free(OUT)
                    pe.wait_ge(*at("b_copied", h))
                    if h == 0:
                        pe.wait_ge(*at("evac", "vb1"))
                    values = slice(h * DV, h * DV + DV)
                    pe.matmul(B[OUT][:, 0:DV], turned[:, 0:P], vb[:, 0, values], start=True, stop=True)
                    pe.matmul(B[OUT][:, DV:2 * DV], turned[:, P:2 * P], vb[:, 0, values], start=True, stop=False)
                    pe.matmul(B[OUT][:, DV:2 * DV], turned[:, 2 * P:3 * P], vb[:, 1, values],
                              start=False, stop=True).then_inc(*up("b_summed", h))
                    last_read[OUT] = ("yb", h)

    @core.program("scalar")
    def _(act):
        with act.Fori(0, DEPTH) as layer:
            s.layer = layer
            for what in plan.steps:
                kind, arg = what[0], what[1] if len(what) > 1 else None
                if kind == "norm":
                    row_squares(act, s, [((core.x_ready, layer * 2 + (c + 1)) if tb == 0 else None,
                                          core.x[:, tb, c * CH:c * CH + CH], t.ssq[:, c, tb:tb + 1])
                                         for c in range(2) for tb in range(TB)], junk, "x0")
                if kind == "norm":
                    for g in range(LEAD):
                        core.split_hi(act, layer, base, plan, g)
                if kind == "piece" and arg + LEAD < P_:
                    core.split_hi(act, layer, base, plan, arg + LEAD)
                if kind == "turn" and arg in xt_of:
                    f = what[2]
                    act.wait_ge(*at("turned", (arg, f)))
                    bank = B[t.turn_bank[arg, f]][:, :].rearrange("p (j t) -> p j t", j=2)
                    xh = core.xh[xt_of[arg]]
                    if arg in gain_of:
                        for j in range(2):
                            gain = t.gain[:, gain_of[arg][2 * f + j]:gain_of[arg][2 * f + j] + 1]
                            act.activation(xh[:, 2 * f + j, :], bank[:, j, :], ACT.Copy,
                                           scale=gain).then_inc(*up("high", (arg, f, j)))
                    else:
                        act.activation(xh[:, 2 * f:2 * f + 2, :], bank, ACT.Copy).then_inc(*up("high", (arg, f, 1)))
                if kind == "evac" and arg[:2] in ("za", "zb", "ga", "gb"):
                    c = int(arg[2])
                    if arg == "zb0":
                        act.wait_ge(*at("gated", "a"))
                    if arg == "ga0":
                        act.wait_ge(*at("turned", ("qb", 3)))
                    if arg == "gb0":
                        act.wait_ge(*at("turned", ("kb", 3)))
                    for tb in range(TB):
                        act.wait_ge(core.pieces_used, layer * P_ + (base + plan.end[arg] + RING + 1))
                        ins = act.activation(role[arg[:2]][:, tb, c * CH:c * CH + CH],
                                             B[plan.by_name[arg].banks[tb]][:, :], ACT.Sigmoid)
                        if tb == TB - 1:
                            ins.then_inc(*up("sigmoid", arg))
                if kind == "a_scores":
                    h = arg
                    act.wait_ge(*at("a_max", h))
                    if h >= 2:
                        act.wait_ge(*at("a_turned", h - 2))
                    for tb, cols, _ in parts:
                        ins = act.activation(prob[h % 2][:, 0, cols], masked[:, h % 2, cols], ACT.Exp, scale=SCALE,
                                             bias=t.negmax[:, h % 2, tb:tb + 1],
                                             accum_out=t.total[:, h % 4, tb:tb + 1])
                    ins.then_inc(*up("a_prob", h))
                if kind == "b_scores":
                    h = arg
                    for m in range(2):
                        act.wait_ge(*at("b_max", (h, m)))
                        if h >= 2:
                            act.wait_ge(*at("b_diff", h - 2))
                        for tb, cols, _ in parts:
                            ins = act.activation(prob[h % 2][:, m, cols], masked[:, m, cols], ACT.Exp, scale=SCALE,
                                                 bias=t.negmax[:, m, tb:tb + 1],
                                                 accum_out=t.total[:, (h % 2) * 2 + m, tb:tb + 1])
                        ins.then_inc(*up("b_prob", (h, m)))
                if kind in ("a_turn", "b_turn"):
                    w, h = kind[0], arg
                    act.wait_ge(*at(f"{w}_turned", h))
                    if h >= 1:
                        act.wait_ge(*at(f"{w}_summed", h - 1))
                    act.activation(turned, B[TURN][:, 0:3 * P], ACT.Copy).then_inc(*up(f"{w}_copied", h))
                if kind == "b_out":
                    h = arg
                    act.wait_ge(*at("yb", h))
                    for tb in range(TB):
                        if h or tb:
                            act.wait_ge(*at("yb_square", (h, 0) if tb else (h - 1, 1)))
                        act.activation(junk[:, 0:DV], yb[:, tb, h * DV:h * DV + DV], ACT.Square,
                                       accum_out=t.head_ssq[:, tb, h:h + 1]).then_inc(*up("yb_square", (h, tb)))

    @core.program("vector")
    def _(dve):
        with dve.Fori(0, DEPTH) as layer:
            s.layer = layer
            dve.tensor_copy(t.gain[:, 0:KB + 1], t.gain_all[:, layer, :]).then_inc(*up("gain", 0))
            dve.tensor_copy(t.neglam[:, 0:1], t.neglam_all[:, layer, :]).then_inc(*up("gain", 1))
            for what in plan.steps:
                kind, arg = what[0], what[1] if len(what) > 1 else None
                if kind == "piece" and arg + LO_LEAD < P_ and core.lo_engine(arg + LO_LEAD) == "dve":
                    core.split_lo(dve, layer, base, plan, arg + LO_LEAD)
                if kind == "norm":
                    rstd_diagonal(dve, s, core, "x0", up("h_ready", 0))
                if kind == "norm":
                    for g in range(LO_LEAD):
                        if core.lo_engine(g) == "dve":
                            core.split_lo(dve, layer, base, plan, g)
                if kind == "turn":
                    f = what[2]
                    bank = B[t.turn_bank[arg, f]][:, :].rearrange("p (j t) -> p j t", j=2)
                    if arg in xt_of:
                        xh, xl = core.xh[xt_of[arg]], core.xl[xt_of[arg]]
                        if arg in gain_of:
                            for j in range(2):
                                n = 2 * f + j
                                gain = t.gain[:, gain_of[arg][n]:gain_of[arg][n] + 1]
                                dve.wait_ge(*at("high", (arg, f, 1)))
                                ins = dve.scalar_tensor_tensor(xl[:, n, :], bank[:, j, :], gain,
                                                               xh[:, n, :].bitcast(F32), ALU.mult, ALU.subtract)
                        else:
                            dve.wait_ge(*at("high", (arg, f, 1)))
                            ins = dve.tensor_tensor(xl[:, 2 * f:2 * f + 2, :], bank,
                                                    xh[:, 2 * f:2 * f + 2, :].bitcast(F32), ALU.subtract)
                        ins.then_inc(*up("cut", (arg, f)))
                    else:
                        dve.wait_ge(*at("turned", (arg, f)))
                        if arg in ("qb", "kb") and f == 0:
                            dve.wait_ge(*at("a_scored", HEADS - 1))
                        dve.tensor_copy(qT_(target[arg])[:, 2 * f:2 * f + 2, :], bank)\
                           .then_inc(*up("turn_copied", (arg, f)))
                if kind == "evac":
                    job, c = plan.by_name[arg], int(arg[-1])
                    cols = slice(c * CH, c * CH + CH)
                    name = arg[:-1]
                    done = (core.pieces_used, layer * P_ + (base + plan.end[arg] + RING + 1))
                    if name in ("qa", "ka", "va", "qb", "kb", "vb"):
                        if arg == "qb0":
                            dve.wait_ge(*at("turned", ("qa", 3)))
                        if arg == "kb0":
                            dve.wait_ge(*at("turned", ("ka", 3)))
                        for tb in range(TB):
                            dve.wait_ge(*done)
                            ins = dve.tensor_copy(role[name][:, tb, cols], B[job.banks[tb]][:, :])
                        ins.then_inc(*up("evac", arg))
                    if name in ("za", "zb"):
                        for tb in range(TB):
                            dve.wait_ge(*at("sigmoid", arg))
                            ins = dve.tensor_tensor(z[:, tb, cols], B[job.banks[tb]][:, :], z[:, tb, cols], ALU.mult)
                        ins.then_inc(*up("evac", arg))
                    if name == "pa":
                        for tb in range(TB):
                            dve.wait_ge(*done)
                            dve.wait_ge(*at("sigmoid", "ga1"))
                            dve.wait_ge(*at("b_scored", (DHEADS - 1, 1)))
                            ins = dve.tensor_tensor(qT[:, tb, cols], B[job.banks[tb]][:, :], q_tok[:, tb, cols], ALU.mult)
                        ins.then_inc(*up("evac", arg))
                    if name == "pb":
                        for tb in range(TB):
                            dve.wait_ge(*done)
                            dve.wait_ge(*at("sigmoid", "gb1"))
                            dve.tensor_tensor(k_tok[:, tb, cols], B[job.banks[tb]][:, :], k_tok[:, tb, cols],
                                              ALU.mult).then_inc(*up("evac", (arg, tb)))
                        dve.wait_ge(*at("evac", (arg, 1)))
                        dve.wait_ge(*at("evac", "pa1"))
                        dve.tensor_tensor(qT[:, :, cols], qT[:, :, cols], k_tok[:, :, cols], ALU.add)\
                           .then_inc(*up("mix", c))
                        s.keys["evac", arg] = s.keys["evac", (arg, 1)]
                    if name == "out":
                        for tb in range(TB):
                            dve.wait_ge(*done)
                            ins = dve.tensor_tensor(core.x[:, tb, cols], B[job.banks[tb]][:, :],
                                                    core.x[:, tb, cols], ALU.add)
                        ins.then_inc(core.x_ready, 1)
                if kind == "a_scores":
                    h = arg
                    masked_max(dve, core, s, B[SCORE[h % 2]], masked[:, h % 2, :], t.top[:, h % 2, :],
                               t.negmax[:, h % 2, :], parts, 0, ("a_scored", h), ("a_prob", h - 2) if h >= 2 else None,
                               ("a_top", h), ("a_max", h))
                if kind == "b_scores":
                    h = arg
                    for m in range(2):
                        masked_max(dve, core, s, B[SCORE[m]], masked[:, m, :], t.top[:, m, :],
                                   t.negmax[:, m, :], parts, 1, ("b_scored", (h, m)),
                                   ("b_prob", (h - 1, m)) if h >= 1 else ("a_prob", HEADS - 1),
                                   ("b_top", (h, m)), ("b_max", (h, m)))
                if kind == "a_turn":
                    h = arg
                    dve.wait_ge(*at("a_prob", h))
                    dve.reciprocal(t.inverse[:, h % 4, :], t.total[:, h % 4, :]).then_inc(*up("a_inverse", h))
                if kind == "a_out":
                    h = arg
                    dve.wait_ge(*at("a_summed", h))
                    dve.wait_ge(*at("a_inverse", h))
                    dve.tensor_tensor(ya[:, :, h * HD:h * HD + HD],
                                      B[OUT][:, 0:2 * HD].rearrange("p (t d) -> p t d", t=TB),
                                      bcast(t.inverse[:, h % 4, :], 2, HD), ALU.mult).then_inc(*up("ya", h))
                if kind == "gate" and arg == "b":
                    c = what[2]
                    dve.wait_ge(*at("head_rstd"))
                    dve.wait_ge(*at("evac", f"zb{c}"))
                    for h in range(c * CH // DV, (c + 1) * CH // DV):
                        for tb in range(TB):
                            v = yb[:, tb, h * DV:h * DV + DV]
                            ins = dve.scalar_tensor_tensor(v, v, t.head_rstd[:, tb, h:h + 1],
                                                           z[:, tb, h * DV:h * DV + DV], ALU.mult, ALU.mult)
                    ins.then_inc(*up("yb_gated", c))
                if kind == "b_turn":
                    h = arg
                    i = (h % 2) * 2
                    dve.wait_ge(*at("b_prob", (h, 1)))
                    dve.reciprocal(t.inverse[:, i:i + 2, :], t.total[:, i:i + 2, :]).then_inc(*up("b_inverse", h))
                    dve.wait_ge(*at("b_inverse", h))
                    dve.scalar_tensor_tensor(t.weight[:, 0:2], t.inverse[:, i + 1, :], t.neglam[:, 0:1],
                                             t.total[:, i, :], ALU.mult, ALU.mult).then_inc(*up("b_weight", h))
                    dve.wait_ge(*at("b_weight", h))
                    if h >= 1:
                        dve.wait_ge(*at("b_turned", h - 1))
                    for tb, cols, _ in parts:
                        ins = dve.scalar_tensor_tensor(diff[:, cols], prob[h % 2][:, 1, cols], t.weight[:, tb:tb + 1],
                                                       prob[h % 2][:, 0, cols], ALU.mult, ALU.add)
                    ins.then_inc(*up("b_diff", h))
                if kind == "b_out":
                    h = arg
                    i = (h % 2) * 2
                    dve.wait_ge(*at("b_summed", h))
                    dve.tensor_tensor(yb[:, :, h * DV:h * DV + DV],
                                      B[OUT][:, 0:2 * DV].rearrange("p (t d) -> p t d", t=TB),
                                      bcast(t.inverse[:, i, :], 2, DV), ALU.mult).then_inc(*up("yb", h))

    @core.program("gpsimd")
    def _(pool):
        with pool.Fori(0, DEPTH) as layer:
            s.layer = layer
            for what in plan.steps:
                kind, arg = what[0], what[1] if len(what) > 1 else None
                if kind == "piece" and arg + LO_LEAD < P_ and core.lo_engine(arg + LO_LEAD) == "pool":
                    core.split_lo(pool, layer, base, plan, arg + LO_LEAD)
                if kind == "norm":
                    row_rstd(pool, s, core, "x0", 2)
                if kind == "norm":
                    for g in range(LO_LEAD):
                        if core.lo_engine(g) == "pool":
                            core.split_lo(pool, layer, base, plan, g)
                if kind == "rope":
                    rotate(pool, s, what[2], role[arg], core.rope1, t.rot[0], t.rot[1], ("evac", f"{arg}1"), arg, HEADS)
                if kind == "head_norm":
                    pool.wait_ge(*at("yb_square", (DHEADS - 1, 1)))
                    rsqrt(pool, s, core, t.head_ssq, t.head_rstd, 1.0 / DV, 1e-5, "head_mean", "head_rstd", 0)
                if kind == "gate" and arg == "a":
                    pool.wait_ge(*at("evac", "za1"))
                    pool.wait_ge(*at("ya", HEADS - 1))
                    pool.tensor_tensor(ya[:, :, :], ya[:, :, :], z[:, :, :], ALU.mult).then_inc(*up("gated", arg))

    @core.program("sync")
    def _(sp):
        with sp.Fori(0, DEPTH) as layer:
            for u, (job, n) in enumerate(plan.units):
                job.weight = ins[job.weight] if isinstance(job.weight, str) else job.weight
                core.load_unit(sp, layer, base, P_, u, job, n)


def qT_(buf):
    return buf[:, :, :].rearrange("p a b -> p (a b)").rearrange("p (k t) -> p k t", t=S)


def masked_max(dve, core, s, bank, masked, top, negmax, parts, which, scored, tile_free, top_sig, done, sink=None):
    dve.wait_ge(*s.at(*scored))
    if tile_free:
        dve.wait_ge(*s.at(*tile_free))
    dve.sem_inc(core.passed, 1)
    for tb, cols, keys in parts:
        ins = dve.tensor_tensor_reduce(masked[:, cols], bank[:, cols], core.masks[:, which, keys], 1.0,
                                       NEG if sink is None else sink[0],
                                       ALU.add, ALU.max, top[:, tb:tb + 1])
    ins.then_inc(*s.up(*top_sig))
    dve.wait_ge(*s.at(*top_sig))
    if sink:
        dve.tensor_scalar(sink[1], top[:, :], sink[0], -SCALE, ALU.subtract, ALU.mult)
    dve.tensor_scalar(negmax[:, :], top[:, :], -SCALE, None, ALU.mult).then_inc(*s.up(*done))


def rsqrt(pool, s, core, total, out, scale, eps, mean_sig, done_sig, key):
    pool.sem_inc(core.passed, 1)
    pool.tensor_scalar(out, total, scale, eps, ALU.mult, ALU.add).then_inc(*s.up(mean_sig, key))
    pool.wait_ge(*s.at(mean_sig, key))
    n = int(np.prod(out.shape[1:]))
    half = core.t1.minus_half[:, 0:n]
    if len(out.shape) == 3:
        half = half.rearrange("p (a b) -> p a b", b=out.shape[2])
    pool.tensor_tensor(out, out, half, ALU.pow).then_inc(*s.up(done_sig, key))


def rotate(pool, s, tb, buf, table, r0, r1, ready, name, heads):
    half = ROT // 2
    pool.wait_ge(*s.at(*ready))
    v = buf[:, tb, 0:heads * HD].rearrange("p (h d) -> p h d", d=HD)
    a, b = v[:, :, 0:half], v[:, :, half:ROT]
    cos = bcast(table[:, tb, 0, :], 1, heads)
    if tb == 0 and name in s.rot_before:
        pool.wait_ge(*s.at("rotated", s.rot_before[name]))
    if tb:
        pool.wait_ge(*s.at("rot_done", (name, 0)))
    pool.tensor_tensor(r0[:, 0:heads, 0:half], b, bcast(table[:, tb, 2, :], 1, heads), ALU.mult)
    pool.tensor_tensor(r0[:, 0:heads, half:ROT], a, bcast(table[:, tb, 3, :], 1, heads), ALU.mult)
    pool.tensor_tensor(r1[:, 0:heads, 0:half], a, cos, ALU.mult)
    pool.tensor_tensor(r1[:, 0:heads, half:ROT], b, cos, ALU.mult).then_inc(*s.up("rot_parts", (name, tb)))
    pool.wait_ge(*s.at("rot_parts", (name, tb)))
    pool.tensor_tensor(v[:, :, 0:ROT], r0[:, 0:heads, :], r1[:, 0:heads, :], ALU.add)\
        .then_inc(*s.up("rot_done" if tb < TB - 1 else "rotated", (name, tb) if tb < TB - 1 else name))


class Tiles:
    pass


def setup(nc, core, s, ins):
    t = core.t1 = Tiles()
    t.ssq, t.rstd = core.tile(2, TB), core.tile(TB)
    t.head_ssq, t.head_rstd = core.tile(TB, DHEADS), core.tile(TB, DHEADS)
    t.top, t.negmax = core.tile(2, TB), core.tile(2, TB)
    t.total, t.inverse, t.weight = core.tile(4, TB), core.tile(4, TB), core.tile(TB)
    t.gain, t.gain_all = core.tile(KB + 1), core.tile(DEPTH, KB + 1)
    t.neglam, t.neglam_all = core.tile(1), core.tile(DEPTH, 1)
    t.minus_half = core.tile(32)
    t.rot = [core.scratch[:, first:first + HEADS * ROT].rearrange("p (h d) -> p h d", d=ROT)
             for first in (4608, 4864)]
    t.turn_bank = {}
    s.rot_before = {"ka": "qa", "qb": "ka", "kb": "qb"}
    at, up = s.at, s.up
    rows = core.buf[8][:, 0, 0:P]
    lam = core.scratch[:, 0:4 * DEPTH * HD].rearrange("p (n l d) -> p n l d", n=4, l=DEPTH)
    dots = core.tile(2, DEPTH)
    junk = core.scratch[:, 1024:1024 + HD]
    R = KB + 1

    @core.program("sync")
    def _(sp):
        for tb in range(TB):
            sp.dma_start(core.x[:, tb, :], ins["x"][0, tb * P:tb * P + P, :]).then_inc(*up("x_loaded", tb, 16))
        sp.dma_start(core.square[:, :, :], ins["square"]).then_inc(*up("square_loaded", 0, 16))
        for l in range(DEPTH):
            sp.dma_start(rows[l * R:l * R + KB, :], ins["norm_w"][l].rearrange("(k p) -> k p", p=P))\
              .then_inc(*up("rows_loaded", (l, 0), 16))
            sp.dma_start(rows[l * R + KB:l * R + R, :], ins["subln_w"][l:l + 1, :])\
              .then_inc(*up("rows_loaded", (l, 1), 16))
        for n, name in enumerate(("lambda_q1", "lambda_k1", "lambda_q2", "lambda_k2")):
            sp.dma_start(lam[:, n, :, :], ins[name].partition_broadcast(P)).then_inc(*up("lambda_loaded", n, 16))
        sp.dma_start(core.masks[:, :, :], ins["masks"]).then_inc(*up("tables_loaded", 0, 16))
        sp.dma_start(core.rope1[:, :, :, :], ins["rope"].rearrange("t p (r d) -> p t r d", d=ROT // 2))\
          .then_inc(*up("tables_loaded", 1, 16))

    @core.program("tensor")
    def _(pe):
        pe.wait_ge(*at("square_loaded"))
        pe.wait_ge(*at("rows_loaded", (DEPTH - 1, 1)))
        pe.transpose(core.bank[TURN][:, 0:DEPTH * R], rows[0:DEPTH * R, :],
                     core.ident[0:DEPTH * R, 0:DEPTH * R]).then_inc(*up("gains_turned"))

    @core.program("scalar")
    def _(act):
        act.wait_ge(*at("dots", (1, DEPTH - 1)))
        act.activation(dots, dots, ACT.Exp).then_inc(*up("dots_exp"))

    @core.program("vector")
    def _(dve):
        dve.memset(t.minus_half, -0.5).then_inc(*up("minus_half"))
        dve.wait_ge(*at("gains_turned"))
        dve.tensor_copy(t.gain_all, core.bank[TURN][:, 0:DEPTH * R].rearrange("p (l r) -> p l r", r=R))\
           .then_inc(*up("gains", 0))
        dve.wait_ge(*at("lambda_loaded", 3))
        for n in range(2):
            for l in range(DEPTH):
                if n or l:
                    dve.wait_ge(*at("dots", (n, 0) if l else (n - 1, DEPTH - 1)))
                dve.tensor_tensor_reduce(junk, lam[:, 2 * n, l, :], lam[:, 2 * n + 1, l, :], 1.0, 0.0,
                                         ALU.mult, ALU.add, dots[:, n, l:l + 1]).then_inc(*up("dots", (n, l)))
        dve.wait_ge(*at("dots_exp"))
        dve.tensor_tensor(t.neglam_all.rearrange("p l a -> p (l a)"), dots[:, 1, :], dots[:, 0, :], ALU.subtract).then_inc(*up("neglam", 0))
        dve.wait_ge(*at("neglam", 0))
        dve.wait_ge(*at("gains", 0))
        for l in range(DEPTH):
            dve.tensor_scalar(t.neglam_all[:, l, :], t.neglam_all[:, l, :], -lambda_init(l), None,
                              ALU.add).then_inc(*up("neglam", l + 1))
            g = t.gain_all[:, l, KB:KB + 1]
            dve.tensor_scalar(g, g, 1.0 - lambda_init(l), None, ALU.mult).then_inc(*up("gains", l + 1))
        dve.wait_ge(*at("neglam", DEPTH))
        dve.wait_ge(*at("gains", DEPTH))
        dve.wait_ge(*at("tables_loaded", 1))
        dve.wait_ge(*at("x_loaded", 1))
        dve.memset(t.top, 0.0).then_inc(core.x_ready, 2)


def final_norm(nc, core, s, ins):
    t = core.t1
    row = core.buf[3][:, 0, :]
    junk = core.buf[3][:, 1, :]
    at, up = s.at, s.up

    @core.program("scalar")
    def _(act):
        act.dma_start(row, ins["final_norm_w"].partition_broadcast(P)).then_inc(*up("row_loaded", 0, 16))
        row_squares(act, s, [((core.x_ready, 2 * DEPTH + 1 + c) if tb == 0 else None,
                              core.x[:, tb, c * CH:c * CH + CH], t.ssq[:, c, tb:tb + 1])
                             for c in range(2) for tb in range(TB)], junk, "final")

    @core.program("gpsimd")
    def _(pool):
        row_rstd(pool, s, core, "final", 2)

    @core.program("vector")
    def _(dve):
        dve.wait_ge(*at("row_loaded"))
        dve.wait_ge(*at("rstd", "final"))
        for tb in range(TB):
            dve.scalar_tensor_tensor(core.x[:, tb, :], core.x[:, tb, :], t.rstd[:, tb:tb + 1], row,
                                     ALU.mult, ALU.mult).then_inc(core.x_ready, 1)


def store(nc, core, s, out, layers):
    @core.program("sync")
    def _(sp):
        for tb in range(TB):
            sp.wait_ge(core.x_ready, 2 * layers - 1 + tb)
            sp.dma_start(out[0, tb * P:tb * P + P, :], core.x[:, tb, :]).then_inc(*s.up("stored", tb, 16))
        sp.wait_ge(*s.at("stored", TB - 1))



def plan_two():
    p = Plan()
    sec = lambda n, col: section(n, "w_in_2", col, 0)
    small = 2 * DHEADS + 256
    at_sw = 4 * D
    p.step("norm")
    start_turns(p, "h", [Job("ba0", "w_in_2", 0, at_sw, KB, small, 2, 0, 0, (2, 3))])
    p.run(sec("sq", at_sw + small), [[("decay",)], [("decay_sum",)]])
    work = [w[:1] + w[:0:-1] if len(w) == 3 else w for w in attention("s", HEADS)]
    p.run(sec("dq", 0), [[("rope", "sk", 0), ("rope", "sk", 1), ("rope", "sq", 0)], [("rope", "sq", 1)], [],
                         [("turn", "sk", 0)]] + turns("sq", 0, 3) + [turns("sq", 3)[0] + work[0]])
    conv = lambda n: spread(turns(n), 2)
    p.run(sec("dk", D), [b + a for a, b in zip(conv("dq"), work[1:9])])
    p.run(sec("dv", 2 * D), [b + a for a, b in zip(
                              [a + b for a, b in zip([[("silu", "dq")]] + conv("dk")[:7],
                                                     [[], [], [("square", "dq")], [], [], [("squares", "dq")], [], []])],
                              work[9:17])])
    groups = delta_rule()
    before = [work[17], [("turn", "dv", 0)], [("silu", "dk"), ("square", "dk")], [("turn", "dv", 1)], [],
              [("turn", "dv", 2), ("squares", "dk")], [], [("turn", "dv", 3)], [("silu", "dv"), ("scales",)]]
    slots = [[] for _ in range(64)]
    for i, b in enumerate(before):
        slots[i] += b
    first = 9
    back = [[("turn", "v", f)] for f in range(4)] + [[("turn", "kd", f)] for f in range(2)]
    for i, b in enumerate(back):
        slots[11 + i] += b
    room = len(slots) - first - 1
    for i, b in enumerate(groups):
        slots[first + i * room // len(groups)] += b
    ys = turns("ys")
    for i in range(4):
        slots[34 + 3 * i] += ys[i]
    p.run(sec("gb", at_sw + small + 2 * CH + D), slots[:16], halves=True)
    p.run(sec("ga", at_sw + small + 2 * CH), slots[16:32], halves=True)
    p.run(sec("zz", 3 * D), slots[32:48], halves=True)
    for i, g in enumerate((0, 1, 2)):
        slots[52 + 2 * i] += [("head_norm", g)]
    slots[63] += [("head_norm", 3)]
    p.run(section("us", "w_up_sw_2", 0, 1), slots[48:], halves=True)
    p.step("post_rows")
    ud = section("ud", "w_up_dn_2", 0, 0)
    start_turns(p, "yd", ud[:1])
    p.run(ud[1:], [[], [("turn", "mix", 0)], [("turn", "mix", 1)], []])
    p.run(section("oo", "w_o_2", 0, 1), turns("mix", 2))
    p.step("post", 0)
    p.step("norm_mlp")
    parts = 4 * D // CH
    up_ = lambda j: [Job(f"up{j}", "w_ff1_2", 0, j * CH, KB, CH, 4, 0, 0, SCORE if j else (2, 3))]
    start_turns(p, "h2", up_(0))
    for j in range(parts):
        turn = [[], [("turn", f"f{j}", 0)], [("turn", f"f{j}", 1)], []]
        if j + 1 < parts:
            p.run(up_(j + 1), turn)
        else:
            for steps in turn:
                p.steps.extend(steps)
        p.run([Job(f"dn{j}_{c}", "w_ff2_2", 4 * j, c * CH, 4, CH, 4, 1, 4 * (j % 2), (2 * c, 2 * c + 1),
                   start=j == 0, stop=j == parts - 1) for c in range(2)])
    p.step("post", 1)
    return p.close()


def delta_rule():
    prepare = lambda g: {"t3": ("rows", g), "y4": ("betas", g), "t4": ("gram", g), "y5": ("gram_q", g),
                         "t5": ("inverse", g), "y6": ("join", g)}
    finish = lambda g: {at: (f"delta_{n}", g) for at, n in zip(("y1", "t1", "y2", "t2", "y3"), "usrvo")}
    out = [[step] for step in prepare(0).values()]
    out[-3:-1] = [out[-3] + out[-2]]
    for g in range(DHEADS // 2):
        before = finish(g - 1) if g else {}
        after = prepare(g + 1) if g + 1 < DHEADS // 2 else {}
        for l in range(1, LEVELS):
            for part in "yt":
                out.append([(f"level_{part}", g, l)] + [d[f"{part}{l}"] for d in (after, before) if f"{part}{l}" in d])
    return out + [[step] for step in finish(g).values()]


def setup_two(nc, core, s, ins):
    t2 = core.t2 = Tiles()
    R = 2 * KB + 1 + 4 * 3 * DHEADS
    t2.cols, t2.cols_all = core.tile(R), core.tile(DEPTH, R)
    t2.sink, t2.sink_all = core.tile(HEADS), core.tile(DEPTH, HEADS)
    t2.nega, t2.nega_all = core.tile(DHEADS), core.tile(DEPTH, DHEADS)
    t2.dtb, t2.dtb_all = core.tile(DHEADS), core.tile(DEPTH, DHEADS)
    at, up = s.at, s.up
    half = ROT // 2
    late = core.buf[7][:, :, :].rearrange("p a b -> p (a b)")
    rows = [late[:, l * P:l * P + P] for l in range(DEPTH)]
    work = late[:, 1024:1024 + 12 * TB * half].rearrange("p (n t r) -> p n t r", n=12, t=TB)
    pos_i = late[:, 1400:1400 + TB].bitcast(I32)
    pos = late[:, 1404:1404 + TB]
    inv = late[:, 1410:1410 + half]
    chain = [0]

    @core.program("scalar")
    def _(act):
        act.dma_start(inv, ins["inv_freq"]).then_inc(*up("positions", 0, 16))
        for tb in range(TB):
            act.dma_start(pos_i[:, tb:tb + 1], ins["positions_2"][0, tb * P:tb * P + P].unsqueeze(1))\
              .then_inc(*up("positions", 1 + tb, 16))
        act.dma_start(t2.sink_all, ins["sw_sinks_2"].partition_broadcast(P)).then_inc(*up("vectors", 0, 16))
        act.dma_start(t2.nega_all, ins["dn_a_log_2"].partition_broadcast(P)).then_inc(*up("vectors", 1, 16))
        act.dma_start(t2.dtb_all, ins["dn_dt_bias_2"].partition_broadcast(P)).then_inc(*up("vectors", 2, 16))
        for l in range(DEPTH):
            for n, (name, k) in enumerate((("pre_mix_g_2", KB), ("pre_mlp_g_2", KB))):
                act.dma_start(rows[l][n * KB:n * KB + k, :], ins[name][l].rearrange("(k p) -> k p", p=P))\
                  .then_inc(*up("rows", (l, n), 16))
            act.dma_start(rows[l][2 * KB:2 * KB + 1, :], ins["dn_norm_g_2"][l:l + 1, :]).then_inc(*up("rows", (l, 2), 16))
            act.dma_start(rows[l][2 * KB + 1:R, :], ins["dn_conv_w_2"][l].rearrange("j (k p) -> (j k) p", p=P))\
              .then_inc(*up("rows", (l, 3), 16))

    @core.program("vector")
    def _(dve):
        core.seed_ring(dve)

        def link(ins_):
            chain[0] += 1
            ins_.then_inc(*up("chain", chain[0]))
            dve.wait_ge(*at("chain", chain[0]))

        def parts(x):
            out = []
            for _ in range(3):
                a = float(np.float32(x)) if len(out) == 2 else math.ldexp(round(math.ldexp(x, 10 - math.frexp(x)[1])), math.frexp(x)[1] - 10)
                out.append(a)
                x -= a
            return out

        dve.wait_ge(*at("positions", TB))
        link(dve.tensor_copy(pos, pos_i))
        ang, n, r, c = (work[:, i, :, :] for i in range(4))
        for tb in range(TB):
            link(dve.tensor_scalar(ang[:, tb, :], inv, pos[:, tb:tb + 1], None, ALU.mult))
        magic = 1.5 * 2.0 ** 23

        def reduce(out, src, period, shift):
            link(dve.tensor_scalar(n, src, 1.0 / period, shift, ALU.mult, ALU.add))
            link(dve.tensor_scalar(n, n, magic, None, ALU.add))
            link(dve.tensor_scalar(n, n, -magic, None, ALU.add))
            for i, part in enumerate(parts(period)):
                link(dve.scalar_tensor_tensor(out, n, -part, src if i == 0 else out, ALU.mult, ALU.add))

        two_pi = 2 * math.pi
        reduce(r, ang, 2048 * two_pi, 0.0)
        reduce(c, r, two_pi, 0.25)
        link(dve.tensor_scalar(c, c, math.pi / 2, None, ALU.add))
        reduce(r, r, two_pi, 0.0)
        edge = float(np.float32(3.1415925))
        for a in (c, r):
            link(dve.tensor_scalar(a, a, edge, -edge, ALU.min, ALU.max))
        s.keys["chain", "reduced"] = s.keys["chain", chain[0]]
        dve.wait_ge(*at("sines", 1))
        rope = core.rope2
        link(dve.tensor_copy(rope[:, :, 0, :], work[:, 4, :, :]))
        link(dve.tensor_copy(rope[:, :, 1, :], work[:, 4, :, :]))
        link(dve.tensor_copy(rope[:, :, 3, :], work[:, 5, :, :]))
        dve.tensor_scalar(rope[:, :, 2, :], work[:, 5, :, :], -1.0, None, ALU.mult).then_inc(*up("rope"))

    @core.program("scalar")
    def _(act):
        act.wait_ge(*at("chain", "reduced"))
        act.activation(work[:, 4, :, :], work[:, 3, :, :], ACT.Sin).then_inc(*up("sines", 0))
        act.activation(work[:, 5, :, :], work[:, 2, :, :], ACT.Sin).then_inc(*up("sines", 1))


def setup_columns(nc, core, s, ins):
    t2 = core.t2
    R = t2.cols.shape[-1]
    late = core.buf[7][:, :, :].rearrange("p a b -> p (a b)")
    rows = [late[:, l * P:l * P + P] for l in range(DEPTH)]
    at, up = s.at, s.up

    @core.program("tensor")
    def _(pe):
        pe.wait_ge(*at("rows", (DEPTH - 1, 3)))
        for l in range(DEPTH):
            pe.transpose(core.bank[SCORE[l]][:, 0:R], rows[l][0:R, :], core.ident[0:R, 0:R]).then_inc(*up("turned", l))

    @core.program("vector")
    def _(dve):
        for l in range(DEPTH):
            dve.wait_ge(*at("turned", l))
            dve.tensor_copy(t2.cols_all[:, l, :], core.bank[SCORE[l]][:, 0:R]).then_inc(*up("cols", l))
        dve.wait_ge(*at("exp_a"))
        dve.tensor_scalar(t2.nega_all, t2.nega_all, -1.0, None, ALU.mult).then_inc(*up("nega"))

    @core.program("scalar")
    def _(act):
        act.wait_ge(*at("vectors", 2))
        act.activation(t2.nega_all, t2.nega_all, ACT.Exp).then_inc(*up("exp_a"))


def block_two(nc, core, s, plan, ins, base):
    b0, b1, qd, kd_T, vb, qs, ys, zz, b8 = core.buf
    flat8 = b8[:, :, :].rearrange("p a b -> p (a b)")
    k_dup = flat8[:, 0:512].rearrange("p (t c) -> p t c", t=TB)
    ks = flat8[:, 512:1024].rearrange("p (k t) -> p k t", t=S)
    vs = flat8[:, 1024:1280].rearrange("p (t c) -> p t c", t=TB)
    k_dec = flat8[:, 0:1024].rearrange("p (h d) -> p h d", d=P)
    source = {"sq": b0, "sk": k_dup, "dq": b1, "dk": b0, "dv": b1, "ys": ys, "yd": vb,
              "mix": qs}
    xt_of = {"h": 0, "ys": 1, "yd": 0, "mix": 1, "h2": 0}
    gain_of = {"h": list(range(KB)), "h2": list(range(KB, 2 * KB)), "yd": [2 * KB] * KB}
    tap = lambda j, n: 2 * KB + 1 + j * 3 * DHEADS + n
    conv_out = {"dq": (qd, 0), "dk": (kd_T, DHEADS), "dv": (zz, 2 * DHEADS)}
    scr = core.scratch
    prob = [scr[:, i * 384:(i + 1) * 384] for i in range(2)]
    masked = [scr[:, 768 + i * 384:768 + (i + 1) * 384] for i in range(2)]
    turned = scr[:, 2304:2688]
    junk = scr[:, 3072:4096]

    def region(first, n, *shape):
        a = scr[:, first:first + n]
        if len(shape) == 2:
            return a.rearrange("p (a b) -> p a b", b=shape[1])
        return a.rearrange("p (h c t) -> p h c t", c=shape[1], t=shape[2])

    lm = [region(1024 + 512 * i, 512, 2, TB, P) for i in range(2)]
    wide = qs[:, :, :].rearrange("p a b -> p (a b)")
    pick = lambda g, first: (wide[:, first:first + 512] if g % 2 == 0 else
                             scr[:, first + 1024 * (first >= 1024):first + 1024 * (first >= 1024) + 512])
    four = lambda a: a.rearrange("p (h c t) -> p h c t", c=TB, t=P)
    decay = [four(pick(g, 0)) for g in range(2)]
    score = [four(pick(g, 512)) for g in range(2)]
    pair = [(wide[:, 1024:2048], scr[:, 2048:3072])[g] for g in range(2)]
    tr = [[a[:, 512 * j:512 * j + 512].rearrange("p (c w t) -> p c w t", c=TB, w=2) for j in range(2)] for a in pair]
    tr_all = [a.rearrange("p (h c w t) -> p (h c) w t", h=2, c=TB, w=2) for a in pair]
    beta_rows = [four(a[:, 0:512]) for a in pair]
    yy = region(3072, 512, 2, TB, P)
    state, uu, rr, xx = (region(3584 + 256 * i, 256, 2, P) for i in range(4))
    t1, t = core.t1, core.t2
    t.ba = core.tile(TB, 2 * DHEADS)
    t.beta, t.g, t.abs, t.soft = (core.tile(TB, DHEADS) for _ in range(4))
    t.cum, t.ec = core.tile(TB, DHEADS), core.tile(2, DHEADS)
    t.ssq2, t.rk, t.rq, t.brk = (core.tile(TB, DHEADS) for _ in range(4))
    t.kds, t.rs = core.tile(DHEADS), core.tile(DHEADS)
    t.sinkexp = core.tile(2, TB)
    t.junk = scr[:, 4608:4736]
    t.future = scr[:, 4864:4864 + P]
    t.turn_bank = {}
    s.rot_before = {"sq": "sk"}
    P_ = len(plan.pieces)
    at, up = s.at, s.up
    B = core.bank
    own, both = slice(P, 2 * P), slice(0, 2 * P)
    parts = [(0, slice(0, P), own), (1, slice(P, 3 * P), both)]
    HC = [(h, c) for h in range(2) for c in range(TB)]
    level_mask = lambda l: core.square[:, 3 + l, :]
    f_src = lambda j: b0 if j % 2 == 0 else b1

    def ended(name, layer):
        return core.pieces_used, layer * P_ + (base + plan.end[name] + RING + 1)

    def is_cut(name):
        return name in xt_of or name[0] == "f"

    @core.program("tensor")
    def _(pe):
        with pe.Fori(0, DEPTH) as layer:
            s.layer = layer
            last_read = {}
            turn_at = 0

            def free(b):
                if b in last_read:
                    pe.wait_ge(*at(*last_read[b]))

            for what in plan.steps:
                kind, arg = what[0], what[1] if len(what) > 1 else None
                if kind == "piece":
                    job, n = plan.pieces[arg]
                    if n == 0 and job.start:
                        for b in job.banks:
                            free(b)
                    if n == 0:
                        ready = {"us0": ("cut", ("ys", 3))}.get(job.name)
                        if ready:
                            pe.wait_ge(*at(*ready))
                        if job.name[:2] == "dn":
                            pe.wait_ge(*at("cut", ("f" + job.name[2], 1)))
                    if job.name == "ba0" and n % 2 == 0:
                        pe.wait_ge(*at("cut", ("h", n // 2)))
                    if job.name in ("up0", "ud0"):
                        pe.wait_ge(*at("cut", ({"up0": "h2", "ud0": "yd"}[job.name], n)))
                    if job.name == "oo0":
                        pe.wait_ge(*at("cut", ("mix", n)))
                    core.multiply(pe, layer, base, plan, arg, (0,) if what[-1] == "half" else (0, 1))
                if kind == "more":
                    job, n = plan.pieces[arg]
                    core.multiply(pe, layer, base, plan, arg, (1,))
                if kind in ("piece", "more"):
                    if n == job.pieces - 1 and what[-1] != "half":
                        name = "sigmoid" if job.name[:2] in ("ga", "gb") else "evac"
                        for b in job.banks:
                            last_read[b] = (name, job.name)
                if kind == "post":
                    for b in range(2 * TB):
                        last_read[b] = ("post", (arg, 1))
                if kind == "turn":
                    f = what[2]
                    b = (TURN, OUT)[turn_at % 2]
                    turn_at += 1
                    if arg in ("dq", "dk"):
                        b = OUT
                    free(b)
                    wait = {"h": ("h_ready", 0), "h2": ("h_ready", 1), "sq": ("rotated", "sq"), "sk": ("rotated", "sk"),
                            "dq": ("evac", "dq1"), "dk": ("evac", "dk1"), "dv": ("evac", "dv1"),
                            "ys": ("ys", HEADS - 1), "yd": ("yd_gated", f), "mix": ("mix", f // 2),
                            "v": ("silu", "dv"), "kd": ("silu", "dk")}.get(arg) or ("evac", f"up{arg[1:]}")
                    pe.wait_ge(*at(*wait))
                    if arg == "v":
                        for j in range(2):
                            for tb in range(TB):
                                mm = pe.transpose(B[b][:, (j * TB + tb) * P:(j * TB + tb + 1) * P],
                                                  qT_(zz)[:, 2 * f + j, tb * P:tb * P + P], core.ident)
                    elif arg == "kd":
                        for j in range(4):
                            mm = pe.transpose(B[b][:, j * P:j * P + P], qT_(kd_T)[:, 4 * f + j, 0:P], core.ident)
                    elif arg[0] == "h":
                        mm = turn_scaled(pe, core, B[b], f)
                    elif arg[0] == "f":
                        mm = turn_fill(nc, pe, core, B[b], f_src(int(arg[1:])), f)
                    else:
                        mm = turn_fill(nc, pe, core, B[b], source[arg], f)
                    mm.then_inc(*up("turned", (arg, f)))
                    t.turn_bank[arg, f] = b
                    if arg[0] == "f":
                        last_read[b] = ("cut", (arg, f))
                    elif arg in xt_of:
                        last_read[b] = ("cut", (arg, f))
                    elif arg in conv_out:
                        last_read[b] = ("convolved", (arg, f))
                    elif arg == "sq":
                        last_read[b] = ("sq_copied", f)
                    else:
                        last_read[b] = ("turn_copied", (arg, f))
                if kind == "decay_sum":
                    free(TURN)
                    pe.wait_ge(*at("g"))
                    for c in range(TB):
                        pe.matmul(B[TURN][:, c * DHEADS:(c + 1) * DHEADS], core.upper, t.g[:, c, :], start=True, stop=True)
                    pe.matmul(B[TURN][:, 16:16 + DHEADS], core.ones, t.g[:, 0, :], start=True, stop=True)\
                      .then_inc(*up("decay_summed"))
                    last_read[TURN] = ("cum", 1)
                if kind == "squares":
                    free(TURN)
                    pe.wait_ge(*at("squared", arg))
                    for tb in range(TB):
                        for h in range(DHEADS):
                            mm = pe.matmul(B[TURN][:, tb * DHEADS + h:tb * DHEADS + h + 1],
                                           qT_(vb)[:, h, tb * P:tb * P + P], core.ones[:, 0:1], start=True, stop=True)
                    mm.then_inc(*up("squares_summed", arg))
                    last_read[TURN] = ("ssq", arg)
                if kind == "s_scores":
                    h, b = arg, SCORE[arg % 2]
                    free(b)
                    pe.wait_ge(*at("sq_copied", h // 4))
                    if h == 0:
                        pe.wait_ge(*at("turn_copied", ("sk", 0)))
                    r = slice(HD * (h % 2), HD * (h % 2) + HD)
                    q, k = qT_(qs)[r, h // 2, :], ks[r, h // (HEADS // 2), :]
                    pe.matmul(B[b][:, 0:P], q[:, 0:P], k[:, 0:P], start=True, stop=True)
                    pe.matmul(B[b][:, P:3 * P], q[:, P:S], k, start=True, stop=True).then_inc(*up("s_scored", h))
                    last_read[b] = ("s_max", h)
                if kind == "s_turn":
                    h = arg
                    free(TURN)
                    pe.wait_ge(*at("s_prob", h))
                    for c in range(3):
                        mm = pe.transpose(B[TURN][:, c * P:c * P + P], prob[h % 2][:, c * P:c * P + P], core.ident)
                    mm.then_inc(*up("s_turned", h))
                    last_read[TURN] = ("s_copied", h)
                if kind == "s_out":
                    h = arg
                    free(OUT)
                    pe.wait_ge(*at("s_copied", h))
                    v = slice(HD * (h // (HEADS // 2)), HD * (h // (HEADS // 2)) + HD)
                    pe.matmul(B[OUT][:, 0:HD], turned[:, 0:P], vs[:, 0, v], start=True, stop=True)
                    pe.matmul(B[OUT][:, HD:2 * HD], turned[:, P:2 * P], vs[:, 0, v], start=True, stop=False)
                    pe.matmul(B[OUT][:, HD:2 * HD], turned[:, 2 * P:3 * P], vs[:, 1, v],
                              start=False, stop=True).then_inc(*up("s_summed", h))
                    last_read[OUT] = ("ys", h)
                if kind == "rows":
                    free(OUT)
                    for i, (j, c) in enumerate(HC):
                        h = 2 * arg + j
                        mm = pe.matmul(B[OUT][:, i * P:i * P + P], t.g[:, c, h:h + 1].to_broadcast([P, P]), core.upper,
                                       start=True, stop=True)
                    mm.then_inc(*up("rows", arg))
                    last_read[OUT] = ("decay", arg)
                if kind == "betas":
                    free(OUT)
                    pe.wait_ge(*at("brk"))
                    for i, (j, c) in enumerate(HC):
                        h = 2 * arg + j
                        mm = pe.matmul(B[OUT][:, i * P:i * P + P], t.brk[:, c, h:h + 1].to_broadcast([P, P]), core.ident,
                                       start=True, stop=True)
                    mm.then_inc(*up("betas", arg))
                    last_read[OUT] = ("betas_copied", arg)
                if kind in ("gram", "gram_q"):
                    free(OUT)
                    for i, (j, c) in enumerate(HC):
                        k = qT_(kd_T)[:, 2 * arg + j, c * P:c * P + P]
                        other = k if kind == "gram" else qT_(qd)[:, 2 * arg + j, c * P:c * P + P]
                        mm = pe.matmul(B[OUT][:, i * P:i * P + P], k, other, start=True, stop=True)
                    mm.then_inc(*up(kind, arg))
                    last_read[OUT] = ("lower" if kind == "gram" else "score", arg)
                if kind == "inverse":
                    free(TURN)
                    pe.wait_ge(*at("inverse", (arg, 0)))
                    for i, (h, c) in enumerate(HC):
                        mm = pe.transpose(B[TURN][:, i * P:i * P + P], tr[arg % 2][h][:, c, 1, :], core.ident)
                    mm.then_inc(*up("inverse_turned", arg))
                    last_read[TURN] = ("inverse_copied", arg)
                if kind == "level_y":
                    g, l = arg, what[2]
                    free(TURN)
                    pe.wait_ge(*at("level_mask", (g, l)))
                    if l == 1:
                        pe.wait_ge(*at("inverse_copied", g))
                    else:
                        pe.wait_ge(*at("inverse", (g, l - 1)))
                    for i, (h, c) in enumerate(HC):
                        mm = pe.matmul(B[TURN][:, i * P:i * P + P], lm[l % 2][:, h, c, :], tr[g % 2][h][:, c, 0, :],
                                       start=True, stop=True)
                    mm.then_inc(*up("level_y", (g, l)))
                    last_read[TURN] = ("y_copied", (g, l))
                if kind == "level_t":
                    g, l = arg, what[2]
                    for h in range(2):
                        free(SCORE[h])
                    pe.wait_ge(*at("y_copied", (g, l)))
                    for h, c in HC:
                        o = B[SCORE[h]][:, 2 * c * P:2 * (c + 1) * P]
                        if l < LEVELS - 1:
                            pe.matmul(o[:, 0:P], tr[g % 2][h][:, c, 1, :], yy[:, h, c, :], start=True, stop=True)
                        mm = pe.matmul(o[:, P:2 * P], yy[:, h, c, :], tr[g % 2][h][:, c, 1, :], start=True, stop=True)
                    mm.then_inc(*up("level_t", (g, l)))
                    for h in range(2):
                        last_read[SCORE[h]] = ("inverse", (g, l))
                if kind == "delta_u":
                    free(TURN)
                    pe.wait_ge(*at("inverse", (arg, LEVELS - 1)))
                    if arg == 0:
                        pe.wait_ge(*at("turn_copied", ("v", 3)))
                    for j in range(2):
                        h = 2 * arg + j
                        mm = pe.matmul(B[TURN][:, j * P:j * P + P], tr[arg % 2][j][:, 0, 1, :], vb[:, 0, h * DV:h * DV + DV],
                                       start=True, stop=True)
                    mm.then_inc(*up("u", arg))
                    last_read[TURN] = ("u_copied", arg)
                if kind == "delta_s":
                    free(OUT)
                    pe.wait_ge(*at("u_copied", arg))
                    if arg == 0:
                        pe.wait_ge(*at("turn_copied", ("kd", 1)))
                    for j in range(2):
                        pe.matmul(B[OUT][:, j * P:j * P + P], k_dec[:, 2 * arg + j, :], uu[:, j, :], start=True, stop=True)
                    for j in range(2):
                        mm = pe.matmul(B[OUT][:, (2 + j) * P:(3 + j) * P], score[arg % 2][:, j, 0, :], uu[:, j, :],
                                       start=True, stop=True)
                    mm.then_inc(*up("state", arg))
                    last_read[OUT] = ("out0", arg)
                if kind == "delta_r":
                    free(TURN)
                    pe.wait_ge(*at("state_copied", arg))
                    for i, a in enumerate((kd_T, kd_T, qd, qd)):
                        mm = pe.matmul(B[TURN][:, i * P:i * P + P], qT_(a)[:, 2 * arg + i % 2, P:S], state[:, i % 2, :],
                                       start=True, stop=True)
                    mm.then_inc(*up("from_state", arg))
                    last_read[TURN] = ("x1", arg)
                if kind == "delta_v":
                    free(OUT)
                    pe.wait_ge(*at("rest", arg))
                    for j in range(2):
                        mm = pe.matmul(B[OUT][:, j * P:j * P + P], tr[arg % 2][j][:, 1, 1, :], rr[:, j, :], start=True, stop=True)
                    mm.then_inc(*up("v_new", arg))
                    last_read[OUT] = ("v_copied", arg)
                if kind == "delta_o":
                    free(TURN)
                    pe.wait_ge(*at("v_copied", arg))
                    for j in range(2):
                        mm = pe.matmul(B[TURN][:, j * P:j * P + P], score[arg % 2][:, j, 1, :], uu[:, j, :], start=True, stop=True)
                    mm.then_inc(*up("o1", arg))
                    last_read[TURN] = ("o_sum", arg)

    @core.program("scalar")
    def _(act):
        with act.Fori(0, DEPTH) as layer:
            s.layer = layer
            for what in plan.steps:
                kind, arg = what[0], what[1] if len(what) > 1 else None
                if kind in ("norm", "norm_mlp"):
                    n = int(kind == "norm_mlp")
                    row_squares(act, s, [(at("x_mid", tb) if n else (core.x_ready, layer * 2 + (2 * DEPTH + 3 + tb)),
                                          core.x[:, tb, :], t1.ssq[:, 0, tb:tb + 1]) for tb in range(TB)],
                                junk, f"x{n}")
                if kind == "evac" and arg[:2] in ("oo", "dn"):
                    c = int(arg[-1])
                    row_squares(act, s, [(ended(arg, layer), B[2 * c + tb][:, :], t1.ssq[:, c, tb:tb + 1])
                                         for tb in range(TB)], junk[:, c * CH:c * CH + CH], arg)
                if kind == "post_rows":
                    act.wait_ge(*at("from_state", DHEADS // 2 - 1))
                    for i, name in enumerate(("post_mix_g_2", "post_mlp_g_2")):
                        act.dma_start(kd_T[:, i, :], ins[name][layer].partition_broadcast(P))\
                           .then_inc(*up("post_rows", i, 16))
                if kind == "norm":
                    for g in range(LEAD):
                        core.split_hi(act, layer, base, plan, g)
                if kind == "piece" and arg + LEAD < P_:
                    core.split_hi(act, layer, base, plan, arg + LEAD)
                if kind == "decay":
                    act.wait_ge(*at("evac", "ba0"))
                    act.activation(t.beta, t.ba[:, :, 0:DHEADS], ACT.Sigmoid).then_inc(*up("beta"))
                    act.wait_ge(*at("abs"))
                    act.activation(t.abs, t.abs, ACT.Exp, scale=-1.0).then_inc(*up("soft", 0))
                    act.wait_ge(*at("soft", 0))
                    act.activation(t.abs, t.abs, ACT.Ln, bias=1.0).then_inc(*up("soft", 1))
                if kind == "decay_sum":
                    act.wait_ge(*at("cum", 1))
                    act.activation(t.ec, t.ec, ACT.Exp).then_inc(*up("ec"))
                if kind == "turn" and is_cut(arg):
                    f = what[2]
                    act.wait_ge(*at("turned", (arg, f)))
                    bank = B[t.turn_bank[arg, f]][:, :].rearrange("p (j t) -> p j t", j=2)
                    if arg[0] == "f":
                        k = 4 * (int(arg[1:]) % 2) + 2 * f
                        act.activation(core.xh[1][:, k:k + 2, :], bank, ACT.Copy).then_inc(*up("high", (arg, f, 1)))
                    elif arg in gain_of:
                        for j in range(2):
                            gain = t.cols[:, gain_of[arg][2 * f + j]:gain_of[arg][2 * f + j] + 1]
                            act.activation(core.xh[xt_of[arg]][:, 2 * f + j, :], bank[:, j, :], ACT.Copy,
                                           scale=gain).then_inc(*up("high", (arg, f, j)))
                    else:
                        act.activation(core.xh[xt_of[arg]][:, 2 * f:2 * f + 2, :], bank, ACT.Copy)\
                           .then_inc(*up("high", (arg, f, 1)))
                if kind == "turn" and arg == "sq":
                    f = what[2]
                    act.wait_ge(*at("turned", (arg, f)))
                    act.activation(qT_(qs)[:, 2 * f:2 * f + 2, :],
                                   B[t.turn_bank[arg, f]][:, :].rearrange("p (j t) -> p j t", j=2), ACT.Copy)\
                       .then_inc(*up("sq_copied", f))
                if kind == "silu":
                    a = qT_(conv_out[arg][0])
                    act.wait_ge(*at("convolved", (arg, 3)))
                    act.activation(a, a, ACT.Silu).then_inc(*up("silu", arg))
                if kind == "square":
                    act.wait_ge(*at("silu", arg))
                    if arg == "dk":
                        act.wait_ge(*at("squares_summed", "dq"))
                    act.activation(qT_(vb), qT_(conv_out[arg][0]), ACT.Square).then_inc(*up("squared", arg))
                if kind == "evac" and arg[:2] in ("zz", "ga", "gb"):
                    c = int(arg[2])
                    dst = {"zz": zz, "ga": b1, "gb": b0}[arg[:2]]
                    if arg == "zz0":
                        act.wait_ge(*at("turned", ("v", 3)))
                    if arg == "gb0":
                        act.wait_ge(*at("turned", ("dk", 3)))
                    if arg == "ga0":
                        act.wait_ge(*at("turned", ("dv", 3)))
                    for tb in range(TB):
                        act.wait_ge(*ended(arg, layer))
                        ins_ = act.activation(dst[:, tb, c * CH:c * CH + CH],
                                              B[plan.by_name[arg].banks[tb]][:, :], ACT.Sigmoid)
                    ins_.then_inc(*up("sigmoid", arg))
                if kind == "evac" and arg[:2] == "up":
                    j = int(arg[2:])
                    if j == 0:
                        act.wait_ge(*at("mix", 1))
                    if j >= 2:
                        act.wait_ge(*at("turned", (f"f{j - 2}", 1)))
                    for tb in range(TB):
                        act.wait_ge(*ended(arg, layer))
                        ins_ = act.activation(f_src(j)[:, tb, 0:CH], B[plan.by_name[arg].banks[tb]][:, :], ACT.Relu)
                    ins_.then_inc(*up("relu", j))
                if kind == "s_scores":
                    h = arg
                    act.wait_ge(*at("s_max", h))
                    if h >= 2:
                        act.wait_ge(*at("s_turned", h - 2))
                    for tb, cols, _ in parts:
                        act.activation(prob[h % 2][:, cols], masked[h % 2][:, cols], ACT.Exp, scale=SCALE,
                                       bias=t1.negmax[:, h % 2, tb:tb + 1],
                                       accum_out=t1.total[:, h % 4, tb:tb + 1])
                    act.activation(t.sinkexp[:, h % 2, :], t.sinkexp[:, h % 2, :], ACT.Exp).then_inc(*up("s_prob", h))
                if kind == "s_turn":
                    h = arg
                    act.wait_ge(*at("s_turned", h))
                    if h >= 1:
                        act.wait_ge(*at("s_summed", h - 1))
                    act.activation(turned, B[TURN][:, 0:3 * P], ACT.Copy).then_inc(*up("s_copied", h))
                if kind == "rows":
                    act.wait_ge(*at("decay", arg))
                    act.activation(score[arg % 2], decay[arg % 2], ACT.Exp).then_inc(*up("decay_exp", arg))
                if kind == "betas":
                    act.wait_ge(*at("betas", arg))
                    act.activation(beta_rows[arg % 2], B[OUT][:, :].rearrange("p (h c t) -> p h c t", c=TB, t=P),
                                   ACT.Copy).then_inc(*up("betas_copied", arg))
                if kind == "inverse":
                    act.wait_ge(*at("inverse_turned", arg))
                    act.activation(tr_all[arg % 2][:, :, 0, :], B[TURN][:, :].rearrange("p (i t) -> p i t", t=P), ACT.Copy)\
                       .then_inc(*up("inverse_copied", arg))
                if kind == "level_y":
                    g, l = arg, what[2]
                    act.wait_ge(*at("level_y", (g, l)))
                    act.activation(yy.rearrange("p h c t -> p (h c t)"), B[TURN][:, :], ACT.Copy).then_inc(*up("y_copied", (g, l)))
                if kind == "delta_u":
                    act.wait_ge(*at("u", arg))
                    act.activation(uu.rearrange("p h t -> p (h t)"), B[TURN][:, 0:2 * P], ACT.Copy).then_inc(*up("u_copied", arg))
                if kind == "delta_v":
                    act.wait_ge(*at("v_new", arg))
                    act.activation(uu.rearrange("p h t -> p (h t)"), B[OUT][:, 0:2 * P], ACT.Copy).then_inc(*up("v_copied", arg))
                if kind == "delta_o":
                    act.wait_ge(*at("yd", arg))
                    for j in range(2):
                        for tb in range(TB):
                            h = 2 * arg + j
                            if arg or j or tb:
                                act.wait_ge(*at("yd_square", last))
                            last = (arg, j, tb)
                            act.activation(t.junk, vb[:, tb, h * DV:h * DV + DV], ACT.Square,
                                           accum_out=t1.head_ssq[:, tb, h:h + 1]).then_inc(*up("yd_square", last))

    @core.program("vector")
    def _(dve):
        with dve.Fori(0, DEPTH) as layer:
            s.layer = layer
            dve.tensor_copy(t.cols, t.cols_all[:, layer, :]).then_inc(*up("small", 0))
            dve.tensor_scalar(t.sink, t.sink_all[:, layer, :], 1.0 / SCALE, None, ALU.mult).then_inc(*up("small", 1))
            dve.tensor_copy(t.nega, t.nega_all[:, layer, :]).then_inc(*up("small", 2))
            dve.tensor_copy(t.dtb, t.dtb_all[:, layer, :]).then_inc(*up("small", 3))
            for what in plan.steps:
                kind, arg = what[0], what[1] if len(what) > 1 else None
                if kind == "piece" and arg + LO_LEAD < P_ and core.lo_engine(arg + LO_LEAD) == "dve":
                    core.split_lo(dve, layer, base, plan, arg + LO_LEAD)
                if kind in ("norm", "norm_mlp"):
                    n = int(kind == "norm_mlp")
                    rstd_diagonal(dve, s, core, f"x{n}", up("h_ready", n))
                if kind == "norm":
                    for g in range(LO_LEAD):
                        if core.lo_engine(g) == "dve":
                            core.split_lo(dve, layer, base, plan, g)
                if kind == "turn":
                    f = what[2]
                    bank = B[t.turn_bank[arg, f]][:, :].rearrange("p (j t) -> p j t", j=2)
                    if is_cut(arg):
                        if arg[0] == "f":
                            k = 4 * (int(arg[1:]) % 2) + 2 * f
                            dve.wait_ge(*at("high", (arg, f, 1)))
                            dve.tensor_tensor(core.xl[1][:, k:k + 2, :], bank, core.xh[1][:, k:k + 2, :].bitcast(F32),
                                              ALU.subtract).then_inc(*up("cut", (arg, f)))
                            continue
                        xh, xl = core.xh[xt_of[arg]], core.xl[xt_of[arg]]
                        dve.wait_ge(*at("high", (arg, f, 1)))
                        if arg in gain_of:
                            for j in range(2):
                                n = 2 * f + j
                                ins_ = dve.scalar_tensor_tensor(xl[:, n, :], bank[:, j, :],
                                                                t.cols[:, gain_of[arg][n]:gain_of[arg][n] + 1],
                                                                xh[:, n, :].bitcast(F32), ALU.mult, ALU.subtract)
                        else:
                            ins_ = dve.tensor_tensor(xl[:, 2 * f:2 * f + 2, :], bank,
                                                     xh[:, 2 * f:2 * f + 2, :].bitcast(F32), ALU.subtract)
                        ins_.then_inc(*up("cut", (arg, f)))
                    elif arg in conv_out:
                        out, first = conv_out[arg]
                        dve.wait_ge(*at("turned", (arg, f)))
                        for j in (3, 2, 1, 0):
                            if j < 3:
                                dve.wait_ge(*at("taps", (arg, f, j + 1)))
                            for n in range(2):
                                w = t.cols[:, tap(j, first + 2 * f + n):tap(j, first + 2 * f + n) + 1]
                                y = qT_(out)[:, 2 * f + n, 3 - j:S]
                                x = bank[:, n, 0:S - 3 + j]
                                if j == 3:
                                    ins_ = dve.tensor_scalar(y, x, w, None, ALU.mult)
                                else:
                                    ins_ = dve.scalar_tensor_tensor(y, x, w, y, ALU.mult, ALU.add)
                            if j:
                                ins_.then_inc(*up("taps", (arg, f, j)))
                        ins_.then_inc(*up("convolved", (arg, f)))
                    elif arg == "v":
                        dve.wait_ge(*at("turned", (arg, f)))
                        dve.wait_ge(*at("beta"))
                        for j in range(2):
                            h = 2 * f + j
                            ins_ = dve.tensor_tensor(vb[:, :, h * DV:h * DV + DV],
                                                     B[t.turn_bank[arg, f]][:, j * S:j * S + S].rearrange("p (t d) -> p t d", d=DV),
                                                     bcast(t.beta[:, :, h], 2, DV), ALU.mult)
                        ins_.then_inc(*up("turn_copied", (arg, f)))
                    elif arg == "kd":
                        dve.wait_ge(*at("turned", (arg, f)))
                        dve.wait_ge(*at("kds"))
                        dve.tensor_tensor(k_dec[:, 4 * f:4 * f + 4, :],
                                          B[t.turn_bank[arg, f]][:, :].rearrange("p (h d) -> p h d", d=P),
                                          bcast(t.kds[:, 4 * f:4 * f + 4], 2, P), ALU.mult)\
                           .then_inc(*up("turn_copied", (arg, f)))
                    elif arg == "sk":
                        dve.wait_ge(*at("turned", (arg, f)))
                        dve.tensor_copy(ks, bank).then_inc(*up("turn_copied", (arg, f)))
                if kind == "decay":
                    y = t.ba[:, :, DHEADS:2 * DHEADS]
                    dve.wait_ge(*at("evac", "ba0"))
                    dve.wait_ge(*at("small", 3))
                    dve.tensor_tensor(y, y, bcast(t.dtb, 1, TB), ALU.add).then_inc(*up("y"))
                    dve.wait_ge(*at("y"))
                    dve.scalar_tensor_tensor(t.abs, y, -1.0, y, ALU.mult, ALU.max).then_inc(*up("abs"))
                    dve.wait_ge(*at("soft", 1))
                    dve.scalar_tensor_tensor(t.soft, y, 0.0, t.abs, ALU.max, ALU.add).then_inc(*up("softplus"))
                    dve.wait_ge(*at("softplus"))
                    dve.tensor_tensor(t.g, t.soft, bcast(t.nega, 1, TB), ALU.mult).then_inc(*up("g"))
                if kind == "decay_sum":
                    dve.wait_ge(*at("decay_summed"))
                    dve.tensor_copy(t.cum.rearrange("p c h -> p (c h)"), B[TURN][:, 0:2 * DHEADS]).then_inc(*up("cum", 0))
                    dve.wait_ge(*at("cum", 0))
                    dve.tensor_copy(t.ec[:, 0, :], t.cum[:, 1, :])
                    dve.tensor_tensor(t.ec[:, 1, :], B[TURN][:, 16:16 + DHEADS], t.cum[:, 0, :], ALU.subtract)\
                       .then_inc(*up("cum", 1))
                if kind == "squares":
                    dve.wait_ge(*at("squares_summed", arg))
                    if arg == "dk":
                        dve.wait_ge(*at("rq"))
                    dve.tensor_copy(t.ssq2.rearrange("p c h -> p (c h)"), B[TURN][:, 0:2 * DHEADS]).then_inc(*up("ssq", arg))
                if kind == "scales":
                    dve.wait_ge(*at("rk"))
                    dve.wait_ge(*at("beta"))
                    dve.wait_ge(*at("ec"))
                    dve.wait_ge(*at("rotated", "sq"))
                    dve.tensor_scalar(t.future, core.upper, -1.0, -NEG, ALU.add, ALU.mult).then_inc(*up("future"))
                    dve.tensor_tensor(t.brk, t.beta, t.rk, ALU.mult).then_inc(*up("brk"))
                    dve.tensor_tensor(t.kds, t.ec[:, 1, :], t.rk[:, 0, :], ALU.mult).then_inc(*up("kds"))
                    dve.wait_ge(*at("brk"))
                    dve.scalar_tensor_tensor(t.rs, t.ec[:, 0, :], -1.0, t.brk[:, 1, :], ALU.mult, ALU.mult)\
                       .then_inc(*up("rs"))
                if kind == "evac":
                    job, name = plan.by_name[arg], arg[:2]
                    c = int(arg[-1])
                    cols = slice(c * CH, c * CH + CH)
                    done = ended(arg, layer)
                    if arg == "ba0":
                        for tb in range(TB):
                            dve.wait_ge(*done)
                            dve.tensor_copy(t.ba[:, tb, :], B[job.banks[tb]][:, 0:16])
                            ins_ = dve.tensor_copy(b0[:, tb, 0:256], B[job.banks[tb]][:, 16:272])
                        ins_.then_inc(*up("evac", arg))
                    if arg == "sq0":
                        for tb in range(TB):
                            dve.wait_ge(*done)
                            ins_ = dve.tensor_copy(b0[:, tb, 256:768], B[job.banks[tb]][:, :])
                        ins_.then_inc(*up("evac", arg))
                    if arg == "sq1":
                        for tb in range(TB):
                            bank = B[job.banks[tb]]
                            dve.wait_ge(*done)
                            dve.tensor_copy(b0[:, tb, 768:1024], bank[:, 0:256])
                            for r in range(2):
                                dve.tensor_copy(k_dup[:, tb, :].rearrange("p (k r d) -> p k r d", k=2, r=2)[:, :, r, :],
                                                bank[:, 256:384].rearrange("p (k d) -> p k d", k=2))
                            ins_ = dve.tensor_copy(vs[:, tb, :], bank[:, 384:512])
                        ins_.then_inc(*up("evac", arg))
                    if name in ("dq", "dk", "dv"):
                        dst, before = {"dq": (b1, None), "dk": (b0, ("sq", 3)), "dv": (b1, ("dq", 3))}[name]
                        if c == 0 and before:
                            dve.wait_ge(*at("turned", before))
                        for tb in range(TB):
                            dve.wait_ge(*done)
                            ins_ = dve.tensor_copy(dst[:, tb, cols], B[job.banks[tb]][:, :])
                        ins_.then_inc(*up("evac", arg))
                    if name == "zz":
                        for tb in range(TB):
                            dve.wait_ge(*at("sigmoid", arg))
                            ins_ = dve.tensor_tensor(zz[:, tb, cols], B[job.banks[tb]][:, :], zz[:, tb, cols], ALU.mult)
                        ins_.then_inc(*up("evac", arg))
                    if name == "us":
                        for tb in range(TB):
                            dve.wait_ge(*done)
                            dve.wait_ge(*at("sigmoid", "gb1"))
                            ins_ = dve.tensor_tensor(b0[:, tb, cols], B[job.banks[tb]][:, :], b0[:, tb, cols], ALU.mult)
                        ins_.then_inc(*up("evac", arg))
                    if name == "ud":
                        for tb in range(TB):
                            dve.wait_ge(*done)
                            dve.wait_ge(*at("sigmoid", "ga1"))
                            dve.tensor_tensor(b1[:, tb, cols], B[job.banks[tb]][:, :], b1[:, tb, cols],
                                              ALU.mult).then_inc(*up("evac", (arg, tb)))
                        dve.wait_ge(*at("evac", (arg, 1)))
                        dve.wait_ge(*at("evac", "us1"))
                        dve.tensor_tensor(qs[:, :, cols], b0[:, :, cols], b1[:, :, cols], ALU.add).then_inc(*up("mix", c))
                        s.keys["evac", arg] = s.keys["evac", (arg, 1)]
                    if name == "up":
                        j = int(arg[2:])
                        for tb in range(TB):
                            dve.wait_ge(*at("relu", j))
                            f = f_src(j)[:, tb, 0:CH]
                            ins_ = dve.tensor_tensor(f, B[job.banks[tb]][:, :], f, ALU.mult)
                        ins_.then_inc(*up("evac", arg))
                if kind == "post":
                    last = ("oo1", "dn7_1")[arg]
                    dve.wait_ge(*at("rstd", last))
                    dve.wait_ge(*at("post_rows", 1))
                    for tb in range(TB):
                        for c in range(2):
                            cols = slice(c * CH, c * CH + CH)
                            ins_ = dve.scalar_tensor_tensor(ys[:, tb, cols], B[2 * c + tb][:, :], t1.rstd[:, tb:tb + 1],
                                                            kd_T[:, arg, cols], ALU.mult, ALU.mult)
                        ins_.then_inc(*up("post", (arg, tb)))
                        dve.wait_ge(*at("post", (arg, tb)))
                        dve.tensor_tensor(core.x[:, tb, :], core.x[:, tb, :], ys[:, tb, :], ALU.add)\
                           .then_inc(*(up("x_mid", tb) if arg == 0 else (core.x_ready, 1)))
                if kind == "s_scores":
                    h = arg
                    masked_max(dve, core, s, B[SCORE[h % 2]], masked[h % 2], t1.top[:, h % 2, :],
                               t1.negmax[:, h % 2, :], parts, 2, ("s_scored", h), ("s_prob", h - 2) if h >= 2 else None,
                               ("s_top", h), ("s_max", h), sink=(t.sink[:, h:h + 1], t.sinkexp[:, h % 2, :]))
                if kind == "s_turn":
                    h = arg
                    dve.wait_ge(*at("s_prob", h))
                    tot = t1.total[:, h % 4, :]
                    dve.tensor_tensor(tot, tot, t.sinkexp[:, h % 2, :], ALU.add).then_inc(*up("s_total", h))
                    dve.wait_ge(*at("s_total", h))
                    dve.reciprocal(t1.inverse[:, h % 4, :], tot).then_inc(*up("s_inverse", h))
                if kind == "s_out":
                    h = arg
                    dve.wait_ge(*at("s_summed", h))
                    dve.wait_ge(*at("s_inverse", h))
                    dve.tensor_tensor(ys[:, :, h * HD:h * HD + HD],
                                      B[OUT][:, 0:2 * HD].rearrange("p (t d) -> p t d", t=TB),
                                      bcast(t1.inverse[:, h % 4, :], 2, HD), ALU.mult).then_inc(*up("ys", h))
                if kind == "rows":
                    dve.wait_ge(*at("rows", arg))
                    dve.wait_ge(*at("future"))
                    for i, (j, c) in enumerate(HC):
                        h = 2 * arg + j
                        ins_ = dve.scalar_tensor_tensor(decay[arg % 2][:, j, c, :], B[OUT][:, i * P:i * P + P],
                                                        t.cum[:, c, h:h + 1], t.future, ALU.subtract, ALU.min)
                    ins_.then_inc(*up("decay", arg))
                if kind == "betas":
                    dve.wait_ge(*at("decay_exp", arg))
                    dve.wait_ge(*at("betas_copied", arg))
                    dve.tensor_tensor(decay[arg % 2], beta_rows[arg % 2], score[arg % 2], ALU.mult).then_inc(*up("decay_beta", arg))
                if kind == "gram":
                    dve.wait_ge(*at("gram", arg))
                    dve.wait_ge(*at("decay_beta", arg))
                    for i, (j, c) in enumerate(HC):
                        h = 2 * arg + j
                        ins_ = dve.scalar_tensor_tensor(decay[arg % 2][:, j, c, :], B[OUT][:, i * P:i * P + P],
                                                        t.rk[:, c, h:h + 1], decay[arg % 2][:, j, c, :], ALU.mult, ALU.mult)
                    ins_.then_inc(*up("lower", arg))
                if kind == "gram_q":
                    dve.wait_ge(*at("gram_q", arg))
                    for i, (j, c) in enumerate(HC):
                        h = 2 * arg + j
                        ins_ = dve.scalar_tensor_tensor(score[arg % 2][:, j, c, :], B[OUT][:, i * P:i * P + P],
                                                        t.rk[:, c, h:h + 1], score[arg % 2][:, j, c, :], ALU.mult, ALU.mult)
                    ins_.then_inc(*up("score", arg))
                if kind == "inverse":
                    dve.wait_ge(*at("level_mask", (arg, 0)))
                    first = tr_all[arg % 2][:, :, 1, :]
                    dve.tensor_tensor(first, bcast(core.ident, 1, 4), first, ALU.subtract).then_inc(*up("inverse", (arg, 0)))
                if kind == "level_t":
                    g, l = arg, what[2]
                    dve.wait_ge(*at("level_t", (g, l)))
                    for h in range(2):
                        w = slice(0, 2) if l < LEVELS - 1 else slice(1, 2)
                        bank = B[SCORE[h]][:, :].rearrange("p (c w t) -> p c w t", c=TB, w=2)[:, :, w, :]
                        part = tr[g % 2][h][:, :, w, :]
                        ins_ = dve.tensor_tensor(part, part, bank, ALU.subtract)
                    ins_.then_inc(*up("inverse", (g, l)))
                if kind == "delta_s":
                    dve.wait_ge(*at("state", arg))
                    dve.tensor_copy(state.rearrange("p h t -> p (h t)"), B[OUT][:, 0:2 * P]).then_inc(*up("state_copied", arg))
                    v = vb[:, 0, 2 * arg * DV:2 * (arg + 1) * DV].rearrange("p (h d) -> p h d", d=DV)
                    dve.tensor_tensor(v, B[OUT][:, 2 * P:4 * P].rearrange("p (h d) -> p h d", d=DV),
                                      bcast(t.rq[:, 0, 2 * arg:2 * arg + 2], 2, DV), ALU.mult).then_inc(*up("out0", arg))
                if kind == "delta_r":
                    dve.wait_ge(*at("from_state", arg))
                    dve.wait_ge(*at("rs"))
                    for j in range(2):
                        h = 2 * arg + j
                        ins_ = dve.scalar_tensor_tensor(rr[:, j, :], B[TURN][:, j * P:j * P + P], t.rs[:, h:h + 1],
                                                        vb[:, 1, h * DV:h * DV + DV], ALU.mult, ALU.add)
                    ins_.then_inc(*up("rest", arg))
                    dve.tensor_tensor(xx, B[TURN][:, 2 * P:4 * P].rearrange("p (h d) -> p h d", d=DV),
                                      bcast(t.ec[:, 0, 2 * arg:2 * arg + 2], 2, DV), ALU.mult).then_inc(*up("x1", arg))
                if kind == "delta_o":
                    dve.wait_ge(*at("o1", arg))
                    dve.wait_ge(*at("x1", arg))
                    dve.tensor_tensor(xx, xx, B[TURN][:, 0:2 * P].rearrange("p (h d) -> p h d", d=DV), ALU.add)\
                       .then_inc(*up("o_sum", arg))
                    dve.wait_ge(*at("o_sum", arg))
                    v = vb[:, 1, 2 * arg * DV:2 * (arg + 1) * DV].rearrange("p (h d) -> p h d", d=DV)
                    dve.tensor_tensor(v, xx, bcast(t.rq[:, 1, 2 * arg:2 * arg + 2], 2, DV), ALU.mult).then_inc(*up("yd", arg))
                if kind == "head_norm":
                    dve.wait_ge(*at("head_rstd", arg))
                    dve.wait_ge(*at("evac", "zz1"))
                    for h in (2 * arg, 2 * arg + 1):
                        for tb in range(TB):
                            v = vb[:, tb, h * DV:h * DV + DV]
                            ins_ = dve.scalar_tensor_tensor(v, v, t1.head_rstd[:, tb, h:h + 1],
                                                            zz[:, tb, h * DV:h * DV + DV], ALU.mult, ALU.mult)
                    ins_.then_inc(*up("yd_gated", arg))

    @core.program("gpsimd")
    def _(pool):
        with pool.Fori(0, DEPTH) as layer:
            s.layer = layer
            for what in plan.steps:
                kind, arg = what[0], what[1] if len(what) > 1 else None
                if kind == "piece" and arg + LO_LEAD < P_ and core.lo_engine(arg + LO_LEAD) == "pool":
                    core.split_lo(pool, layer, base, plan, arg + LO_LEAD)
                if kind in ("norm", "norm_mlp"):
                    row_rstd(pool, s, core, "x0" if kind == "norm" else "x1", 1)
                if kind == "norm":
                    for g in range(LO_LEAD):
                        if core.lo_engine(g) == "pool":
                            core.split_lo(pool, layer, base, plan, g)
                if kind == "post":
                    row_rstd(pool, s, core, ("oo1", "dn7_1")[arg], 2)
                if kind == "rope":
                    if arg == "sk":
                        rotate(pool, s, what[2], k_dup, core.rope2, t1.rot[0], t1.rot[1], ("evac", "sq1"), "sk", 4)
                    else:
                        rotate(pool, s, what[2], b0, core.rope2, t1.rot[0], t1.rot[1], ("evac", "sq1"), "sq", HEADS)
                if kind == "squares":
                    pool.wait_ge(*at("ssq", arg))
                    if arg == "dq":
                        rsqrt(pool, s, core, t.ssq2, t.rq, DV, 1e-6 * DV, "rq_mean", "rq", 0)
                    else:
                        rsqrt(pool, s, core, t.ssq2, t.rk, 1.0, 1e-6, "rk_mean", "rk", 0)
                if kind == "inverse":
                    pool.wait_ge(*at("lower", arg))
                    pool.tensor_tensor(tr_all[arg % 2][:, :, 1, :], decay[arg % 2].rearrange("p h c t -> p (h c) t"),
                                       bcast(level_mask(0), 1, 4), ALU.mult).then_inc(*up("level_mask", (arg, 0)))
                if kind == "join" or kind == "level_t" and what[2] < LEVELS - 1:
                    l = 1 if kind == "join" else what[2] + 1
                    if l > 2:
                        pool.wait_ge(*at("level_y", (arg, l - 2)))
                    elif arg:
                        pool.wait_ge(*at("level_y", (arg - 1, LEVELS + l - 3)))
                    pool.tensor_tensor(lm[l % 2].rearrange("p h c t -> p (h c) t"),
                                       decay[arg % 2].rearrange("p h c t -> p (h c) t"),
                                       bcast(level_mask(l), 1, 4), ALU.mult).then_inc(*up("level_mask", (arg, l)))
                if kind == "head_norm":
                    pool.wait_ge(*at("yd_square", (arg, 1, TB - 1)))
                    two = slice(2 * arg, 2 * arg + 2)
                    rsqrt(pool, s, core, t1.head_ssq[:, :, two], t1.head_rstd[:, :, two], 1.0 / DV, 1e-6,
                          "head_mean", "head_rstd", arg)

    @core.program("sync")
    def _(sp):
        with sp.Fori(0, DEPTH) as layer:
            for u, (job, n) in enumerate(plan.units):
                job.weight = ins[job.weight] if isinstance(job.weight, str) else job.weight
                core.load_unit(sp, layer, base, P_, u, job, n)


def row_squares(act, s, parts, junk, key):
    for i, (wait, rows, total) in enumerate(parts):
        if wait:
            act.wait_ge(*wait)
        if i:
            act.wait_ge(*s.at("row_square", (key, i - 1)))
        act.activation(junk[:, 0:rows.shape[-1]], rows, ACT.Square, accum_out=total)\
           .then_inc(*s.up("row_square", (key, i)))


def row_rstd(pool, s, core, key, chunks):
    t = core.t1
    pool.wait_ge(*s.at("row_square", (key, (TB if key in ("oo1", "dn7_1") else chunks * TB) - 1)))
    if chunks == 2:
        pool.tensor_tensor(t.ssq[:, 0, :], t.ssq[:, 0, :], t.ssq[:, 1, :], ALU.add).then_inc(*s.up("row_sum", key))
        pool.wait_ge(*s.at("row_sum", key))
    rsqrt(pool, s, core, t.ssq[:, 0, :], t.rstd[:, 0:TB], 1.0 / D, 1e-6, "rstd_mean", "rstd", key)


def rstd_diagonal(dve, s, core, key, done):
    dve.wait_ge(*s.at("rstd", key))
    for tb in range(TB):
        ins = dve.tensor_scalar(core.diagonal[:, tb, :], core.ident, core.t1.rstd[:, tb:tb + 1], None, ALU.mult)
    ins.then_inc(*done)


def turn_scaled(pe, core, bank, f):
    for j in range(2):
        for tb in range(TB):
            c = (2 * f + j) * P
            mm = pe.matmul(bank[:, (j * TB + tb) * P:(j * TB + tb + 1) * P], core.x[:, tb, c:c + P],
                           core.diagonal[:, tb, :], start=True, stop=True)
    return mm


def build(nc, ins, out, tally=None):
    with ExitStack() as ctx:
        core = Core(nc, ctx)
        names = ["setup", "one", "final", "setup2", "two"] + ["end"]
        sig = {n: Signals(nc, ctx, n, tally and tally[n]) for n in names}
        sig["two"].after = sig["one"]
        setup_two(nc, core, sig["setup2"], ins)
        setup(nc, core, sig["setup"], ins)
        setup_columns(nc, core, sig["setup2"], ins)
        block_one(nc, core, sig["one"], plan_one(), ins)
        sig["one"].rot_before = sig["setup"].rot_before
        final_norm(nc, core, sig["final"], ins)
        block_two(nc, core, sig["two"], plan_two(), ins, len(plan_one().pieces) * DEPTH)
        store(nc, core, sig["end"], out, 2 * DEPTH + 2)
        block = ctx.enter_context(nc.Block())

        @block.tensor
        def _(pe):
            for part in core.programs["tensor"]:
                part(pe)

        @block.scalar
        def _(act):
            for part in core.programs["scalar"]:
                part(act)

        @block.vector
        def _(dve):
            for part in core.programs["vector"]:
                part(dve)

        @block.gpsimd
        def _(pool):
            for part in core.programs["gpsimd"]:
                part(pool)

        @block.sync
        def _(sp):
            for part in core.programs["sync"]:
                part(sp)

        return {n: x.totals() for n, x in sig.items()}


_INS = ["x", "norm_w", "w_in", "lambda_q1", "lambda_k1", "lambda_q2", "lambda_k2", "subln_w", "w_proj_a",
        "w_proj_b", "w_out", "final_norm_w"]
_INS2 = ["positions_2", "pre_mix_g_2", "w_in_2", "dn_conv_w_2", "dn_a_log_2", "dn_dt_bias_2", "dn_norm_g_2",
         "sw_sinks_2", "w_up_dn_2", "w_up_sw_2", "w_o_2", "post_mix_g_2", "pre_mlp_g_2", "w_ff1_2", "w_ff2_2",
         "post_mlp_g_2"]


def kernel(**inputs):
    import concourse.bacc as bacc
    from concourse.bass_utils import run_bass_kernel_spmd

    names = _INS + _INS2
    arrays = {n: np.ascontiguousarray(inputs[n]) for n in names}
    arrays.update(shape_constants())

    def program(tally):
        nc = bacc.Bacc("TRN2", target_bir_lowering=False, num_devices=1)
        ins = {n: nc.dram_tensor(f"in_{n}", a.shape, mybir.dt.from_np(a.dtype), kind="ExternalInput").ap()
               for n, a in arrays.items()}
        out = nc.dram_tensor("out", (1, S, D), F32, kind="ExternalOutput").ap()
        return nc, build(nc, ins, out, tally)

    _, tally = program(None)
    nc, again = program(tally)
    assert again == tally
    r = run_bass_kernel_spmd(nc, [{f"in_{n}": a for n, a in arrays.items()}], core_ids=[0])
    return r.results[0]["out"]
```
